# Optimizing a Trainium2 kernel written in Bass

```python
import math
import jax, jax.numpy as jnp
from jax import lax
import numpy as np

D_MODEL = 2048
BATCH = 1
SEQ = 256
DEPTH = 1
DEC_BATCH = 8
DEC_SEQ = 4
PAST_LEN = 256
PAGE_SIZE = 128

RET_HEADS = 8
RET_DK = D_MODEL // 16
RET_DV = 2 * RET_DK
RET_CHUNK = 128
ROPE_BASE = 10000.0
DIFF_HEADS = 8
DIFF_HD = D_MODEL // 32
Q_BLOCK = 128
REL_BUCKETS = 32
REL_MAX_DIST = 128
MEM_TOKENS = 256
MEM_HEADS = 4
MEM_HD = D_MODEL // 16
PEER_HEADS = 8
PEER_NKEYS = 128
PEER_EXPERTS = PEER_NKEYS * PEER_NKEYS
PEER_TOPK = 16
PEER_DK = 128
PEER_BLOCK = 128
EPS = 1e-6

RET_QK_W = RET_HEADS * RET_DK
RET_V_W = RET_HEADS * RET_DV
DIFF_QK_W = 2 * DIFF_HEADS * DIFF_HD
DIFF_V_W = DIFF_HEADS * 2 * DIFF_HD
MEM_W = MEM_HEADS * MEM_HD
IN_SPLITS = (RET_QK_W, RET_QK_W, RET_V_W, RET_V_W, DIFF_QK_W, DIFF_QK_W, DIFF_V_W, MEM_W, D_MODEL, D_MODEL, D_MODEL)
IN_WIDTH = sum(IN_SPLITS)

kernel_name = 'hybrid_retention_diffattn_peer_decode_step'

def lambda_init(layer):
    return 0.8 - 0.6 * math.exp(-0.3 * layer)

def rmsnorm(x, w=None):
    xf = x.astype(jnp.float32)
    y = xf * lax.rsqrt(jnp.mean(xf * xf, axis=-1, keepdims=True) + EPS)
    if w is not None:
        y = y * w.astype(jnp.float32)
    return y.astype(x.dtype)

def rotary(x, pos):
    half = x.shape[-1] // 2
    inv = 1.0 / (ROPE_BASE ** jnp.linspace(0.0, 1.0, half, dtype=jnp.float32))
    ang = pos.astype(jnp.float32)[:, None] * inv[None, :]
    c = jnp.cos(ang)[None, :, None, :]
    s = jnp.sin(ang)[None, :, None, :]
    xf = x.astype(jnp.float32)
    x1, x2 = xf[..., :half], xf[..., half:]
    return jnp.concatenate([x1 * c - x2 * s, x1 * s + x2 * c], axis=-1)

def ret_log_gamma():
    return jnp.log1p(-jnp.exp2(-5.0 - jnp.arange(RET_HEADS, dtype=jnp.float32)))

def retention_chunk(state, q, k, v):
    c_len = q.shape[2]
    lg = ret_log_gamma()[:, None]
    idx = jnp.arange(c_len, dtype=jnp.float32)
    rel = idx[:, None] - idx[None, :]
    dmask = jnp.where(rel >= 0, jnp.exp(lg[:, :, None] * jnp.maximum(rel, 0.0)), 0.0)
    qk = jnp.einsum('bhid,bhjd->bhij', q, k) * dmask[None]
    inner = jnp.einsum('bhij,bhje->bhie', qk, v)
    cross = jnp.einsum('bhid,bhde->bhie', q, state) * jnp.exp(lg * (idx + 1.0))[None, :, :, None]
    k_dec = k * jnp.exp(lg * (c_len - 1.0 - idx))[None, :, :, None]
    new_state = jnp.exp(lg * c_len)[None, :, :, None] * state + jnp.einsum('bhjd,bhje->bhde', k_dec, v)
    return new_state, inner + cross

def retention(q, k, v, state0):
    b, s, h, _ = q.shape
    c_len = RET_CHUNK if s % RET_CHUNK == 0 else s
    n_chunks = s // c_len

    def to_chunks(t):
        return t.astype(jnp.float32).reshape(b, n_chunks, c_len, h, t.shape[-1]).transpose(1, 0, 3, 2, 4)

    def step(st, qkv):
        return retention_chunk(st, *qkv)

    state_fin, o = lax.scan(step, state0.astype(jnp.float32), (to_chunks(q), to_chunks(k), to_chunks(v)))
    o = o.transpose(1, 0, 3, 2, 4).reshape(b, s, h, -1)
    return o, state_fin

def rel_bucket(rel):
    n = jnp.maximum(rel, 0)
    max_exact = REL_BUCKETS // 2
    nf = jnp.maximum(n, 1).astype(jnp.float32)
    large = max_exact + (jnp.log(nf / max_exact) / math.log(REL_MAX_DIST / max_exact)
                         * (REL_BUCKETS - max_exact)).astype(jnp.int32)
    large = jnp.minimum(large, REL_BUCKETS - 1)
    return jnp.where(n < max_exact, n, large)

def diff_attention(q, k, v, q_pos, k_pos, lam, lam_init, rel_bias, subln_w):
    b, nq = q.shape[:2]
    s = jnp.einsum('bqhd,bkhd->bhqk', q, k).astype(jnp.float32) * (DIFF_HD ** -0.5)
    s = s.reshape(b, DIFF_HEADS, 2, nq, k.shape[1])
    rel = q_pos[:, None] - k_pos[None, :]
    bias = rel_bias.astype(jnp.float32)[rel_bucket(rel)].transpose(2, 0, 1)
    s = jnp.where(rel >= 0, s + bias[None, :, None], -jnp.inf)
    p = jax.nn.softmax(s, axis=-1)
    a = p[:, :, 0] - lam * p[:, :, 1]
    o = jnp.einsum('bhqk,bkhe->bqhe', a, v.astype(jnp.float32))
    o = rmsnorm(o, subln_w) * (1.0 - lam_init)
    return o.reshape(b, nq, DIFF_V_W)

def mem_attention(q, mk, mv):
    b, nq = q.shape[:2]
    s = jnp.einsum('bqhd,bkhd->bhqk', q, mk).astype(jnp.float32) * (MEM_HD ** -0.5)
    p = jax.nn.softmax(s, axis=-1)
    o = jnp.einsum('bhqk,bkhd->bqhd', p, mv.astype(jnp.float32))
    return o.reshape(b, nq, MEM_W)

def peer_ffn(xn, w_q, keys, u, v):
    b, s, d = xn.shape
    t = xn.reshape(b * s, d)
    n = t.shape[0]
    t = jnp.pad(t, ((0, (-n) % PEER_BLOCK), (0, 0)))

    def block(tb):
        nt = tb.shape[0]
        q = (tb @ w_q).reshape(nt, PEER_HEADS, 2, PEER_DK)
        sc = jnp.einsum('thcd,hcnd->thcn', q, keys).astype(jnp.float32)
        s1, i1 = lax.top_k(sc[:, :, 0], PEER_TOPK)
        s2, i2 = lax.top_k(sc[:, :, 1], PEER_TOPK)
        cand_s = (s1[..., :, None] + s2[..., None, :]).reshape(nt, PEER_HEADS, -1)
        cand_i = (i1[..., :, None] * PEER_NKEYS + i2[..., None, :]).reshape(nt, PEER_HEADS, -1)
        top_s, j = lax.top_k(cand_s, PEER_TOPK)
        eid = jnp.take_along_axis(cand_i, j, axis=-1)
        g = jax.nn.softmax(top_s, axis=-1)
        act = jax.nn.gelu(jnp.einsum('thkd,td->thk', u[eid], tb).astype(jnp.float32), approximate=False)
        return jnp.einsum('thk,thkd->td', (g * act).astype(v.dtype), v[eid])

    out = lax.map(block, t.reshape(-1, PEER_BLOCK, d))
    return out.reshape(-1, d)[:n].reshape(b, s, d).astype(xn.dtype)

def decoder_layer(x, pos, ret_state0, mem_k, mem_v, diff_attend, lp):
    b, s, _ = x.shape
    xn = rmsnorm(x, lp['norm_mix_w'])
    z = xn @ lp['w_in']
    offs = [int(o) for o in np.cumsum(IN_SPLITS)[:-1]]
    rq, rk, rv, rg, dq, dk, dv, mq, ga, gb, gc = jnp.split(z, offs, axis=-1)
    rq = rotary(rq.reshape(b, s, RET_HEADS, RET_DK), pos)
    rk = rotary(rk.reshape(b, s, RET_HEADS, RET_DK), pos) * (RET_DK ** -0.5)
    o_r, ret_state = retention(rq, rk, rv.reshape(b, s, RET_HEADS, RET_DV), ret_state0)
    o_r = rmsnorm(o_r).reshape(b, s, RET_V_W) * jax.nn.silu(rg.astype(jnp.float32))
    dk = dk.reshape(b, s, 2 * DIFF_HEADS, DIFF_HD)
    dv = dv.reshape(b, s, DIFF_HEADS, 2 * DIFF_HD)
    o_d = diff_attend(dq.reshape(b, s, 2 * DIFF_HEADS, DIFF_HD), dk, dv)
    o_m = mem_attention(mq.reshape(b, s, MEM_HEADS, MEM_HD), mem_k, mem_v)
    dt = x.dtype
    mixed = (jax.nn.sigmoid(ga.astype(jnp.float32)) * (o_r.astype(dt) @ lp['w_up_ret'])
             + jax.nn.sigmoid(gb.astype(jnp.float32)) * (o_d.astype(dt) @ lp['w_up_diff'])
             + jax.nn.sigmoid(gc.astype(jnp.float32)) * (o_m.astype(dt) @ lp['w_up_mem']))
    h = x + (mixed.astype(dt) @ lp['w_out']).astype(dt)
    h = h + peer_ffn(rmsnorm(h, lp['norm_ffn_w']), lp['peer_w_q'], lp['peer_keys'], lp['peer_u'], lp['peer_v'])
    return h, ret_state, dk, dv

def setup_inputs(seed: int = 0) -> dict:
    key = jax.random.key(seed)
    ks = jax.random.split(key, 32)
    n_pages = PAST_LEN // PAGE_SIZE
    n_phys = (5 * DEC_BATCH * n_pages + 3) // 4
    f32 = jnp.float32

    def nrm(k, shape, scale):
        return jax.random.normal(k, shape, f32) * scale

    def gain(k, shape):
        return 1.0 + 0.05 * jax.random.normal(k, shape, f32)

    page_table = jax.random.permutation(ks[8], n_phys)[: DEC_BATCH * n_pages].reshape(DEC_BATCH, n_pages).astype(jnp.int32)
    return {
        'x_prompt': nrm(ks[0], (BATCH, SEQ, D_MODEL), 1.0),
        'x_sample': nrm(ks[1], (DEC_BATCH, DEC_SEQ, D_MODEL), 1.0),
        'mem_prompt': nrm(ks[2], (BATCH, MEM_TOKENS, D_MODEL), 1.0),
        'state_ret': nrm(ks[3], (DEPTH, DEC_BATCH, RET_HEADS, RET_DK, RET_DV), 0.5),
        'cache_diff_k': nrm(ks[4], (DEPTH, n_phys, PAGE_SIZE, 2 * DIFF_HEADS, DIFF_HD), 1.0),
        'cache_diff_v': nrm(ks[5], (DEPTH, n_phys, PAGE_SIZE, DIFF_HEADS, 2 * DIFF_HD), 1.0),
        'cache_mem_k': nrm(ks[6], (DEPTH, DEC_BATCH, MEM_TOKENS, MEM_HEADS, MEM_HD), 1.0),
        'cache_mem_v': nrm(ks[7], (DEPTH, DEC_BATCH, MEM_TOKENS, MEM_HEADS, MEM_HD), 1.0),
        'page_table': page_table,
        'norm_mix_w': gain(ks[9], (DEPTH, D_MODEL)),
        'norm_mem_w': gain(ks[10], (DEPTH, D_MODEL)),
        'norm_ffn_w': gain(ks[11], (DEPTH, D_MODEL)),
        'norm_final_w': gain(ks[12], (D_MODEL,)),
        'w_in': nrm(ks[13], (DEPTH, D_MODEL, IN_WIDTH), D_MODEL ** -0.5),
        'w_mem_k': nrm(ks[14], (DEPTH, D_MODEL, MEM_W), D_MODEL ** -0.5),
        'w_mem_v': nrm(ks[15], (DEPTH, D_MODEL, MEM_W), D_MODEL ** -0.5),
        'diff_lambda_q1': nrm(ks[16], (DEPTH, DIFF_HD), 0.1),
        'diff_lambda_k1': nrm(ks[17], (DEPTH, DIFF_HD), 0.1),
        'diff_lambda_q2': nrm(ks[18], (DEPTH, DIFF_HD), 0.1),
        'diff_lambda_k2': nrm(ks[19], (DEPTH, DIFF_HD), 0.1),
        'diff_subln_w': gain(ks[20], (DEPTH, 2 * DIFF_HD)),
        'rel_bias': nrm(ks[21], (REL_BUCKETS, DIFF_HEADS), 0.3),
        'w_up_ret': nrm(ks[22], (DEPTH, RET_V_W, D_MODEL), RET_V_W ** -0.5),
        'w_up_diff': nrm(ks[23], (DEPTH, DIFF_V_W, D_MODEL), DIFF_V_W ** -0.5),
        'w_up_mem': nrm(ks[24], (DEPTH, MEM_W, D_MODEL), MEM_W ** -0.5),
        'w_out': nrm(ks[25], (DEPTH, D_MODEL, D_MODEL), D_MODEL ** -0.5),
        'peer_w_q': nrm(ks[26], (DEPTH, D_MODEL, PEER_HEADS * 2 * PEER_DK), D_MODEL ** -0.5),
        'peer_keys': nrm(ks[27], (DEPTH, PEER_HEADS, 2, PEER_NKEYS, PEER_DK), PEER_DK ** -0.5),
        'peer_u': nrm(ks[28], (DEPTH, PEER_EXPERTS, D_MODEL), D_MODEL ** -0.5),
        'peer_v': nrm(ks[29], (DEPTH, PEER_EXPERTS, D_MODEL), 0.25),
    }

def reference(x_prompt, x_sample, mem_prompt, state_ret, cache_diff_k, cache_diff_v, cache_mem_k, cache_mem_v,
              page_table, norm_mix_w, norm_mem_w, norm_ffn_w, norm_final_w, w_in, w_mem_k, w_mem_v,
              diff_lambda_q1, diff_lambda_k1, diff_lambda_q2, diff_lambda_k2, diff_subln_w, rel_bias,
              w_up_ret, w_up_diff, w_up_mem, w_out, peer_w_q, peer_keys, peer_u, peer_v):
    b, s, _ = x_prompt.shape
    db, ds, _ = x_sample.shape
    n_pages = page_table.shape[1]
    past = n_pages * cache_diff_k.shape[2]
    n_mem = mem_prompt.shape[1]
    pos_p = jnp.arange(s, dtype=jnp.int32)
    pos_s = past + jnp.arange(ds, dtype=jnp.int32)
    k_pos_s = jnp.arange(past + ds, dtype=jnp.int32)

    h_p, h_s = x_prompt, x_sample
    rs_p, dk_p, dv_p, mk_ps, mv_ps, rs_s, dk_s, dv_s = [], [], [], [], [], [], [], []
    for l in range(DEPTH):
        lam_init = lambda_init(l)
        lam = (jnp.exp(jnp.sum(diff_lambda_q1[l].astype(jnp.float32) * diff_lambda_k1[l].astype(jnp.float32)))
               - jnp.exp(jnp.sum(diff_lambda_q2[l].astype(jnp.float32) * diff_lambda_k2[l].astype(jnp.float32)))
               + lam_init)
        subln = diff_subln_w[l]
        lp = {'norm_mix_w': norm_mix_w[l], 'norm_ffn_w': norm_ffn_w[l], 'w_in': w_in[l],
              'w_up_ret': w_up_ret[l], 'w_up_diff': w_up_diff[l], 'w_up_mem': w_up_mem[l], 'w_out': w_out[l],
              'peer_w_q': peer_w_q[l], 'peer_keys': peer_keys[l], 'peer_u': peer_u[l], 'peer_v': peer_v[l]}

        mn = rmsnorm(mem_prompt, norm_mem_w[l])
        mk_p = (mn @ w_mem_k[l]).reshape(b, n_mem, MEM_HEADS, MEM_HD)
        mv_p = (mn @ w_mem_v[l]).reshape(b, n_mem, MEM_HEADS, MEM_HD)

        def diff_prompt(q, k, v, lam=lam, lam_init=lam_init, subln=subln):
            nb = s // Q_BLOCK
            qb = q.reshape(b, nb, Q_BLOCK, 2 * DIFF_HEADS, DIFF_HD).transpose(1, 0, 2, 3, 4)

            def blk(args):
                qi, i = args
                q_pos = i * Q_BLOCK + jnp.arange(Q_BLOCK, dtype=jnp.int32)
                return diff_attention(qi, k, v, q_pos, pos_p, lam, lam_init, rel_bias, subln)

            o = lax.map(blk, (qb, jnp.arange(nb, dtype=jnp.int32)))
            return o.transpose(1, 0, 2, 3).reshape(b, s, DIFF_V_W)

        def diff_sample(q, k, v, l=l, lam=lam, lam_init=lam_init, subln=subln):
            pk = cache_diff_k[l][page_table].reshape(db, past, 2 * DIFF_HEADS, DIFF_HD)
            pv = cache_diff_v[l][page_table].reshape(db, past, DIFF_HEADS, 2 * DIFF_HD)
            k_all = jnp.concatenate([pk.astype(k.dtype), k], axis=1)
            v_all = jnp.concatenate([pv.astype(v.dtype), v], axis=1)
            return diff_attention(q, k_all, v_all, pos_s, k_pos_s, lam, lam_init, rel_bias, subln)

        ret0_p = jnp.zeros((b, RET_HEADS, RET_DK, RET_DV), jnp.float32)
        h_p, st_p, k_p, v_p = decoder_layer(h_p, pos_p, ret0_p, mk_p, mv_p, diff_prompt, lp)
        h_s, st_s, k_s, v_s = decoder_layer(h_s, pos_s, state_ret[l], cache_mem_k[l], cache_mem_v[l], diff_sample, lp)
        rs_p.append(st_p); dk_p.append(k_p); dv_p.append(v_p); mk_ps.append(mk_p); mv_ps.append(mv_p)
        rs_s.append(st_s); dk_s.append(k_s); dv_s.append(v_s)

    y_prompt = rmsnorm(h_p, norm_final_w)
    y_sample = rmsnorm(h_s, norm_final_w)
    ret_state_prompt = jnp.stack(rs_p)
    diff_k_prompt = jnp.stack(dk_p)
    diff_v_prompt = jnp.stack(dv_p)
    mem_k_prompt = jnp.stack(mk_ps)
    mem_v_prompt = jnp.stack(mv_ps)
    ret_state_sample = jnp.stack(rs_s)
    diff_k_sample = jnp.stack(dk_s)
    diff_v_sample = jnp.stack(dv_s)
    return (y_prompt, y_sample, ret_state_prompt, diff_k_prompt, diff_v_prompt, mem_k_prompt, mem_v_prompt,
            ret_state_sample, diff_k_sample, diff_v_sample)


_drawn_inputs = setup_inputs


def setup_inputs(seed=0):
    import zlib

    import numpy as np

    out = dict(_drawn_inputs(seed))
    spreads = {}
    factors = {}
    for name, (base, spread) in spreads.items():
        noise = np.random.default_rng([zlib.crc32(name.encode()), seed]).standard_normal(out[name].shape)
        drawn = base * np.exp(spread * noise) if base else spread * noise
        out[name] = __import__('jax').numpy.asarray(drawn.astype(out[name].dtype))
    for name, factor in factors.items():
        out[name] = (out[name] * factor).astype(out[name].dtype)
    return out
```

```python
import math
from contextlib import ExitStack

import numpy as np

import concourse.bass as bass
from concourse import mybir

ALU = mybir.AluOpType
ACT = mybir.ActivationFunctionType
AX = mybir.AxisListType
F32 = mybir.dt.float32
F32R = mybir.dt.float32r
U32 = mybir.dt.uint32
I32 = mybir.dt.int32
ds = bass.ds

P = 128
D_MODEL = 2048
KT = D_MODEL // P
SEQ = 256
DEC_BATCH = 8
DEC_SEQ = 4
PAST = 256
PAGE = 128
N_PAGES = PAST // PAGE
NEW = DEC_BATCH * DEC_SEQ
T = SEQ + NEW
TOKEN_TILES = ((0, P), (P, P), (SEQ, NEW))
RET_HEADS = 8
RET_DK = D_MODEL // 16
RET_DV = 2 * RET_DK
DIFF_HEADS = 8
DIFF_HD = D_MODEL // 32
MEM_TOKENS = 256
MEM_HEADS = 4
MEM_HD = D_MODEL // 16
REL_BUCKETS = 32
REL_MAX_DIST = 128
PEER_HEADS = 8
NKEYS = 128
EXPERTS = NKEYS * NKEYS
TOPK = 16
EPS = 1e-6
LAMBDA_INIT = 0.8 - 0.6 * math.exp(-0.3 * 0)
MASKED = -1e30

RQ, RK, RV, RG, DQ, DK, DV, MQ = 0, 8, 16, 32, 48, 56, 64, 72
Z_TILES = 76
GATE_TILES = 3 * KT
O_RET, O_DIFF, O_MEM, O_TILES = 0, 16, 24, 28


class WeightStream:

    UNITS = 4

    def __init__(self, nc, ctx, psum, name, kt=KT, loads=(1, 1)):
        def sem(what):
            return ctx.enter_context(nc.semaphore(f"{name}_{what}"))

        self.kt = kt
        self.loads = loads
        self.psum = psum
        self.raw = ctx.enter_context(nc.sbuf_tensor(f"{name}_raw", [P, 2, kt, 2 * P], F32))
        self.high = ctx.enter_context(nc.sbuf_tensor(f"{name}_high", [P, 2, kt, P], F32R))
        self.low = ctx.enter_context(nc.sbuf_tensor(f"{name}_low", [P, 2, kt, P], F32R))
        self.loaded = [sem("loaded0"), sem("loaded1")]
        self.high_ready = sem("high_ready")
        self.low_ready = sem("low_ready")
        self.product_done = sem("product_done")
        self.slot_free = sem("slot_free")
        self.bank_free = sem("bank_free")

    def half(self, u):
        return self.raw[:, u // 2, :, (u % 2) * P:(u % 2 + 1) * P]

    def load(self, sp, i, b, columns, first=False):
        if not first:
            sp.wait_ge(self.low_ready, self.UNITS * i - self.UNITS + 2 * b + 2)
        k = 0
        for part in columns:
            sp.dma_start(self.raw[:, b, k:k + part.shape[1], :], part).then_inc(self.loaded[b], 16)
            k += part.shape[1]

    def open(self, pe):
        pe.sem_inc(self.slot_free, 2)
        pe.sem_inc(self.bank_free, 2)

    def wait_product(self, dve, i, u):
        dve.wait_ge(self.product_done, i * self.UNITS + u + 1)
        dve.sem_inc(self.slot_free, 1)

    def split_high(self, act, i, u, kt=None):
        kt = kt or self.kt
        act.wait_ge(self.loaded[u // 2], i * (16 * self.loads[u // 2]) + 16 * self.loads[u // 2])
        act.wait_ge(self.slot_free, i * self.UNITS + u + 1)
        act.activation(self.high[:, u % 2, 0:kt, :], self.half(u)[:, 0:kt, :], ACT.Copy).then_inc(self.high_ready, 1)

    def split_low(self, dve, i, u, kt=None):
        kt = kt or self.kt
        dve.wait_ge(self.high_ready, i * self.UNITS + u + 1)
        dve.tensor_tensor(self.low[:, u % 2, 0:kt, :], self.half(u)[:, 0:kt, :], self.high[:, u % 2, 0:kt, :],
                          ALU.subtract).then_inc(self.low_ready, 1)

    def product(self, pe, i, u, groups):
        n = i * self.UNITS + u + 1
        pe.wait_ge(self.high_ready, n)
        pe.wait_ge(self.bank_free, n)
        for out, k0, (xh, xl) in groups:
            kts = xh.shape[1]
            for k in range(kts):
                w = self.high[:, u % 2, k0 + k, :]
                pe.matmul(out, w, xh[:, k, :], start=(k == 0), stop=False)
                pe.matmul(out, w, xl[:, k, :], start=False, stop=False)
        pe.wait_ge(self.low_ready, n)
        for out, k0, (xh, xl) in groups:
            kts = xh.shape[1]
            for k in range(kts):
                last = pe.matmul(out, self.low[:, u % 2, k0 + k, :], xh[:, k, :], start=False, stop=(k == kts - 1))
        last.then_inc(self.product_done, 1)


def decoder_step_kernel(nc, A, O):
    top = ExitStack()
    with top:
        PS = top.enter_context(nc.psum_tensor("banks", [P, 8, 512], F32))

        def const(name, array):
            t = nc.inline_tensor(np.ascontiguousarray(array, np.float32), name)
            return t.ap() if hasattr(t, "ap") and callable(t.ap) else t

        def scratch(name, shape):
            return nc.dram_tensor(name, shape, F32, kind="Internal").ap()

        C = constants(const)
        S = {"x_T": scratch("x_T", (KT, P, T)), "gates_T": scratch("gates_T", (GATE_TILES, P, T)),
             "bias_rows": scratch("bias_rows", (DIFF_HEADS, P, 512)),
             "peer_weights": scratch("peer_weights", (TOKEN_BLOCKS, P, NKEYS, TB)),
             "mem_T": scratch("mem_T", (2 * MEM_HEADS, P, MEM_TOKENS))}
        ident = top.enter_context(nc.sbuf_tensor("ident", [P, P], F32))
        ones = top.enter_context(nc.sbuf_tensor("ones", [P, P], F32))
        load_constants(nc, C, ident, ones)
        G = dict(PS=PS, ident=ident, ones=ones, A=A, O=O, C=C, S=S)
        memory_projection(nc, G)
        with ExitStack() as left, ExitStack() as right:
            def tensor(stack, side, name, shape, dt=F32):
                return stack.enter_context(nc.sbuf_tensor(name, shape, dt, side=side))

            Z = tensor(left, "left", "Z", [P, Z_TILES, T])
            input_projection(nc, G, Z)
            clear_semaphores(nc)
            ODM = tensor(left, "left", "branch_outputs", [P, DIFF_HEADS + MEM_HEADS, T])
            attention(nc, G, Z, ODM)
            OTH = tensor(right, "right", "o_high", [P, O_TILES, T], F32R)
            OTL = tensor(right, "right", "o_low", [P, O_TILES, T], F32R)
            split_branch_outputs(nc, G, Z, ODM, OTH, OTL)
            clear_semaphores(nc)
            left.close()
            MH = tensor(left, "left", "mixed_high", [P, KT, T], F32R)
            ML = tensor(left, "left", "mixed_low", [P, KT, T], F32R)
            up_projections(nc, G, OTH, OTL, MH, ML)
            right.close()
            hT = tensor(right, "right", "h_T", [P, KT, T])
            output_projection(nc, G, MH, ML, hT)
            left.close()
            XH = tensor(left, "left", "x2_high", [P, KT, T], F32R)
            XL = tensor(left, "left", "x2_low", [P, KT, T], F32R)
            norm_split(nc, G, "ffn", hT, T, A["norm_ffn_w"][0], XH, XL)
            with nc.sbuf_tensor("picks_T", [P, 3, TPAD], F32) as SEL:
                with nc.sbuf_tensor("q_T", [P, 2 * PEER_HEADS, TPAD], F32) as QT:
                    peer_queries(nc, G, XH, XL, QT)
                    peer_selection(nc, G, QT, SEL)
                peer_weights(nc, G, SEL)
            clear_semaphores(nc)
            peer_experts(nc, G, XH, XL, hT)
            norm_split(nc, G, "final", hT, T, A["norm_final_w"], None, None, plain=hT)
            store_outputs(nc, G, hT)


def clear_semaphores(nc):
    free = sorted(nc.free_semaphores)
    with nc.Block() as block:
        @block.gpsimd
        def _(pool):
            runs = [n for n in free if n - 1 not in free]
            for first in runs:
                last = first
                while last + 1 in free:
                    last += 1
                pool.sem_clear(range(first, last + 1))


def constants(const):
    f = np.float32
    C = {"ident": const("c_ident", np.eye(P))}
    half = RET_DK // 2
    inv = f(1.0) / (f(10000.0) ** np.linspace(0.0, 1.0, half, dtype=f))
    pos = np.concatenate([np.arange(SEQ), PAST + np.tile(np.arange(DEC_SEQ), DEC_BATCH)]).astype(f)
    angle = (pos[None, :] * inv[:, None]).astype(f).astype(np.float64)
    cos = np.tile(np.cos(angle), (2, 1))
    sin = np.tile(np.sin(angle), (2, 1))
    scale = RET_DK ** -0.5
    C["cos"] = const("c_cos", np.stack([cos, cos * scale], 1))
    C["sin"] = const("c_sin", np.stack([sin, sin * scale], 1))
    R = np.zeros((P, P))
    for m in range(half):
        R[m + half, m] = -1.0
        R[m, m + half] = 1.0
    C["rotate"] = const("c_rotate", R)
    lg = np.log1p(-np.exp2(-5.0 - np.arange(RET_HEADS)))
    j, i = np.arange(P)[:, None], np.arange(SEQ)[None, :]
    D = np.where(i >= j, np.exp(lg[:, None, None] * np.maximum(i - j, 0)), 0.0)
    C["decay"] = const("c_decay", np.concatenate([D, D[:, :, :P]], 2).transpose(1, 0, 2))
    b, s = np.divmod(np.arange(NEW), DEC_SEQ)
    same = (b[:, None] == b[None, :]) & (s[None, :] >= s[:, None])
    Dn = np.where(same, np.exp(lg[:, None, None] * np.maximum(s[None, :] - s[:, None], 0)), 0.0)
    C["decay_new"] = const("c_decay_new", Dn.transpose(1, 0, 2))
    tok = np.arange(SEQ).reshape(2, P).T
    C["decay_to_end"] = const("c_decay_to_end", np.exp(lg[None, :, None] * (SEQ - 1 - tok[:, None, :])))
    own = (b[:, None] == np.arange(DEC_BATCH)[None, :])
    C["decay_to_end_new"] = const("c_decay_to_end_new", np.exp(lg[None, :, None] * (DEC_SEQ - 1 - s[:, None, None])) * own[:, None, :])
    C["decay_from_state"] = const("c_decay_from_state", np.broadcast_to(np.exp(lg[:, None] * (s[None, :] + 1)), (P, RET_HEADS, NEW)))
    C["decay_state"] = const("c_decay_state", np.broadcast_to(np.exp(lg * DEC_SEQ), (P, RET_HEADS)))
    def bucket(rel):
        n = np.maximum(rel, 0)
        exact = REL_BUCKETS // 2
        nf = np.maximum(n, 1).astype(f)
        large = exact + (np.log(nf / exact) / math.log(REL_MAX_DIST / exact) * (REL_BUCKETS - exact)).astype(np.int32)
        return np.where(n < exact, n, np.minimum(large, REL_BUCKETS - 1))
    rel = 255 - np.arange(512)
    hot = np.zeros((REL_BUCKETS + 1, 512))
    hot[bucket(rel), np.arange(512)] = rel >= 0
    hot[REL_BUCKETS] = np.where(rel < 0, MASKED, 0.0)
    C["buckets"] = const("c_buckets", hot)
    kpos = np.concatenate([np.arange(PAST), PAST + s])
    hot = np.zeros((DEC_SEQ, REL_BUCKETS, PAST + NEW))
    for q in range(DEC_SEQ):
        hot[q, bucket(PAST + q - kpos), np.arange(PAST + NEW)] = 1.0
    C["buckets_new"] = const("c_buckets_new", hot.reshape(P, -1))
    C["own_position"] = const("c_own_position", (np.repeat(np.arange(DEC_SEQ), REL_BUCKETS)[:, None] == np.tile(np.arange(DEC_SEQ), 2)[None, :]))
    rb, rh, rm, rs = np.unravel_index(np.arange(P), (2, DIFF_HEADS, 2, DEC_SEQ))
    mask = np.zeros((P, DEC_BATCH // 2, NEW))
    for pair in range(DEC_BATCH // 2):
        seen = (b[None, :] == 2 * pair + rb[:, None]) & (s[None, :] <= rs[:, None])
        mask[:, pair] = np.where(seen, 0.0, MASKED)
    C["mask_new"] = const("c_mask_new", mask)
    C["map_is_0_1"] = const("c_map_is_0_1", np.stack([rm == 0, rm == 1], 1))
    C["iota"] = const("c_iota", np.broadcast_to(np.arange(P), (P, P)))
    return C


class Stage:

    def __init__(self, nc, ctx, name):
        self.nc, self.ctx, self.name = nc, ctx, name

    def sb(self, what, shape, dt=F32):
        return self.ctx.enter_context(self.nc.sbuf_tensor(f"{self.name}_{what}", shape, dt))

    def sems(self, *names):
        return [self.ctx.enter_context(self.nc.semaphore(f"{self.name}_{w}")) for w in names]


def load_tables(nc, st, tables):
    (loaded,) = st.sems("tables_loaded")
    with nc.Block() as block:
        @block.sync
        def _(sp):
            for dst, src in tables:
                sp.dma_start(dst, src).then_inc(loaded, 16)
            sp.wait_ge(loaded, 16 * len(tables))


def retention(nc, G, Z):
    PS, ident, ones, A, O, C = (G[k] for k in ("PS", "ident", "ones", "A", "O", "C"))
    with ExitStack() as ctx:
        st = Stage(nc, ctx, "ret")
        cos, sin = st.sb("cos", [P, 2, T]), st.sb("sin", [P, 2, T])
        rotate = st.sb("rotate", [P, P])
        decay = st.sb("decay", [P, RET_HEADS, SEQ + P])
        decay_new = st.sb("decay_new", [NEW, RET_HEADS, NEW])
        to_end = st.sb("to_end", [P, RET_HEADS, 2])
        to_end_new = st.sb("to_end_new", [NEW, RET_HEADS, DEC_BATCH])
        from_state = st.sb("from_state", [P, RET_HEADS, NEW])
        state_decay = st.sb("state_decay", [P, RET_HEADS])
        load_tables(nc, st, [(cos[:], C["cos"]), (sin[:], C["sin"]), (rotate[:], C["rotate"]), (decay[:], C["decay"]),
                             (decay_new[:], C["decay_new"]), (to_end[:], C["decay_to_end"]),
                             (to_end_new[:], C["decay_to_end_new"]), (from_state[:], C["decay_from_state"]),
                             (state_decay[:], C["decay_state"])])
        QK = st.sb("qk", [P, 2, T])
        rsin, rcos = st.sb("rsin", [P, 2, T]), st.sb("rcos", [P, 2, T])
        VT = st.sb("vT", [P, 2, T])
        V = st.sb("v", [P, 3, RET_DV])
        KD = st.sb("k_decayed", [P, 2, P])
        KDN = st.sb("k_decayed_new", [NEW, DEC_BATCH, P])
        PT, PTN = st.sb("scores", [P, SEQ + P]), st.sb("scores_new", [NEW, NEW])
        QG = st.sb("q_for_state", [P, NEW])
        ST = st.sb("state", [P, 2, DEC_BATCH, RET_DV])
        NS = st.sb("new_state", [P, DEC_BATCH, RET_DV])
        PST = st.sb("prompt_state", [P, RET_DV])
        SQ = st.sb("squares", [P, 2, T])
        ms, root, rstd, t1, t2, rstd2 = (st.sb(w, [P, T]) for w in ("ms", "root", "rstd", "t1", "t2", "rstd2"))
        ON = st.sb("normed", [P, 2, T])
        (silu_done, vT_ready, rotated, v_turned, v_ready, rope_parts, qk_ready, k_turned, kd_ready, scores_done, pt_ready,
         qg_ready, o_done, states_done, states_added, pstate_done, pstate_ready, squared, summed, rstd_steps, normed, out_ready,
         new_stored, pstate_stored) = st.sems(
            "silu_done", "vT_ready", "rotated", "v_turned", "v_ready", "rope_parts", "qk_ready", "k_turned", "kd_ready",
            "scores_done", "pt_ready", "qg_ready", "o_done", "states_done", "states_added", "pstate_done", "pstate_ready",
            "squared", "summed", "rstd_steps", "normed", "out_ready", "new_stored", "pstate_stored")
        state_loaded = st.sems("state_loaded0", "state_loaded1")
        qk_z = Z[:, RQ:RQ + 16, :].rearrange("p (c h) t -> p h c t", c=2)
        v_z = Z[:, RV:RV + 16, :].rearrange("p (h e) t -> p h e t", e=2)
        g_z = Z[:, RG:RG + 16, :].rearrange("p (h e) t -> p h e t", e=2)
        state_in = A["state_ret"][0].rearrange("b h d e -> h d b e")
        state_out = O["ret_state_sample"][0].rearrange("b h d e -> h d b e")
        with nc.Block() as block:
            @block.sync
            def _(sp):
                for s in range(2):
                    sp.dma_start(ST[:, s, :, :], state_in[s]).then_inc(state_loaded[s], 16)

                def store(h):
                    sp.wait_ge(pstate_ready, h + 1)
                    sp.dma_start(O["ret_state_prompt"][0, 0, h], PST[:]).then_inc(pstate_stored, 16)
                    sp.wait_ge(states_added, h * 4 + 4)
                    sp.dma_start(state_out[h], NS[:]).then_inc(new_stored, 16)

                with sp.Fori(0, RET_HEADS // 2 - 1) as i:
                    for s in range(2):
                        store(i * 2 + s)
                        sp.dma_start(ST[:, s, :, :], state_in[i * 2 + s + 2]).then_inc(state_loaded[s], 16)
                for h in (RET_HEADS - 2, RET_HEADS - 1):
                    store(h)
                sp.wait_ge(pstate_stored, 16 * RET_HEADS)
                sp.wait_ge(new_stored, 16 * RET_HEADS)

            @block.scalar
            def _(act):
                for q in range(4):
                    g = Z[:, RG + 4 * q:RG + 4 * q + 4, :]
                    act.activation(g, g, ACT.Silu).then_inc(silu_done, 1)
                with act.Fori(0, RET_HEADS) as h:
                    act.wait_ge(v_turned, h)
                    act.activation(VT[:], v_z[:, h], ACT.Copy).then_inc(vT_ready, 1)
                    act.wait_ge(v_turned, h + 1)
                    act.wait_ge(states_done, h * 4)
                    act.activation(V[:, 0:2, :], PS[:, 2, :].rearrange("p (t e) -> p t e", t=2), ACT.Copy)
                    act.activation(V[0:NEW, 2, :], PS[0:NEW, 3, 0:RET_DV], ACT.Copy).then_inc(v_ready, 1)
                    act.wait_ge(pstate_done, h + 1)
                    act.wait_ge(pstate_stored, h * 16)
                    act.activation(PST[:], PS[:, 5, 0:RET_DV], ACT.Copy).then_inc(pstate_ready, 1)
                    act.wait_ge(o_done, h + 1)
                    act.wait_ge(summed, h)
                    act.activation(SQ[:], PS[:, 6:8, 0:T], ACT.Square).then_inc(squared, 1)
                    act.wait_ge(rstd_steps, h * 6 + 1)
                    act.activation(root[:], ms[:], ACT.Sqrt).then_inc(rstd_steps, 1)

            @block.vector
            def _(dve):
                with dve.Fori(0, RET_HEADS // 2) as i:
                    for s in range(2):
                        h = i * 2 + s
                        dve.wait_ge(qk_ready, h)
                        dve.tensor_tensor(rcos[:], qk_z[:, h], cos[:], ALU.mult).then_inc(rope_parts, 1)
                        dve.wait_ge(rotated, h + 1)
                        dve.tensor_tensor(rsin[:], PS[:, 0:2, 0:T], sin[:], ALU.mult).then_inc(rope_parts, 1)
                        dve.wait_ge(rope_parts, h * 2 + 2)
                        dve.wait_ge(scores_done, h)
                        dve.wait_ge(qg_ready, h)
                        dve.tensor_tensor(QK[:], rsin[:], rcos[:], ALU.add).then_inc(qk_ready, 1)
                        dve.wait_ge(qk_ready, h + 1)
                        dve.wait_ge(o_done, h)
                        dve.tensor_tensor(QG[:], QK[:, 0, SEQ:T], from_state[:, h, :], ALU.mult).then_inc(qg_ready, 1)
                        dve.wait_ge(k_turned, h + 1)
                        dve.tensor_tensor(KD[:], PS[:, 1, 0:2 * P].rearrange("p (t d) -> p t d", t=2),
                                          to_end[:, h, :].unsqueeze(2).to_broadcast([P, 2, P]), ALU.mult).then_inc(kd_ready, 1)
                        dve.wait_ge(states_done, h * 4)
                        dve.tensor_tensor(KDN[:], PS[0:NEW, 1, 2 * P:3 * P].unsqueeze(1).to_broadcast([NEW, DEC_BATCH, P]),
                                          to_end_new[:, h, :].unsqueeze(2).to_broadcast([NEW, DEC_BATCH, P]), ALU.mult).then_inc(kd_ready, 1)
                        dve.wait_ge(scores_done, h + 1)
                        dve.tensor_tensor(PT[:], PS[:, 4, 0:SEQ + P], decay[:, h, :], ALU.mult).then_inc(pt_ready, 1)
                        dve.tensor_tensor(PTN[:], PS[0:NEW, 4, 3 * P:3 * P + NEW], decay_new[:, h, :], ALU.mult).then_inc(pt_ready, 1)
                        dve.wait_ge(new_stored, h * 16)
                        dve.wait_ge(state_loaded[s], i * 16 + 16)
                        for r in range(4):
                            dve.wait_ge(states_done, h * 4 + r + 1)
                            dve.scalar_tensor_tensor(out=NS[:, 2 * r:2 * r + 2, :], in0=ST[:, s, 2 * r:2 * r + 2, :],
                                                     scalar=state_decay[:, ds(h, 1)],
                                                     in1=PS[:, 2 + r % 2, :].rearrange("p (b e) -> p b e", b=2),
                                                     op0=ALU.mult, op1=ALU.add).then_inc(states_added, 1)
                        dve.wait_ge(summed, h + 1)
                        dve.tensor_scalar(ms[:], PS[:, 0, 0:T], float(P) / RET_DV, EPS, ALU.mult, ALU.add).then_inc(rstd_steps, 1)
                        dve.wait_ge(rstd_steps, h * 6 + 2)
                        dve.reciprocal(rstd[:], root[:]).then_inc(rstd_steps, 1)
                        refine_rstd(dve, ms, rstd, t1, t2, rstd2, rstd_steps, h * 6 + 3)
                        dve.wait_ge(rstd_steps, h * 6 + 6)
                        dve.wait_ge(out_ready, h)
                        dve.tensor_tensor(ON[:], PS[:, 6:8, 0:T], rstd2[:].unsqueeze(1).to_broadcast([P, 2, T]), ALU.mult).then_inc(normed, 1)
                        dve.wait_ge(normed, h + 1)
                        dve.wait_ge(silu_done, 4)
                        dve.tensor_tensor(g_z[:, h], ON[:], g_z[:, h], ALU.mult).then_inc(out_ready, 1)

            @block.tensor
            def _(pe):
                with pe.Fori(0, RET_HEADS // 2) as i:
                    for s in range(2):
                        h = i * 2 + s
                        pe.wait_ge(rstd_steps, h * 6)
                        pe.wait_ge(rope_parts, h * 2)
                        pe.matmul(PS[:, 0, 0:T], rotate[:], qk_z[:, h, 0, :], start=True, stop=True)
                        pe.matmul(PS[:, 1, 0:T], rotate[:], qk_z[:, h, 1, :], start=True, stop=True).then_inc(rotated, 1)
                        pe.wait_ge(vT_ready, h + 1)
                        pe.wait_ge(states_added, h * 4)
                        for e in range(2):
                            for t in range(2):
                                pe.transpose(PS[:, 2, t * RET_DV + e * P:t * RET_DV + (e + 1) * P], VT[:, e, t * P:(t + 1) * P], ident[:])
                            last = pe.transpose(PS[0:NEW, 3, e * P:(e + 1) * P], VT[:, e, SEQ:T], ident[:])
                        last.then_inc(v_turned, 1)
                        pe.wait_ge(qk_ready, h + 1)
                        for t in range(2):
                            pe.transpose(PS[:, 1, t * P:(t + 1) * P], QK[:, 1, t * P:(t + 1) * P], ident[:])
                        pe.transpose(PS[0:NEW, 1, 2 * P:3 * P], QK[:, 1, SEQ:T], ident[:]).then_inc(k_turned, 1)
                        pe.wait_ge(pt_ready, h * 2)
                        pe.matmul(PS[:, 4, 0:SEQ], QK[:, 1, 0:P], QK[:, 0, 0:SEQ], start=True, stop=True)
                        pe.matmul(PS[:, 4, SEQ:SEQ + P], QK[:, 1, P:SEQ], QK[:, 0, P:SEQ], start=True, stop=True)
                        pe.matmul(PS[0:NEW, 4, 3 * P:3 * P + NEW], QK[:, 1, SEQ:T], QK[:, 0, SEQ:T], start=True, stop=True).then_inc(scores_done, 1)
                        pe.wait_ge(v_ready, h + 1)
                        pe.wait_ge(kd_ready, h * 2 + 2)
                        pe.wait_ge(pt_ready, h * 2 + 2)
                        pe.wait_ge(pstate_ready, h)
                        for t in range(2):
                            last = pe.matmul(PS[:, 5, 0:RET_DV], KD[:, t, :], V[:, t, :], start=(t == 0), stop=(t == 1))
                        last.then_inc(pstate_done, 1)
                        pe.wait_ge(qg_ready, h + 1)
                        pe.wait_ge(normed, h)
                        pe.wait_ge(state_loaded[s], i * 16 + 16)
                        for e in range(2):
                            es = slice(e * P, (e + 1) * P)
                            pe.matmul(PS[:, 6 + e, 0:SEQ], V[:, 0, es], PT[:, 0:SEQ], start=True, stop=False, skip_group_check=True)
                            pe.matmul(PS[:, 6 + e, P:SEQ], V[:, 1, es], PT[:, SEQ:SEQ + P], start=False, stop=False, skip_group_check=True)
                            pe.matmul(PS[:, 6 + e, SEQ:T], V[0:NEW, 2, es], PTN[:], start=False, stop=False, skip_group_check=True)
                            for b in range(DEC_BATCH):
                                c = slice(b * DEC_SEQ, (b + 1) * DEC_SEQ)
                                last = pe.matmul(PS[:, 6 + e, SEQ + b * DEC_SEQ:SEQ + (b + 1) * DEC_SEQ], ST[:, s, b, es], QG[:, c],
                                                 start=False, stop=(b == DEC_BATCH - 1), skip_group_check=True)
                        last.then_inc(o_done, 1)
                        for r in range(4):
                            if r >= 2:
                                pe.wait_ge(states_added, h * 4 + r - 1)
                            for b in (2 * r, 2 * r + 1):
                                last = pe.matmul(PS[:, 2 + r % 2, (b % 2) * RET_DV:(b % 2 + 1) * RET_DV], KDN[:, b, :],
                                                 V[0:NEW, 2, :], start=True, stop=True)
                            last.then_inc(states_done, 1)
                        pe.wait_ge(squared, h + 1)
                        for e in range(2):
                            last = pe.matmul(PS[:, 0, 0:T], ones[:], SQ[:, e, :], start=(e == 0), stop=(e == 1))
                        last.then_inc(summed, 1)


def refine_rstd(dve, ms, rstd, t1, t2, out, steps, n):
    dve.wait_ge(steps, n)
    dve.tensor_tensor(t1[:], ms[:], rstd[:], ALU.mult).then_inc(steps, 1)
    dve.wait_ge(steps, n + 1)
    dve.scalar_tensor_tensor(out=t2[:], in0=t1[:], scalar=-0.5, in1=rstd[:], op0=ALU.mult, op1=ALU.mult).then_inc(steps, 1)
    dve.wait_ge(steps, n + 2)
    dve.scalar_tensor_tensor(out=out[:], in0=t2[:], scalar=1.5, in1=rstd[:], op0=ALU.add, op1=ALU.mult).then_inc(steps, 1)


def load_constants(nc, C, ident, ones):
    with nc.semaphore("ident_loaded") as ident_loaded, nc.semaphore("ones_set") as ones_set, nc.Block() as block:
        @block.sync
        def _(sp):
            sp.dma_start(ident[:], C["ident"]).then_inc(ident_loaded, 16)
            sp.wait_ge(ident_loaded, 16)

        @block.vector
        def _(dve):
            dve.memset(ones[:], 1.0 / P).then_inc(ones_set, 1)
            dve.wait_ge(ones_set, 1)


def transposed_norm(nc, G, ctx, name, source, rows, gain, XH, XL, spill=None):
    PS, ident = G["PS"], G["ident"]
    n = sum(r for _, r, _ in rows)
    with ExitStack() as ctx:
        sem = lambda what: ctx.enter_context(nc.semaphore(f"{name}_{what}"))
        x = ctx.enter_context(nc.sbuf_tensor(f"{name}_x", [P, 1, D_MODEL], F32))
        xT = ctx.enter_context(nc.sbuf_tensor(f"{name}_xT", [P, KT, n], F32))
        x_loaded, x_used, transposed, xT_ready, spilled = (sem(w) for w in ("x_loaded", "x_used", "transposed", "xT_ready", "spilled"))
        bank_free = sem("bank_free")
        with nc.Block() as block:
            @block.sync
            def _(sp):
                for i, (_, r, src) in enumerate(rows):
                    if i:
                        sp.wait_ge(transposed, 4 * i)
                    sp.dma_start(x[0:r, 0, :], src).then_inc(x_loaded, 16)
                if spill is not None:
                    sp.wait_ge(xT_ready, 4 * len(rows))
                    sp.dma_start(spill.rearrange("k p t -> p k t"), xT[:]).then_inc(spilled, 16)
                    sp.wait_ge(spilled, 16)

            @block.tensor
            def _(pe):
                for i, (_, r, _src) in enumerate(rows):
                    pe.wait_ge(x_loaded, 16 * (i + 1))
                    for g in range(4):
                        q = 4 * i + g
                        if q >= 4:
                            pe.wait_ge(xT_ready, q - 3)
                        for j in range(4):
                            k = 4 * g + j
                            last = pe.transpose(PS[:, q % 4, j * P:j * P + r], x[0:r, 0, k * P:(k + 1) * P], ident[0:r, 0:r])
                        last.then_inc(transposed, 1)

            @block.vector
            def _(dve):
                for i, (t0, r, _src) in enumerate(rows):
                    for g in range(4):
                        q = 4 * i + g
                        dve.wait_ge(transposed, q + 1)
                        dve.tensor_copy(xT[:, 4 * g:4 * g + 4, t0:t0 + r],
                                        PS[:, q % 4, :].rearrange("p (j t) -> p j t", j=4)[:, :, 0:r]).then_inc(xT_ready, 1)
        norm_split(nc, G, name, xT, n, gain, XH, XL)


def norm_split(nc, G, name, xT, n, gain, XH, XL, plain=None):
    PS, ones = G["PS"], G["ones"]
    with ExitStack() as ctx:
        sem = lambda what: ctx.enter_context(nc.semaphore(f"{name}_{what}"))
        sq = ctx.enter_context(nc.sbuf_tensor(f"{name}_sq", [P, 2, n], F32))
        xn = ctx.enter_context(nc.sbuf_tensor(f"{name}_xn", [P, 2, n], F32))
        ms, root, raw_rstd, t1, t2, rstd = (ctx.enter_context(nc.sbuf_tensor(f"{name}_{w}", [P, n], F32))
                                            for w in ("ms", "root", "raw_rstd", "t1", "t2", "rstd"))
        g = ctx.enter_context(nc.sbuf_tensor(f"{name}_gain", [P, KT], F32))
        gain_loaded, squared, summed, rstd_steps, normed, high, low = (
            sem(w) for w in ("gain_loaded", "squared", "summed", "rstd_steps", "normed", "high", "low"))
        with nc.Block() as block:
            @block.sync
            def _(sp):
                with nc.allow_non_contiguous_dma(reason="one gain per partition"):
                    sp.dma_start(g[:], gain.rearrange("(k p) -> p k", p=P)).then_inc(gain_loaded, 16)

            @block.scalar
            def _(act):
                for k in range(KT):
                    if k >= 2:
                        act.wait_ge(summed, k - 1)
                    act.activation(sq[:, k % 2, :], xT[:, k, :], ACT.Square).then_inc(squared, 1)
                act.wait_ge(rstd_steps, 1)
                act.activation(root[:], ms[:], ACT.Sqrt).then_inc(rstd_steps, 1)
                for k in range(KT) if plain is None else ():
                    act.wait_ge(normed, k + 1)
                    act.activation(XH[:, k, 0:n], xn[:, k % 2, :], ACT.Copy).then_inc(high, 1)

            @block.tensor
            def _(pe):
                for k in range(KT):
                    pe.wait_ge(squared, k + 1)
                    pe.matmul(PS[:, 0, 0:n], ones[:], sq[:, k % 2, :], start=(k == 0), stop=(k == KT - 1)).then_inc(summed, 1)

            @block.vector
            def _(dve):
                dve.wait_ge(summed, KT)
                dve.tensor_scalar(ms[:], PS[:, 0, 0:n], 1.0 / KT, EPS, ALU.mult, ALU.add).then_inc(rstd_steps, 1)
                dve.wait_ge(rstd_steps, 2)
                dve.reciprocal(raw_rstd[:], root[:]).then_inc(rstd_steps, 1)
                refine_rstd(dve, ms, raw_rstd, t1, t2, rstd, rstd_steps, 3)
                dve.wait_ge(rstd_steps, 6)
                dve.wait_ge(gain_loaded, 16)
                for k in range(KT) if plain is not None else ():
                    dve.scalar_tensor_tensor(out=plain[:, k, :], in0=xT[:, k, :], scalar=g[:, k:k + 1], in1=rstd[:],
                                             op0=ALU.mult, op1=ALU.mult).then_inc(normed, 1)
                for k in range(KT + 1) if plain is None else ():
                    if k < KT:
                        if k >= 2:
                            dve.wait_ge(low, k - 1)
                        dve.scalar_tensor_tensor(out=xn[:, k % 2, :], in0=xT[:, k, :], scalar=g[:, k:k + 1], in1=rstd[:],
                                                 op0=ALU.mult, op1=ALU.mult).then_inc(normed, 1)
                    if k:
                        dve.wait_ge(high, k)
                        dve.tensor_tensor(XL[:, k - 1, 0:n], xn[:, (k - 1) % 2, :], XH[:, k - 1, 0:n],
                                          ALU.subtract).then_inc(low, 1)


def memory_projection(nc, G):
    A = G["A"]
    with ExitStack() as ctx:
        MH = ctx.enter_context(nc.sbuf_tensor("mem_high", [P, KT, MEM_TOKENS], F32R))
        ML = ctx.enter_context(nc.sbuf_tensor("mem_low", [P, KT, MEM_TOKENS], F32R))
        mem = A["mem_prompt"][0]
        transposed_norm(nc, G, ctx, "mem", None, [(0, P, mem[0:P]), (P, P, mem[P:2 * P])], A["norm_mem_w"][0], MH, ML)
        w = WeightStream(nc, ctx, G["PS"], "wmem")
        out = ctx.enter_context(nc.sbuf_tensor("mem_kv_T", [P, 4, MEM_TOKENS], F32))
        projected = ctx.enter_context(nc.semaphore("mem_projected"))
        stored = ctx.enter_context(nc.semaphore("mem_stored"))
        ws = [A[n][0].rearrange("(k p) n -> p k n", p=P) for n in ("w_mem_k", "w_mem_v")]
        with nc.Block() as block:
            @block.sync
            def _(sp):
                for i in range(2):
                    for b in range(2):
                        w.load(sp, i, b, [ws[i][:, :, b * 2 * P:(b + 1) * 2 * P]], first=(i == 0))
                for i in range(2):
                    sp.wait_ge(projected, i + 1)
                    sp.dma_start(G["S"]["mem_T"][4 * i:4 * i + 4].rearrange("k p t -> p k t"), out[:]).then_inc(stored, 16)
                sp.wait_ge(stored, 32)

            @block.scalar
            def _(act):
                for i in range(2):
                    for u in range(4):
                        w.split_high(act, i, u)

            @block.tensor
            def _(pe):
                w.open(pe)
                for i in range(2):
                    for u in range(4):
                        w.product(pe, i, u, [(w.psum[:, u % 2, 0:MEM_TOKENS], 0, (MH, ML))])

            @block.vector
            def _(dve):
                for i in range(2):
                    for u in range(4):
                        w.split_low(dve, i, u)
                        dve.wait_ge(w.product_done, 4 * i + u + 1)
                        if i:
                            dve.wait_ge(stored, 16 * i)
                        dve.tensor_copy(out[:, u, :], w.psum[:, u % 2, 0:MEM_TOKENS]).then_inc(w.bank_free, 1)
                        dve.sem_inc(w.slot_free, 1)
                        if u == 3:
                            dve.wait_ge(w.bank_free, 2 + 4 * i + u + 1)
                            dve.sem_inc(projected, 1)


def input_projection(nc, G, Z):
    A, S = G["A"], G["S"]
    with ExitStack() as ctx:
        XH = ctx.enter_context(nc.sbuf_tensor("x_high", [P, KT, T], F32R))
        XL = ctx.enter_context(nc.sbuf_tensor("x_low", [P, KT, T], F32R))
        xp = A["x_prompt"][0]
        xs = A["x_sample"].rearrange("b s d -> (b s) d")
        transposed_norm(nc, G, ctx, "x", None, [(0, P, xp[0:P]), (P, P, xp[P:2 * P]), (SEQ, NEW, xs)],
                        A["norm_mix_w"][0], XH, XL, spill=S["x_T"])
        w = WeightStream(nc, ctx, G["PS"], "win")
        gates = ctx.enter_context(nc.sbuf_tensor("gates", [P, 4, T], F32))
        gates_ready = ctx.enter_context(nc.semaphore("gates_ready"))
        gates_stored = ctx.enter_context(nc.semaphore("gates_stored"))
        win = A["w_in"][0].rearrange("(k p) n -> p k n", p=P)
        ZI = Z_TILES // 4
        GI = GATE_TILES // 4
        gates_dram = S["gates_T"].rearrange("(i u) p t -> i p u t", u=4)
        with nc.Block() as block:
            @block.sync
            def _(sp):
                for b in range(2):
                    w.load(sp, 0, b, [win[:, :, ds(b * 2 * P, 2 * P)]], first=True)
                with sp.Fori(1, ZI + 1) as i:
                    for b in range(2):
                        w.load(sp, i, b, [win[:, :, ds(i * 512 + b * 2 * P, 2 * P)]])
                with sp.Fori(0, GI - 1) as g:
                    for b in range(2):
                        w.load(sp, g + ZI + 1, b, [win[:, :, ds(g * 512 + (ZI + 1) * 512 + b * 2 * P, 2 * P)]])
                    sp.wait_ge(gates_ready, g + 1)
                    sp.dma_start(gates_dram[g], gates[:]).then_inc(gates_stored, 16)
                sp.wait_ge(gates_ready, GI)
                sp.dma_start(gates_dram[GI - 1], gates[:]).then_inc(gates_stored, 16)
                sp.wait_ge(gates_stored, 16 * GI)

            @block.scalar
            def _(act):
                with act.Fori(0, ZI + GI) as i:
                    for u in range(4):
                        w.split_high(act, i, u)

            @block.tensor
            def _(pe):
                w.open(pe)
                with pe.Fori(0, ZI + GI) as i:
                    for u in range(4):
                        w.product(pe, i, u, [(w.psum[:, u % 2, 0:T], 0, (XH, XL))])

            @block.vector
            def _(dve):
                with dve.Fori(0, ZI) as i:
                    for u in range(4):
                        w.split_low(dve, i, u)
                        dve.wait_ge(w.product_done, i * 4 + u + 1)
                        dve.sem_inc(w.slot_free, 1)
                        dve.tensor_copy(Z[:, i * 4 + u, :], w.psum[:, u % 2, 0:T]).then_inc(w.bank_free, 1)
                with dve.Fori(0, GI) as g:
                    for u in range(4):
                        w.split_low(dve, g + ZI, u)
                        dve.wait_ge(w.product_done, g * 4 + 4 * ZI + u + 1)
                        dve.sem_inc(w.slot_free, 1)
                        if u == 0:
                            dve.wait_ge(gates_stored, g * 16)
                        dve.tensor_copy(gates[:, u, :], w.psum[:, u % 2, 0:T]).then_inc(w.bank_free, 1)
                        if u == 3:
                            dve.wait_ge(w.bank_free, g * 4 + 4 * ZI + 2 + 4)
                            dve.sem_inc(gates_ready, 1)


def diff_tables(nc, G, st):
    PS, A, C, S = (G[k] for k in ("PS", "A", "C", "S"))
    bias = st.sb("bias", [P, DIFF_HEADS, SEQ + P])
    bias_new = st.sb("bias_new", [P, PAST])
    bias_own = st.sb("bias_own", [P, DEC_BATCH // 2, NEW])
    neg_lam = st.sb("neg_lam", [P, 1])
    map_weights = st.sb("map_weights", [P, 4])
    row_weights = st.sb("row_weights", [P, 1])
    with ExitStack() as ctx:
        t = Stage(nc, ctx, "tab")
        rb = t.sb("rel_bias", [REL_BUCKETS + 1, DIFF_HEADS])
        rb_wide = t.sb("rel_bias_wide", [REL_BUCKETS + 1, DIFF_HEADS, P])
        buckets = t.sb("buckets", [REL_BUCKETS + 1, 512])
        rows = t.sb("bias_rows", [P, 2, 512])
        rb4 = t.sb("rel_bias_by_position", [P, DIFF_HEADS])
        own_pos = t.sb("own_position", [P, 8])
        picks = t.sb("picks", [P, 2, DIFF_HEADS, 8])
        buckets_new = t.sb("buckets_new", [P, PAST + NEW])
        mask_new = t.sb("mask_new", [P, DEC_BATCH // 2, NEW])
        lq = t.sb("lambda_parts", [P, 4, DIFF_HD])
        lp, le = t.sb("lambda_products", [P, 2, DIFF_HD]), t.sb("lambda_sums", [P, 2])
        lexp, ld = t.sb("lambda_exps", [P, 2]), t.sb("lambda_difference", [P, 1])
        maps = t.sb("maps", [P, 2])
        stored = t.sems("stored0", "stored1")
        ones_row, loaded, wide, biased, rows_ready, picked, new_done, lam_steps, read = t.sems(
            "ones_row", "loaded", "wide", "biased", "rows_ready", "picked", "new_done", "lam_steps", "read")
        with nc.Block() as block:
            @block.sync
            def _(sp):
                n = 0
                for dst, src in [(rb[0:REL_BUCKETS, :], A["rel_bias"]), (buckets[:], C["buckets"]),
                                 (own_pos[:], C["own_position"]), (buckets_new[:], C["buckets_new"]),
                                 (mask_new[:], C["mask_new"]), (maps[:], C["map_is_0_1"])] + [
                                     (rb4[q * REL_BUCKETS:(q + 1) * REL_BUCKETS, :], A["rel_bias"]) for q in range(DEC_SEQ)] + [
                                     (lq[:, j, :], A[k][0].partition_broadcast(P)) for j, k in enumerate(
                                         ("diff_lambda_q1", "diff_lambda_k1", "diff_lambda_q2", "diff_lambda_k2"))]:
                    sp.dma_start(dst, src).then_inc(loaded, 16)
                    n += 16
                G["table_loads"] = n
                for h in range(DIFF_HEADS):
                    sp.wait_ge(rows_ready, h + 1)
                    sp.dma_start(S["bias_rows"][h], rows[:, h % 2, :]).then_inc(stored[h % 2], 16)
                for b in range(2):
                    sp.wait_ge(stored[b], 16 * DIFF_HEADS // 2)
                whole = S["bias_rows"]
                skewed = bass.AP(whole.tensor, P - 1, [[511, P], [P * 512, DIFF_HEADS], [1, SEQ + P]])
                sp.dma_start(bias[:], skewed).then_inc(read, 16)
                sp.wait_ge(read, 16)
            n_loads = G["table_loads"]

            @block.vector
            def _(dve):
                dve.memset(rb[REL_BUCKETS:REL_BUCKETS + 1, :], 1.0).then_inc(ones_row, 1)
                dve.wait_ge(ones_row, 1)
                dve.wait_ge(loaded, n_loads)
                dve.tensor_copy(rb_wide[:], rb[:].unsqueeze(2).to_broadcast([REL_BUCKETS + 1, DIFF_HEADS, P])).then_inc(wide, 1)
                for b in range(2):
                    dve.tensor_tensor(picks[:, b], rb4[:].unsqueeze(2).to_broadcast([P, DIFF_HEADS, 8]),
                                      own_pos[:].unsqueeze(1).to_broadcast([P, DIFF_HEADS, 8]), ALU.mult).then_inc(picked, 1)
                for h in range(DIFF_HEADS):
                    dve.wait_ge(biased, h + 1)
                    if h >= 2:
                        dve.wait_ge(stored[h % 2], 16 * (h // 2))
                    dve.tensor_copy(rows[:, h % 2, :], PS[:, h % 4, :]).then_inc(rows_ready, 1)
                dve.wait_ge(new_done, 1)
                dve.tensor_copy(bias_new[:], PS[:, 4, 0:PAST])
                dve.tensor_tensor(bias_own[:], PS[:, 4, PAST:PAST + NEW].unsqueeze(1).to_broadcast([P, DEC_BATCH // 2, NEW]),
                                  mask_new[:], ALU.add)
                for j in range(2):
                    dve.tensor_tensor_reduce(lp[:, j, :], lq[:, 2 * j, :], lq[:, 2 * j + 1, :], 1.0, 0.0, ALU.mult, ALU.add,
                                             le[:, j:j + 1]).then_inc(lam_steps, 1)
                dve.wait_ge(lam_steps, 3)
                dve.tensor_tensor(ld[:], lexp[:, 1:2], lexp[:, 0:1], ALU.subtract).then_inc(lam_steps, 1)
                dve.wait_ge(lam_steps, 4)
                dve.tensor_scalar(neg_lam[:], ld[:], -LAMBDA_INIT, None, ALU.add).then_inc(lam_steps, 1)
                dve.wait_ge(lam_steps, 5)
                dve.memset(map_weights[:], 1.0).then_inc(lam_steps, 1)
                dve.wait_ge(lam_steps, 6)
                dve.tensor_scalar(map_weights[:, 2:4], map_weights[:, 2:4], neg_lam[:], None, ALU.mult)
                dve.scalar_tensor_tensor(out=row_weights[:], in0=maps[:, 1:2], scalar=neg_lam[:], in1=maps[:, 0:1],
                                         op0=ALU.mult, op1=ALU.add)

            @block.scalar
            def _(act):
                act.wait_ge(lam_steps, 2)
                act.activation(lexp[:], le[:], ACT.Exp).then_inc(lam_steps, 1)

            @block.tensor
            def _(pe):
                pe.wait_ge(wide, 1)
                for h in range(DIFF_HEADS):
                    if h >= 4:
                        pe.wait_ge(rows_ready, h - 3)
                    pe.matmul(PS[:, h % 4, :], rb_wide[:, h, :], buckets[:], start=True, stop=True).then_inc(biased, 1)
                pe.wait_ge(picked, 2)
                pe.matmul(PS[:, 4, 0:PAST + NEW], picks[:].rearrange("p b h m -> p (b h m)"), buckets_new[:], start=True, stop=True).then_inc(new_done, 1)
    return bias, bias_new, bias_own, map_weights, row_weights


def diff_prompt(nc, G, Z, OD, v_new, bias, map_weights):
    PS, ident, O = (G[k] for k in ("PS", "ident", "O"))
    with ExitStack() as ctx:
        st = Stage(nc, ctx, "dp")
        QKV = st.sb("qkv_T", [P, 3, T])
        KV = st.sb("kv", [P, 2, 3, P])
        S, E = st.sb("scores", [P, 2, 2, SEQ]), st.sb("exps", [P, 2, 2, SEQ])
        A1, A_ = st.sb("second_map", [P, 2, SEQ]), st.sb("a", [P, 2, SEQ])
        AT = st.sb("a_T", [P, SEQ + P])
        mx, nmx, sums, rec, coef = (st.sb(w, [P, 4]) for w in ("max", "neg_max", "sums", "reciprocals", "coefficients"))
        (staged, turned, kv_ready, scores_done, biased, soft, exps, parts, a_ready, a_turned, aT_ready, o_done, o_ready,
         kv_stored) = st.sems("staged", "turned", "kv_ready", "scores_done", "biased", "soft", "exps", "parts", "a_ready",
                              "a_turned", "aT_ready", "o_done", "o_ready", "kv_stored")
        qkv_z = Z[:, DQ:DQ + 24, :].rearrange("p (c h) t -> p h c t", c=3)
        outs = []
        for c, (prompt, new) in enumerate((("diff_k_prompt", "diff_k_sample"), ("diff_v_prompt", "diff_v_sample"))):
            outs.append((O[prompt][0, 0].rearrange("(t p) m d -> p t (m d)", p=P), O[new][0].rearrange("b s m d -> (b s) (m d)")))
        with nc.Block() as block:
            @block.sync
            def _(sp):
                with sp.Fori(0, DIFF_HEADS) as h:
                    sp.wait_ge(kv_ready, h + 1)
                    for c in range(2):
                        sp.dma_start(outs[c][0][:, :, ds(h * P, P)], KV[:, c, 0:2, :]).then_inc(kv_stored, 16)
                        sp.dma_start(outs[c][1][:, ds(h * P, P)], KV[0:NEW, c, 2, :]).then_inc(kv_stored, 16)
                sp.wait_ge(kv_stored, 64 * DIFF_HEADS)

            @block.scalar
            def _(act):
                with act.Fori(0, DIFF_HEADS) as h:
                    act.wait_ge(scores_done, h)
                    act.activation(QKV[:], qkv_z[:, h], ACT.Copy).then_inc(staged, 1)
                    act.wait_ge(turned, h + 1)
                    act.wait_ge(kv_stored, h * 64)
                    act.wait_ge(o_done, h)
                    act.activation(KV[:, :, 0:2, :], PS[:, 0:2, 0:2 * P].rearrange("p c (t d) -> p c t d", t=2), ACT.Copy)
                    act.activation(v_new[:, ds(h * P, P)], PS[0:NEW, 1, 2 * P:3 * P], ACT.Copy)
                    act.activation(KV[0:NEW, :, 2, :], PS[0:NEW, 0:2, 2 * P:3 * P], ACT.Copy).then_inc(kv_ready, 1)
                    act.wait_ge(soft, h * 4 + 2)
                    act.wait_ge(a_ready, h * 2)
                    for j in range(4):
                        act.activation(E[:, j // 2, j % 2, :], S[:, j // 2, j % 2, :], ACT.Exp, bias=nmx[:, j:j + 1],
                                       accum_out=sums[:, j:j + 1]).then_inc(exps, 1)
                    act.wait_ge(a_turned, h + 1)
                    act.wait_ge(o_done, h)
                    act.activation(AT[:], PS[:, 4, 0:SEQ + P], ACT.Copy).then_inc(aT_ready, 1)
                    act.wait_ge(o_done, h + 1)
                    act.activation(OD[:, h, 0:SEQ], PS[:, 5, 0:SEQ], ACT.Copy).then_inc(o_ready, 1)

            @block.vector
            def _(dve):
                with dve.Fori(0, DIFF_HEADS) as h:
                    dve.wait_ge(scores_done, h + 1)
                    dve.wait_ge(exps, h * 4)
                    dve.wait_ge(soft, h * 4)
                    for q in range(2):
                        tile = bias[:, h, P - q * P:P - q * P + SEQ]
                        dve.scalar_tensor_tensor(out=S[:, :, q, :], in0=PS[:, 2:4, q * SEQ:(q + 1) * SEQ], scalar=DIFF_HD ** -0.5,
                                                 in1=tile.unsqueeze(1).to_broadcast([P, 2, SEQ]), op0=ALU.mult, op1=ALU.add).then_inc(biased, 1)
                    dve.wait_ge(biased, h * 2 + 2)
                    dve.tensor_reduce(mx[:], S[:].rearrange("p m q k -> p (m q) k"), AX.X, ALU.max).then_inc(soft, 1)
                    dve.wait_ge(soft, h * 4 + 1)
                    dve.tensor_scalar(nmx[:], mx[:], -1.0, None, ALU.mult).then_inc(soft, 1)
                    dve.wait_ge(exps, h * 4 + 4)
                    dve.reciprocal(rec[:], sums[:]).then_inc(soft, 1)
                    dve.wait_ge(soft, h * 4 + 3)
                    dve.wait_ge(a_ready, h * 2)
                    dve.tensor_tensor(coef[:], rec[:], map_weights[:], ALU.mult).then_inc(soft, 1)
                    dve.wait_ge(soft, h * 4 + 4)
                    for q in range(2):
                        dve.tensor_scalar(A1[:, q, :], E[:, 1, q, :], coef[:, 2 + q:3 + q], None, ALU.mult).then_inc(parts, 1)
                    dve.wait_ge(a_turned, h)
                    for q in range(2):
                        dve.wait_ge(parts, h * 2 + 1 + q)
                        dve.scalar_tensor_tensor(out=A_[:, q, :], in0=E[:, 0, q, :], scalar=coef[:, q:q + 1], in1=A1[:, q, :],
                                                 op0=ALU.mult, op1=ALU.add).then_inc(a_ready, 1)

            @block.tensor
            def _(pe):
                with pe.Fori(0, DIFF_HEADS) as h:
                    pe.wait_ge(staged, h + 1)
                    pe.wait_ge(kv_ready, h)
                    for c in range(2):
                        for t, (t0, r) in enumerate(TOKEN_TILES):
                            last = pe.transpose(PS[0:r, c, t * P:(t + 1) * P], QKV[:, 1 + c, t0:t0 + r], ident[:])
                    last.then_inc(turned, 1)
                    pe.wait_ge(biased, h * 2)
                    for m in range(2):
                        rows = slice(m * DIFF_HD, (m + 1) * DIFF_HD)
                        for q in range(2):
                            last = pe.matmul(PS[:, 2 + m, q * SEQ:(q + 1) * SEQ], QKV[rows, 0, q * P:(q + 1) * P], QKV[rows, 1, 0:SEQ],
                                             start=True, stop=True)
                    last.then_inc(scores_done, 1)
                    pe.wait_ge(a_ready, h * 2 + 2)
                    pe.wait_ge(aT_ready, h)
                    pe.transpose(PS[:, 4, 0:P], A_[:, 0, 0:P], ident[:])
                    pe.transpose(PS[:, 4, P:SEQ], A_[:, 1, 0:P], ident[:])
                    pe.transpose(PS[:, 4, SEQ:SEQ + P], A_[:, 1, P:SEQ], ident[:]).then_inc(a_turned, 1)
                    pe.wait_ge(aT_ready, h + 1)
                    pe.wait_ge(kv_ready, h + 1)
                    pe.wait_ge(o_ready, h)
                    pe.matmul(PS[:, 5, 0:SEQ], KV[:, 1, 0, :], AT[:, 0:SEQ], start=True, stop=False)
                    pe.matmul(PS[:, 5, P:SEQ], KV[:, 1, 1, :], AT[:, SEQ:SEQ + P], start=False, stop=True).then_inc(o_done, 1)


def diff_sample(nc, G, Z, OD, v_new, bias_new, bias_own, row_weights):
    PS, ident, A = (G[k] for k in ("PS", "ident", "A"))
    ROWS = DIFF_HEADS * 2 * DEC_SEQ
    FT = DIFF_HEADS
    with ExitStack() as ctx:
        st = Stage(nc, ctx, "ds")
        pages = st.sb("pages", [1, DEC_BATCH * N_PAGES], I32)
        KP, VP = st.sb("k_pages", [P, 2, N_PAGES, FT * P]), st.sb("v_pages", [P, 2, N_PAGES, FT * P])
        KTT = st.sb("k_T", [P, 2, FT, PAST])
        QB = st.sb("q_blocks", [P, 2, FT * (ROWS + 8)])
        S, E, PN = (st.sb(w, [P, PAST + NEW]) for w in ("scores", "exps", "probs"))
        AT, ATN = st.sb("a_T", [P, 2, ROWS]), st.sb("a_T_new", [NEW, ROWS])
        mx, nmx, sums, rec, coef = (st.sb(w, [P, 1]) for w in ("max", "neg_max", "sums", "reciprocal", "coefficient"))
        (pages_loaded, zeroed, k_turned, kT_act, kT_dve, q_ready, scores_done, biased, soft, exps, probs, p_turned,
         aT_ready, o_done, o_ready) = st.sems(
            "pages_loaded", "zeroed", "k_turned", "kT_act", "kT_dve", "q_ready", "scores_done", "biased", "soft", "exps",
            "probs", "p_turned", "aT_ready", "o_done", "o_ready")
        kv_loaded = st.sems("kv_loaded0", "kv_loaded1")
        cache_k = A["cache_diff_k"][0].rearrange("n t m d -> n t (m d)")
        cache_v = A["cache_diff_v"][0].rearrange("n t m d -> n t (m d)")
        n_phys = cache_k.shape[0]
        q_blocks = QB[:].rearrange("p b (f c) -> p b f c", f=FT)

        def load(sp, i, s):
            for g in range(N_PAGES):
                page = sp.value_load(pages[0:1, ds(i * 4 + s * 2 + g, 1)], min_val=0, max_val=n_phys - 1)
                sp.dma_start(KP[:, s, g, :], cache_k[page]).then_inc(kv_loaded[s], 16)
                sp.dma_start(VP[:, s, g, :], cache_v[page]).then_inc(kv_loaded[s], 16)

        with nc.Block() as block:
            @block.sync
            def _(sp):
                sp.dma_start(pages[:], A["page_table"].rearrange("(o b) g -> o (b g)", o=1)).then_inc(pages_loaded, 16)
                sp.wait_ge(pages_loaded, 16)
                for s in range(2):
                    load(sp, 0, s)
                with sp.Fori(1, DEC_BATCH // 2) as i:
                    sp.wait_ge(o_done, i)
                    for s in range(2):
                        load(sp, i, s)

            @block.scalar
            def _(act):
                with act.Fori(0, DEC_BATCH // 2) as i:
                    for s in range(2):
                        act.wait_ge(scores_done, i * 2 + s)
                        for j in (0, 2):
                            act.wait_ge(k_turned, i * 8 + s * 4 + j + 1)
                            act.activation(KTT[:, s, 2 * j:2 * j + 2, :], PS[:, j, :].rearrange("p (f t) -> p f t", f=2), ACT.Copy).then_inc(kT_act, 1)
                    act.wait_ge(soft, i * 4 + 2)
                    act.wait_ge(probs, i)
                    act.activation(E[:], S[:], ACT.Exp, bias=nmx[:], accum_out=sums[:]).then_inc(exps, 1)
                    act.wait_ge(o_done, i + 1)
                    act.activation(OD[:, 0:FT, ds(i * 8 + SEQ, 8)].rearrange("p h (b s) -> p h b s", b=2),
                                   PS[:, 6, 0:ROWS].rearrange("p (b h s) -> p h b s", b=2, s=DEC_SEQ), ACT.Copy).then_inc(o_ready, 1)

            @block.vector
            def _(dve):
                dve.memset(QB[:], 0.0).then_inc(zeroed, 1)
                dve.wait_ge(zeroed, 1)
                with dve.Fori(0, DEC_BATCH // 2) as i:
                    for s in range(2):
                        dve.wait_ge(scores_done, i * 2 + s)
                        for m in range(2):
                            rows = slice(m * DIFF_HD, (m + 1) * DIFF_HD)
                            dve.tensor_scalar(q_blocks[rows, s, :, m * DEC_SEQ:(m + 1) * DEC_SEQ],
                                              Z[rows, DQ:DQ + FT, ds(i * 8 + SEQ + s * DEC_SEQ, DEC_SEQ)],
                                              DIFF_HD ** -0.5, None, ALU.mult).then_inc(q_ready, 1)
                        for j in (1, 3):
                            dve.wait_ge(k_turned, i * 8 + s * 4 + j + 1)
                            dve.tensor_copy(KTT[:, s, 2 * j:2 * j + 2, :], PS[:, j, :].rearrange("p (f t) -> p f t", f=2)).then_inc(kT_dve, 1)
                    dve.wait_ge(scores_done, i * 2 + 2)
                    dve.wait_ge(exps, i)
                    dve.tensor_tensor(S[:, 0:PAST], PS[:, 4, 0:PAST], bias_new[:], ALU.add).then_inc(biased, 1)
                    dve.tensor_tensor(S[:, PAST:PAST + NEW], PS[:, 4, PAST:PAST + NEW], bias_own[:, i, :], ALU.add).then_inc(biased, 1)
                    dve.wait_ge(biased, i * 2 + 2)
                    dve.tensor_reduce(mx[:], S[:], AX.X, ALU.max).then_inc(soft, 1)
                    dve.wait_ge(soft, i * 4 + 1)
                    dve.tensor_scalar(nmx[:], mx[:], -1.0, None, ALU.mult).then_inc(soft, 1)
                    dve.wait_ge(exps, i + 1)
                    dve.reciprocal(rec[:], sums[:]).then_inc(soft, 1)
                    dve.wait_ge(soft, i * 4 + 3)
                    dve.wait_ge(probs, i)
                    dve.tensor_tensor(coef[:], rec[:], row_weights[:], ALU.mult).then_inc(soft, 1)
                    dve.wait_ge(soft, i * 4 + 4)
                    dve.wait_ge(p_turned, i)
                    dve.tensor_scalar(PN[:], E[:], coef[:], None, ALU.mult).then_inc(probs, 1)
                    dve.wait_ge(p_turned, i + 1)
                    dve.wait_ge(o_done, i)
                    turned = PS[:, 5, 0:2 * P].rearrange("p (g x m s) -> p g x m s", g=2, m=2, s=DEC_SEQ)
                    at = AT[:].rearrange("p g (x s) -> p g x s", s=DEC_SEQ)
                    dve.tensor_copy(at, turned[:, :, :, 0, :]).then_inc(aT_ready, 1)
                    dve.wait_ge(aT_ready, i * 4 + 1)
                    dve.tensor_tensor(at, at, turned[:, :, :, 1, :], ALU.add).then_inc(aT_ready, 1)
                    turned = PS[0:NEW, 5, 2 * P:3 * P].rearrange("p (x m s) -> p x m s", m=2, s=DEC_SEQ)
                    at = ATN[:].rearrange("p (x s) -> p x s", s=DEC_SEQ)
                    dve.tensor_copy(at, turned[:, :, 0, :]).then_inc(aT_ready, 1)
                    dve.wait_ge(aT_ready, i * 4 + 3)
                    dve.tensor_tensor(at, at, turned[:, :, 1, :], ALU.add).then_inc(aT_ready, 1)

            @block.tensor
            def _(pe):
                with pe.Fori(0, DEC_BATCH // 2) as i:
                    for s in range(2):
                        pe.wait_ge(kv_loaded[s], i * 64 + 64)
                        for j in range(4):
                            if j % 2 == 0:
                                pe.wait_ge(kT_act, i * 4 + 2 * s + j // 2)
                            else:
                                pe.wait_ge(kT_dve, i * 4 + 2 * s + j // 2)
                            for f in range(2):
                                for g in range(N_PAGES):
                                    ft = 2 * j + f
                                    last = pe.transpose(PS[:, j, f * PAST + g * P:f * PAST + (g + 1) * P],
                                                        KP[:, s, g, ft * P:(ft + 1) * P], ident[:])
                            last.then_inc(k_turned, 1)
                        pe.wait_ge(q_ready, i * 4 + 2 * s + 2)
                        pe.wait_ge(kT_act, i * 4 + 2 * s + 2)
                        pe.wait_ge(kT_dve, i * 4 + 2 * s + 2)
                        pe.wait_ge(biased, i * 2)
                        rows = slice(s * ROWS, (s + 1) * ROWS)
                        for f in range(FT):
                            q = QB[:, s, f * ROWS:(f + 1) * ROWS]
                            pe.matmul(PS[rows, 4, 0:PAST], q, KTT[:, s, f, :], start=(f == 0), stop=(f == FT - 1), skip_group_check=True)
                            last = pe.matmul(PS[rows, 4, PAST:PAST + NEW], q, Z[:, DK + f, SEQ:T], start=False, stop=(f == FT - 1),
                                             skip_group_check=True)
                        last.then_inc(scores_done, 1)
                    pe.wait_ge(probs, i + 1)
                    pe.wait_ge(aT_ready, i * 4)
                    for g in range(2):
                        pe.transpose(PS[:, 5, g * P:(g + 1) * P], PN[:, g * P:(g + 1) * P], ident[:])
                    pe.transpose(PS[0:NEW, 5, 2 * P:3 * P], PN[:, PAST:PAST + NEW], ident[:]).then_inc(p_turned, 1)
                    pe.wait_ge(aT_ready, i * 4 + 4)
                    pe.wait_ge(o_ready, i)
                    for s in range(2):
                        for h in range(FT):
                            c = slice(s * ROWS // 2 + h * DEC_SEQ, s * ROWS // 2 + (h + 1) * DEC_SEQ)
                            out = PS[:, 6, c]
                            for g in range(N_PAGES):
                                pe.matmul(out, VP[:, s, g, h * P:(h + 1) * P], AT[:, g, c], start=(s == 0 and h == 0 and g == 0),
                                          stop=False, skip_group_check=True)
                            last = pe.matmul(out, v_new[:, h * P:(h + 1) * P], ATN[:, c], start=False, stop=True, skip_group_check=True)
                    last.then_inc(o_done, 1)


def mem_prompt(nc, G, Z, OM):
    PS, ident, O, S_ = (G[k] for k in ("PS", "ident", "O", "S"))
    SCALE = MEM_HD ** -0.5
    with ExitStack() as ctx:
        st = Stage(nc, ctx, "mp")
        Q, KVT = st.sb("q_T", [P, SEQ]), st.sb("kv_T", [P, 2, MEM_TOKENS])
        KV = st.sb("kv", [P, 2, 2, P])
        E, PN, PT = st.sb("exps", [P, 2, MEM_TOKENS]), st.sb("probs", [P, 2, MEM_TOKENS]), st.sb("probs_T", [P, 2, SEQ])
        mx, nmx, sums, rec = (st.sb(w, [P, 2]) for w in ("max", "neg_max", "sums", "reciprocals"))
        (loaded, staged, turned, kv_ready, scores_done, soft, exps, probs, p_turned, pT_ready, o_done, o_ready, kv_stored) = st.sems(
            "loaded", "staged", "turned", "kv_ready", "scores_done", "soft", "exps", "probs", "p_turned", "pT_ready", "o_done",
            "o_ready", "kv_stored")
        kv_dram = S_["mem_T"].rearrange("(c h) p t -> h p c t", c=2)
        outs = [O[n][0, 0].rearrange("(t p) h d -> h p t d", p=P) for n in ("mem_k_prompt", "mem_v_prompt")]
        with nc.Block() as block:
            @block.sync
            def _(sp):
                with sp.Fori(0, MEM_HEADS) as h:
                    sp.wait_ge(scores_done, h)
                    sp.dma_start(KVT[:], kv_dram[h]).then_inc(loaded, 16)
                    sp.wait_ge(kv_ready, h + 1)
                    for c in range(2):
                        sp.dma_start(outs[c][h], KV[:, c, :, :]).then_inc(kv_stored, 16)
                sp.wait_ge(kv_stored, 32 * MEM_HEADS)

            @block.scalar
            def _(act):
                with act.Fori(0, MEM_HEADS) as h:
                    act.wait_ge(scores_done, h)
                    act.activation(Q[:], Z[:, h + MQ, 0:SEQ], ACT.Copy).then_inc(staged, 1)
                    act.wait_ge(turned, h + 1)
                    act.wait_ge(kv_stored, h * 32)
                    act.wait_ge(o_done, h)
                    act.activation(KV[:], PS[:, 0, :].rearrange("p (c t d) -> p c t d", c=2, t=2), ACT.Copy).then_inc(kv_ready, 1)
                    act.wait_ge(soft, h * 3 + 2)
                    act.wait_ge(probs, h)
                    for q in range(2):
                        act.activation(E[:, q, :], PS[:, 1, q * MEM_TOKENS:(q + 1) * MEM_TOKENS], ACT.Exp, bias=nmx[:, q:q + 1],
                                       scale=SCALE, accum_out=sums[:, q:q + 1]).then_inc(exps, 1)
                    act.wait_ge(p_turned, h + 1)
                    act.activation(PT[:], PS[:, 2, :].rearrange("p (k q) -> p k q", k=2), ACT.Copy).then_inc(pT_ready, 1)
                    act.wait_ge(o_done, h + 1)
                    act.activation(OM[:, h, 0:SEQ], PS[:, 3, 0:SEQ], ACT.Copy).then_inc(o_ready, 1)

            @block.vector
            def _(dve):
                with dve.Fori(0, MEM_HEADS) as h:
                    dve.wait_ge(scores_done, h + 1)
                    dve.wait_ge(soft, h * 3)
                    dve.tensor_reduce(mx[:], PS[:, 1, :].rearrange("p (q k) -> p q k", q=2), AX.X, ALU.max).then_inc(soft, 1)
                    dve.wait_ge(soft, h * 3 + 1)
                    dve.wait_ge(exps, h * 2)
                    dve.tensor_scalar(nmx[:], mx[:], -SCALE, None, ALU.mult).then_inc(soft, 1)
                    dve.wait_ge(exps, h * 2 + 2)
                    dve.wait_ge(probs, h)
                    dve.reciprocal(rec[:], sums[:]).then_inc(soft, 1)
                    dve.wait_ge(soft, h * 3 + 3)
                    dve.wait_ge(p_turned, h)
                    dve.tensor_tensor(PN[:], E[:], rec[:].unsqueeze(2).to_broadcast([P, 2, MEM_TOKENS]), ALU.mult).then_inc(probs, 1)

            @block.tensor
            def _(pe):
                with pe.Fori(0, MEM_HEADS) as h:
                    pe.wait_ge(loaded, h * 16 + 16)
                    pe.wait_ge(kv_ready, h)
                    for c in range(2):
                        for t in range(2):
                            last = pe.transpose(PS[:, 0, (2 * c + t) * P:(2 * c + t + 1) * P], KVT[:, c, t * P:(t + 1) * P], ident[:])
                    last.then_inc(turned, 1)
                    pe.wait_ge(staged, h + 1)
                    pe.wait_ge(exps, h * 2)
                    for q in range(2):
                        last = pe.matmul(PS[:, 1, q * MEM_TOKENS:(q + 1) * MEM_TOKENS], Q[:, q * P:(q + 1) * P], KVT[:, 0, :], start=True, stop=True)
                    last.then_inc(scores_done, 1)
                    pe.wait_ge(probs, h + 1)
                    pe.wait_ge(pT_ready, h)
                    for k in range(2):
                        for q in range(2):
                            last = pe.transpose(PS[:, 2, k * SEQ + q * P:k * SEQ + (q + 1) * P], PN[:, q, k * P:(k + 1) * P], ident[:])
                    last.then_inc(p_turned, 1)
                    pe.wait_ge(pT_ready, h + 1)
                    pe.wait_ge(kv_ready, h + 1)
                    pe.wait_ge(o_ready, h)
                    for k in range(2):
                        last = pe.matmul(PS[:, 3, 0:SEQ], KV[:, 1, k, :], PT[:, k, :], start=(k == 0), stop=(k == 1))
                    last.then_inc(o_done, 1)


def mem_sample(nc, G, Z, OM):
    PS, ident, A = (G[k] for k in ("PS", "ident", "A"))
    SCALE = MEM_HD ** -0.5
    ROWS, GROUP, FT = 32, 4, MEM_HEADS
    with ExitStack() as ctx:
        st = Stage(nc, ctx, "msm")
        K, V = (st.sb(w, [P, GROUP, 2, FT * P]) for w in ("k", "v"))
        KTT = st.sb("k_T", [P, 2, FT, MEM_TOKENS])
        QB = st.sb("q_blocks", [P, 2, FT * (ROWS + DEC_SEQ)])
        E, PN, PT = st.sb("exps", [P, MEM_TOKENS]), st.sb("probs", [P, MEM_TOKENS]), st.sb("probs_T", [P, 2, P])
        mx, nmx, sums, rec = (st.sb(w, [P, 1]) for w in ("max", "neg_max", "sums", "reciprocal"))
        (loaded, zeroed, k_turned, kT_ready, q_ready, scores_done, soft, exps, probs, p_turned, pT_ready, o_done, o_ready) = st.sems(
            "loaded", "zeroed", "k_turned", "kT_ready", "q_ready", "scores_done", "soft", "exps", "probs", "p_turned", "pT_ready",
            "o_done", "o_ready")
        k_in, v_in = (A[n][0].rearrange("(i b) (t p) h d -> i b p t (h d)", b=GROUP, p=P) for n in ("cache_mem_k", "cache_mem_v"))
        q_blocks = QB[:].rearrange("p b (f c) -> p b f c", f=FT)
        with nc.Block() as block:
            @block.sync
            def _(sp):
                with sp.Fori(0, DEC_BATCH // GROUP) as i:
                    sp.wait_ge(o_done, i)
                    for b in range(GROUP):
                        sp.dma_start(K[:, b, :, :], k_in[i, b]).then_inc(loaded, 16)
                    for b in range(GROUP):
                        sp.dma_start(V[:, b, :, :], v_in[i, b]).then_inc(loaded, 16)

            @block.scalar
            def _(act):
                with act.Fori(0, DEC_BATCH // GROUP) as i:
                    for b in range(GROUP):
                        act.wait_ge(k_turned, i * 4 + b + 1)
                        act.activation(KTT[:, b % 2, :, :].rearrange("p (j f) t -> p j f t", j=2),
                                       PS[:, 2 * (b % 2):2 * (b % 2) + 2, :].rearrange("p j (f t) -> p j f t", f=2), ACT.Copy).then_inc(kT_ready, 1)
                    act.wait_ge(soft, i * 3 + 2)
                    act.wait_ge(probs, i)
                    act.activation(E[:], PS[:, 4, 0:MEM_TOKENS], ACT.Exp, bias=nmx[:], scale=SCALE, accum_out=sums[:]).then_inc(exps, 1)
                    act.wait_ge(p_turned, i + 1)
                    act.activation(PT[:], PS[:, 5, 0:2 * P].rearrange("p (k r) -> p k r", k=2), ACT.Copy).then_inc(pT_ready, 1)
                    act.wait_ge(o_done, i + 1)
                    act.activation(OM[:, 0:FT, ds(i * 16 + SEQ, 16)].rearrange("p h (b s) -> p h b s", b=GROUP),
                                   PS[:, 6, 0:64].rearrange("p (b h s) -> p h b s", b=GROUP, s=DEC_SEQ), ACT.Copy).then_inc(o_ready, 1)

            @block.vector
            def _(dve):
                dve.memset(QB[:], 0.0).then_inc(zeroed, 1)
                dve.wait_ge(zeroed, 1)
                with dve.Fori(0, DEC_BATCH // GROUP) as i:
                    for b in range(GROUP):
                        n = i * 4 + b
                        if b >= 2:
                            dve.wait_ge(scores_done, n - 1)
                        else:
                            dve.wait_ge(scores_done, i * 4)
                        dve.tensor_copy(q_blocks[:, b % 2, :, 0:DEC_SEQ],
                                        Z[:, MQ:MQ + FT, ds(i * 16 + SEQ + b * DEC_SEQ, DEC_SEQ)]).then_inc(q_ready, 1)
                    dve.wait_ge(scores_done, i * 4 + 4)
                    dve.wait_ge(soft, i * 3)
                    dve.tensor_reduce(mx[:], PS[:, 4, 0:MEM_TOKENS], AX.X, ALU.max).then_inc(soft, 1)
                    dve.wait_ge(soft, i * 3 + 1)
                    dve.wait_ge(exps, i)
                    dve.tensor_scalar(nmx[:], mx[:], -SCALE, None, ALU.mult).then_inc(soft, 1)
                    dve.wait_ge(exps, i + 1)
                    dve.wait_ge(probs, i)
                    dve.reciprocal(rec[:], sums[:]).then_inc(soft, 1)
                    dve.wait_ge(soft, i * 3 + 3)
                    dve.wait_ge(p_turned, i)
                    dve.tensor_scalar(PN[:], E[:], rec[:], None, ALU.mult).then_inc(probs, 1)

            @block.tensor
            def _(pe):
                with pe.Fori(0, DEC_BATCH // GROUP) as i:
                    pe.wait_ge(loaded, i * 128 + 128)
                    for b in range(GROUP):
                        if b >= 2:
                            pe.wait_ge(kT_ready, i * 4 + b - 1)
                        for f in range(FT):
                            for k in range(2):
                                last = pe.transpose(PS[:, 2 * (b % 2) + f // 2, (f % 2) * MEM_TOKENS + k * P:(f % 2) * MEM_TOKENS + (k + 1) * P],
                                                    K[:, b, k, f * P:(f + 1) * P], ident[:])
                        last.then_inc(k_turned, 1)
                        pe.wait_ge(kT_ready, i * 4 + b + 1)
                        pe.wait_ge(q_ready, i * 4 + b + 1)
                        if b == 0:
                            pe.wait_ge(exps, i)
                        for f in range(FT):
                            last = pe.matmul(PS[b * ROWS:(b + 1) * ROWS, 4, 0:MEM_TOKENS], QB[:, b % 2, f * ROWS:(f + 1) * ROWS],
                                             KTT[:, b % 2, f, :], start=(f == 0), stop=(f == FT - 1))
                        last.then_inc(scores_done, 1)
                    pe.wait_ge(probs, i + 1)
                    pe.wait_ge(pT_ready, i)
                    for k in range(2):
                        last = pe.transpose(PS[:, 5, k * P:(k + 1) * P], PN[:, k * P:(k + 1) * P], ident[:])
                    last.then_inc(p_turned, 1)
                    pe.wait_ge(pT_ready, i + 1)
                    pe.wait_ge(o_ready, i)
                    for b in range(GROUP):
                        for h in range(FT):
                            for k in range(2):
                                last = pe.matmul(PS[:, 6, (b * FT + h) * DEC_SEQ:(b * FT + h + 1) * DEC_SEQ], V[:, b, k, h * P:(h + 1) * P],
                                                 PT[:, k, b * ROWS + h * DEC_SEQ:b * ROWS + (h + 1) * DEC_SEQ],
                                                 start=(b == 0 and h == 0 and k == 0), stop=True, skip_group_check=True)
                    last.then_inc(o_done, 1)


def diff_norm(nc, G, OD):
    PS, ones, A = (G[k] for k in ("PS", "ones", "A"))
    with ExitStack() as ctx:
        st = Stage(nc, ctx, "dn")
        w, ws = st.sb("subln", [P, 1]), st.sb("subln_scaled", [P, 1])
        sq = st.sb("squares", [P, 4, T])
        ms, root, rstd, t1, t2, rstd2 = (st.sb(x, [P, 4, T]) for x in ("ms", "root", "rstd", "t1", "t2", "rstd2"))
        loaded, scaled, squared, summed, steps = st.sems("loaded", "scaled", "squared", "summed", "rstd_steps")
        with nc.Block() as block:
            @block.sync
            def _(sp):
                with nc.allow_non_contiguous_dma(reason="one weight per partition"):
                    sp.dma_start(w[:], A["diff_subln_w"][0].rearrange("(p o) -> p o", o=1)).then_inc(loaded, 16)

            @block.scalar
            def _(act):
                for g in range(2):
                    if g:
                        act.wait_ge(summed, g)
                    act.activation(sq[:], OD[:, 4 * g:4 * g + 4, :], ACT.Square).then_inc(squared, 1)
                    act.wait_ge(steps, 7 * g + 1)
                    act.activation(root[:], ms[:], ACT.Sqrt).then_inc(steps, 1)

            @block.tensor
            def _(pe):
                for g in range(2):
                    pe.wait_ge(squared, g + 1)
                    if g:
                        pe.wait_ge(steps, 7 * g)
                    for j in range(4):
                        last = pe.matmul(PS[:, j, 0:T], ones[:], sq[:, j, :], start=True, stop=True)
                    last.then_inc(summed, 1)

            @block.vector
            def _(dve):
                dve.wait_ge(loaded, 16)
                dve.tensor_scalar(ws[:], w[:], 1.0 - LAMBDA_INIT, None, ALU.mult).then_inc(scaled, 1)
                dve.wait_ge(scaled, 1)
                for g in range(2):
                    dve.wait_ge(summed, g + 1)
                    dve.tensor_scalar(ms[:], PS[:, 0:4, 0:T], EPS, None, ALU.add).then_inc(steps, 1)
                    dve.wait_ge(steps, 7 * g + 2)
                    dve.reciprocal(rstd[:], root[:]).then_inc(steps, 1)
                    refine_rstd(dve, ms, rstd, t1, t2, rstd2, steps, 7 * g + 3)
                    dve.wait_ge(steps, 7 * g + 6)
                    dve.scalar_tensor_tensor(out=OD[:, 4 * g:4 * g + 4, :], in0=OD[:, 4 * g:4 * g + 4, :], scalar=ws[:],
                                             in1=rstd2[:], op0=ALU.mult, op1=ALU.mult).then_inc(steps, 1)
                    dve.wait_ge(steps, 7 * g + 7)


def attention(nc, G, Z, ODM):
    OD, OM = ODM[:, 0:DIFF_HEADS, :], ODM[:, DIFF_HEADS:, :]
    retention(nc, G, Z)
    with ExitStack() as ctx:
        st = Stage(nc, ctx, "diff")
        v_new = st.sb("v_new", [NEW, DIFF_HEADS * P])
        bias, bias_new, bias_own, map_weights, row_weights = diff_tables(nc, G, st)
        diff_prompt(nc, G, Z, OD, v_new, bias, map_weights)
        diff_sample(nc, G, Z, OD, v_new, bias_new, bias_own, row_weights)
    mem_prompt(nc, G, Z, OM)
    mem_sample(nc, G, Z, OM)
    diff_norm(nc, G, OD)


def split_branch_outputs(nc, G, Z, ODM, OTH, OTL):
    with ExitStack() as ctx:
        (high,) = Stage(nc, ctx, "so").sems("high")
        parts = [(4 * q, Z[:, RG + 4 * q:RG + 4 * q + 4, :]) for q in range(4)] + [
            (O_DIFF + 4 * q, ODM[:, 4 * q:4 * q + 4, :]) for q in range(3)]
        with nc.Block() as block:
            @block.scalar
            def _(act):
                for o, src in parts:
                    act.activation(OTH[:, o:o + 4, :], src, ACT.Copy).then_inc(high, 1)

            @block.vector
            def _(dve):
                for n, (o, src) in enumerate(parts):
                    dve.wait_ge(high, n + 1)
                    dve.tensor_tensor(OTL[:, o:o + 4, :], src, OTH[:, o:o + 4, :], ALU.subtract)


def up_projections(nc, G, OTH, OTL, MH, ML):
    A, S, PS = G["A"], G["S"], G["PS"]
    with ExitStack() as ctx:
        w = WeightStream(nc, ctx, PS, "wup", loads=(1, 2))
        st = Stage(nc, ctx, "up")
        gates = st.sb("gates", [P, 3, 2, T])
        mix = st.sb("mix", [P, 2, T])
        t1, t2, t3, t4 = (st.sb(x, [P, T]) for x in ("diff_part", "mem_part", "sum", "total"))
        gates_loaded, sigmoids, mixed = st.sems("gates_loaded", "sigmoids", "mixed")
        ret, diff, mem = (A[n][0].rearrange("(k p) n -> p k n", p=P) for n in ("w_up_ret", "w_up_diff", "w_up_mem"))
        gates_dram = S["gates_T"].rearrange("(g i f) p t -> g i p f t", g=3, f=2)
        STEPS = KT // 2
        o = (OTH, OTL)

        def branch(a, n):
            return tuple(x[:, a:a + n, :] for x in o)

        with nc.Block() as block:
            @block.sync
            def _(sp):
                def step(i, first):
                    cols = ds(i * 2 * P, 2 * P)
                    w.load(sp, i, 0, [ret[:, :, cols]], first)
                    w.load(sp, i, 1, [diff[:, :, cols], mem[:, :, cols]], first)
                    sp.wait_ge(mixed, i * 14)
                    for g in range(3):
                        sp.dma_start(gates[:, g, :, :], gates_dram[g, i]).then_inc(gates_loaded, 16)
                step(0, True)
                with sp.Fori(1, STEPS) as i:
                    step(i, False)

            @block.scalar
            def _(act):
                with act.Fori(0, STEPS) as i:
                    for u in range(4):
                        w.split_high(act, i, u, KT if u < 2 else 12)
                        if u == 0:
                            act.wait_ge(gates_loaded, i * 48 + 48)
                            act.activation(gates[:], gates[:], ACT.Sigmoid).then_inc(sigmoids, 1)

            @block.vector
            def _(dve):
                with dve.Fori(0, STEPS) as i:
                    for u in range(4):
                        w.split_low(dve, i, u, KT if u < 2 else 12)
                        w.wait_product(dve, i, u)
                        f = u % 2
                        n = i * 14 + (u if u < 2 else 2 + 6 * (u - 2))
                        if u < 2:
                            if u == 0:
                                dve.wait_ge(sigmoids, i + 1)
                            dve.wait_ge(mixed, n)
                            dve.tensor_tensor(mix[:, f, :], PS[:, f, 0:T], gates[:, 0, f, :], ALU.mult).then_inc(mixed, 1)
                            dve.wait_ge(mixed, n + 1)
                            dve.sem_inc(w.bank_free, 1)
                        else:
                            dve.wait_ge(mixed, n)
                            dve.tensor_tensor(t1[:], PS[:, 2 + f, 0:T], gates[:, 1, f, :], ALU.mult).then_inc(mixed, 1)
                            dve.tensor_tensor(t2[:], PS[:, 4 + f, 0:T], gates[:, 2, f, :], ALU.mult).then_inc(mixed, 1)
                            dve.wait_ge(mixed, n + 2)
                            dve.sem_inc(w.bank_free, 1)
                            dve.tensor_tensor(t3[:], mix[:, f, :], t1[:], ALU.add).then_inc(mixed, 1)
                            dve.wait_ge(mixed, n + 3)
                            dve.tensor_tensor(t4[:], t3[:], t2[:], ALU.add).then_inc(mixed, 1)
                            dve.wait_ge(mixed, n + 4)
                            dve.tensor_copy(MH[:, i * 2 + f, :], t4[:]).then_inc(mixed, 1)
                            dve.wait_ge(mixed, n + 5)
                            dve.tensor_tensor(ML[:, i * 2 + f, :], t4[:], MH[:, i * 2 + f, :], ALU.subtract).then_inc(mixed, 1)

            @block.tensor
            def _(pe):
                w.open(pe)
                with pe.Fori(0, STEPS) as i:
                    for u in range(2):
                        w.product(pe, i, u, [(PS[:, u, 0:T], 0, branch(O_RET, KT))])
                    for u in (2, 3):
                        w.product(pe, i, u, [(PS[:, u, 0:T], 0, branch(O_DIFF, DIFF_HEADS)),
                                             (PS[:, 2 + u, 0:T], DIFF_HEADS, branch(O_MEM, MEM_HEADS))])


def output_projection(nc, G, MH, ML, hT):
    A, S, PS = G["A"], G["S"], G["PS"]
    with ExitStack() as ctx:
        w = WeightStream(nc, ctx, PS, "wout")
        (x_loaded,) = Stage(nc, ctx, "out").sems("x_loaded")
        wout = A["w_out"][0].rearrange("(k p) n -> p k n", p=P)
        with nc.Block() as block:
            @block.sync
            def _(sp):
                for b in range(2):
                    w.load(sp, 0, b, [wout[:, :, b * 2 * P:(b + 1) * 2 * P]], True)
                sp.dma_start(hT[:], S["x_T"].rearrange("k p t -> p k t")).then_inc(x_loaded, 16)
                with sp.Fori(1, KT // 4) as i:
                    for b in range(2):
                        w.load(sp, i, b, [wout[:, :, ds(i * 512 + b * 2 * P, 2 * P)]])

            @block.scalar
            def _(act):
                with act.Fori(0, KT // 4) as i:
                    for u in range(4):
                        w.split_high(act, i, u)

            @block.vector
            def _(dve):
                dve.wait_ge(x_loaded, 16)
                with dve.Fori(0, KT // 4) as i:
                    for u in range(4):
                        w.split_low(dve, i, u)
                        w.wait_product(dve, i, u)
                        dve.tensor_tensor(hT[:, i * 4 + u, :], PS[:, u % 2, 0:T], hT[:, i * 4 + u, :], ALU.add).then_inc(w.bank_free, 1)

            @block.tensor
            def _(pe):
                w.open(pe)
                with pe.Fori(0, KT // 4) as i:
                    for u in range(4):
                        w.product(pe, i, u, [(PS[:, u % 2, 0:T], 0, (MH, ML))])


TPAD = 3 * P


def peer_queries(nc, G, XH, XL, QT):
    A, PS = G["A"], G["PS"]
    with ExitStack() as ctx:
        w = WeightStream(nc, ctx, PS, "wq")
        wq = A["peer_w_q"][0].rearrange("(k p) n -> p k n", p=P)
        with nc.Block() as block:
            @block.sync
            def _(sp):
                for b in range(2):
                    w.load(sp, 0, b, [wq[:, :, b * 2 * P:(b + 1) * 2 * P]], True)
                with sp.Fori(1, KT // 4) as i:
                    for b in range(2):
                        w.load(sp, i, b, [wq[:, :, ds(i * 512 + b * 2 * P, 2 * P)]])

            @block.gpsimd
            def _(pool):
                pool.memset(QT[:, :, T:TPAD], 0.0)

            @block.scalar
            def _(act):
                with act.Fori(0, KT // 4) as i:
                    for u in range(4):
                        w.split_high(act, i, u)

            @block.vector
            def _(dve):
                with dve.Fori(0, KT // 4) as i:
                    for u in range(4):
                        w.split_low(dve, i, u)
                        w.wait_product(dve, i, u)
                        dve.tensor_copy(QT[:, i * 4 + u, 0:T], PS[:, u % 2, 0:T]).then_inc(w.bank_free, 1)

            @block.tensor
            def _(pe):
                w.open(pe)
                with pe.Fori(0, KT // 4) as i:
                    for u in range(4):
                        w.product(pe, i, u, [(PS[:, u % 2, 0:T], 0, (XH, XL))])


LOWEST = -3.0e38


def top16(dve, values, rest, best, index, found, n, base):
    for g in range(n):
        dve.max(best[:, g, 0:8], values[:, g, :]).then_inc(found, 1)
    for g in range(n):
        dve.wait_ge(found, base + g + 1)
        dve.max_index(index[:, g, 0:8], best[:, g, 0:8], values[:, g, :])
        dve.match_replace(rest[:, g, :], best[:, g, 0:8], values[:, g, :], LOWEST).then_inc(found, 1)
    for g in range(n):
        dve.wait_ge(found, base + n + g + 1)
        dve.max(best[:, g, 8:16], rest[:, g, :]).then_inc(found, 1)
    for g in range(n):
        dve.wait_ge(found, base + 2 * n + g + 1)
        dve.max_index(index[:, g, 8:16], best[:, g, 8:16], rest[:, g, :]).then_inc(found, 1)


def peer_selection(nc, G, QT, SEL):
    A, PS, ident, C = (G[k] for k in ("A", "PS", "ident", "C"))
    GR = 2 * PEER_HEADS
    PICKS = PEER_HEADS * TOPK
    with ExitStack() as ctx:
        st = Stage(nc, ctx, "sel")
        keys, KYT = st.sb("keys", [P, GR, P]), st.sb("keys_T", [P, GR, P])
        iota = st.sb("iota", [P, TOPK])
        Q = st.sb("q_tile", [P, GR, P])
        SC, SC2 = st.sb("scores", [P, GR, NKEYS]), st.sb("scores_rest", [P, GR, NKEYS])
        V, IX, IXF = st.sb("best", [P, GR, TOPK]), st.sb("best_index", [P, GR, TOPK], U32), st.sb("best_index_f", [P, GR, TOPK])
        CA, CA2 = st.sb("pairs", [P, PEER_HEADS, TOPK * TOPK]), st.sb("pairs_rest", [P, PEER_HEADS, TOPK * TOPK])
        TS, J = st.sb("top", [P, PEER_HEADS, TOPK]), st.sb("top_index", [P, PEER_HEADS, TOPK], U32)
        JJ = st.sb("top_parts", [P, 2, PICKS], U32)
        JF = st.sb("top_parts_f", [P, 2, PICKS])
        EQ, MU = st.sb("hits", [P, PICKS, TOPK]), st.sb("hit_index", [P, PICKS, TOPK])
        D, E = st.sb("below_top", [P, PEER_HEADS, TOPK]), st.sb("exps", [P, PEER_HEADS, TOPK])
        sums, rec = st.sb("sums", [P, PEER_HEADS]), st.sb("reciprocals", [P, PEER_HEADS])
        PK = st.sb("picks", [P, 3, PICKS])
        (loaded, key_turned, keys_ready, staged, scored, scores_ready, found1, paired, found2, steps, exped, picks_ready,
         picks_turned, sel_ready) = st.sems("loaded", "key_turned", "keys_ready", "staged", "scored", "scores_ready", "found1",
                                            "paired", "found2", "steps", "exped", "picks_ready", "picks_turned", "sel_ready")
        N1, N2, NS_ = 4 * GR, 4 * PEER_HEADS, 14
        with nc.Block() as block:
            @block.sync
            def _(sp):
                sp.dma_start(keys[:], A["peer_keys"][0].rearrange("h c n d -> n (h c) d")).then_inc(loaded, 16)
                sp.dma_start(iota[:], C["iota"][:, 0:TOPK]).then_inc(loaded, 16)

            @block.tensor
            def _(pe):
                pe.wait_ge(loaded, 32)
                for b in range(4):
                    for j in range(4):
                        last = pe.transpose(PS[:, b, j * P:(j + 1) * P], keys[:, 4 * b + j, :], ident[:])
                    last.then_inc(key_turned, 1)
                pe.wait_ge(keys_ready, 4)
                with pe.Fori(0, 3) as t:
                    pe.wait_ge(staged, t + 1)
                    pe.wait_ge(scores_ready, t)
                    for g in range(GR):
                        last = pe.matmul(PS[:, g // 4, (g % 4) * P:(g % 4 + 1) * P], Q[:, g, :], KYT[:, g, :], start=True, stop=True)
                    last.then_inc(scored, 1)
                    pe.wait_ge(picks_ready, t * 3 + 3)
                    pe.wait_ge(sel_ready, t)
                    for j in range(3):
                        last = pe.transpose(PS[:, 4, j * P:(j + 1) * P], PK[:, j, :], ident[:])
                    last.then_inc(picks_turned, 1)

            @block.scalar
            def _(act):
                for b in range(4):
                    act.wait_ge(key_turned, b + 1)
                    act.activation(KYT[:, 4 * b:4 * b + 4, :], PS[:, b, :].rearrange("p (j n) -> p j n", j=4), ACT.Copy).then_inc(keys_ready, 1)
                with act.Fori(0, 3) as t:
                    act.wait_ge(scored, t)
                    act.activation(Q[:], QT[:, :, ds(t * P, P)], ACT.Copy).then_inc(staged, 1)
                    act.wait_ge(scored, t + 1)
                    act.wait_ge(found1, t * N1)
                    act.activation(SC[:].rearrange("p (b j) n -> p b (j n)", b=4), PS[:, 0:4, :], ACT.Copy).then_inc(scores_ready, 1)
                    act.wait_ge(steps, t * NS_ + 1)
                    act.activation(E[:], D[:], ACT.Exp).then_inc(exped, 1)
                    act.wait_ge(picks_turned, t + 1)
                    act.activation(SEL[:, :, ds(t * P, P)], PS[:, 4, 0:3 * P].rearrange("p (j t) -> p j t", j=3), ACT.Copy).then_inc(sel_ready, 1)

            @block.vector
            def _(dve):
                for t in range(3):
                    dve.wait_ge(scores_ready, t + 1)
                    dve.wait_ge(steps, t * NS_)
                    top16(dve, SC, SC2, V, IX, found1, GR, t * N1)
                    dve.wait_ge(found1, t * N1 + N1)
                    best = V[:].rearrange("p (h c) k -> p c h k", c=2)
                    dve.tensor_tensor(CA[:].rearrange("p h (a b) -> p h a b", a=TOPK),
                                      best[:, 0].unsqueeze(3).to_broadcast([P, PEER_HEADS, TOPK, TOPK]),
                                      best[:, 1].unsqueeze(2).to_broadcast([P, PEER_HEADS, TOPK, TOPK]), ALU.add).then_inc(paired, 1)
                    dve.wait_ge(paired, t + 1)
                    top16(dve, CA, CA2, TS, J, found2, PEER_HEADS, t * N2)
                    dve.wait_ge(found2, t * N2 + N2)
                    dve.wait_ge(picks_turned, t)
                    n = t * NS_
                    dve.tensor_tensor(D[:], TS[:], TS[:, :, 0:1].to_broadcast([P, PEER_HEADS, TOPK]), ALU.subtract).then_inc(steps, 1)
                    j = J[:].rearrange("p h k -> p (h k)")
                    dve.tensor_scalar(JJ[:, 0, :], j, 4, None, ALU.logical_shift_right).then_inc(steps, 1)
                    dve.tensor_scalar(JJ[:, 1, :], j, 15, None, ALU.bitwise_and).then_inc(steps, 1)
                    dve.tensor_copy(IXF[:], IX[:]).then_inc(steps, 1)
                    dve.wait_ge(steps, n + 4)
                    dve.tensor_copy(JF[:], JJ[:]).then_inc(steps, 1)
                    dve.wait_ge(steps, n + 5)
                    index = IXF[:].rearrange("p (h c) k -> p c h k", c=2)
                    for c in range(2):
                        dve.tensor_tensor(EQ[:], JF[:, c, :].unsqueeze(2).to_broadcast([P, PICKS, TOPK]),
                                          iota[:].unsqueeze(1).to_broadcast([P, PICKS, TOPK]), ALU.is_equal).then_inc(steps, 1)
                        dve.wait_ge(steps, n + 6 + 3 * c)
                        dve.tensor_tensor(MU[:].rearrange("p (h k) a -> p h k a", h=PEER_HEADS),
                                          EQ[:].rearrange("p (h k) a -> p h k a", h=PEER_HEADS),
                                          index[:, c].unsqueeze(2).to_broadcast([P, PEER_HEADS, TOPK, TOPK]), ALU.mult).then_inc(steps, 1)
                        dve.wait_ge(steps, n + 7 + 3 * c)
                        dve.tensor_reduce(PK[:, c, :], MU[:], AX.X, ALU.add).then_inc(steps, 1)
                        dve.wait_ge(steps, n + 8 + 3 * c)
                    dve.wait_ge(exped, t + 1)
                    dve.tensor_reduce(sums[:], E[:], AX.X, ALU.add).then_inc(steps, 1)
                    dve.wait_ge(steps, n + 12)
                    dve.reciprocal(rec[:], sums[:]).then_inc(steps, 1)
                    dve.wait_ge(steps, n + 13)
                    dve.tensor_tensor(PK[:, 2, :].rearrange("p (h k) -> p h k", h=PEER_HEADS), E[:],
                                      rec[:].unsqueeze(2).to_broadcast([P, PEER_HEADS, TOPK]), ALU.mult).then_inc(steps, 1)
                    dve.wait_ge(steps, n + 14)
                    dve.sem_inc(picks_ready, 3)


TOKEN_BLOCKS = 3
TB = T // TOKEN_BLOCKS


def peer_weights(nc, G, SEL):
    PS, C, S = G["PS"], G["C"], G["S"]
    with ExitStack() as ctx:
        st = Stage(nc, ctx, "pw")
        iota = st.sb("iota", [P, P])
        B_, A_ = st.sb("second_hot", [P, 2, 4, P]), st.sb("first_hot", [P, 2, 4, P])
        W = st.sb("weights", [P, 2, NKEYS, TB])
        loaded, b_ready, a_ready, placed, w_ready = st.sems("loaded", "second_ready", "first_ready", "placed", "weights_ready")
        stored = st.sems("stored0", "stored1")
        HALF = TB // 8
        with nc.Block() as block:
            @block.sync
            def _(sp):
                sp.dma_start(iota[:], C["iota"]).then_inc(loaded, 16)
                for k in range(TOKEN_BLOCKS):
                    sp.wait_ge(w_ready, 2 * HALF * (k + 1))
                    sp.dma_start(S["peer_weights"][k], W[:, k % 2, :, :]).then_inc(stored[k % 2], 16)
                sp.wait_ge(stored[0], 32)
                sp.wait_ge(stored[1], 16)

            @block.vector
            def _(dve):
                dve.wait_ge(loaded, 16)
                with dve.Fori(0, T // 8) as i:
                    for s in range(2):
                        dve.wait_ge(placed, i * 2)
                        dve.tensor_tensor(B_[:, s, :, :], iota[:].unsqueeze(1).to_broadcast([P, 4, P]),
                                          SEL[:, 1, ds(i * 8 + s * 4, 4)].unsqueeze(2).to_broadcast([P, 4, P]),
                                          ALU.is_equal).then_inc(b_ready, 1)
                        for j in range(4):
                            t = i * 8 + s * 4 + j
                            ins = dve.tensor_scalar(A_[:, s, j, :], iota[:], SEL[:, 0, ds(t, 1)], SEL[:, 2, ds(t, 1)],
                                                    ALU.is_equal, ALU.mult)
                        ins.then_inc(a_ready, 1)

            @block.tensor
            def _(pe):
                with pe.Fori(0, T // 8) as i:
                    for s in range(2):
                        n = i * 2 + s
                        pe.wait_ge(a_ready, n + 1)
                        pe.wait_ge(b_ready, n + 1)
                        pe.wait_ge(w_ready, i * 2)
                        for j in range(4):
                            last = pe.matmul(PS[:, s, j * P:(j + 1) * P], B_[:, s, j, :], A_[:, s, j, :], start=True, stop=True)
                        last.then_inc(placed, 1)

            @block.scalar
            def _(act):
                for k in range(TOKEN_BLOCKS):
                    if k >= 2:
                        act.wait_ge(stored[k % 2], 16)
                    with act.Fori(0, HALF) as i:
                        for s in range(2):
                            act.wait_ge(placed, i * 2 + 2 * HALF * k + s + 1)
                            act.activation(W[:, k % 2, :, ds(i * 8 + s * 4, 4)].rearrange("p i t -> p t i"),
                                           PS[:, s, :].rearrange("p (t i) -> p t i", t=4), ACT.Copy).then_inc(w_ready, 1)


def peer_experts(nc, G, XH, XL, hT):
    A, PS, ident, S = (G[k] for k in ("A", "PS", "ident", "S"))
    STEPS = EXPERTS // (2 * P)
    with ExitStack() as ctx:
        st = Stage(nc, ctx, "ex")
        U, V = st.sb("u", [P, 2, D_MODEL]), st.sb("v", [P, 2, D_MODEL])
        UH, UL = st.sb("uT_high", [P, 2, KT, P], F32R), st.sb("uT_low", [P, 2, KT, P], F32R)
        VH, VL = st.sb("v_high", [P, 2, D_MODEL], F32R), st.sb("v_low", [P, 2, D_MODEL], F32R)
        W = st.sb("weights", [P, TOKEN_BLOCKS, 2, TB])
        GE, GA = st.sb("gelu", [P, 2, T]), st.sb("act", [P, 2, T])
        GH, GL = st.sb("act_high", [P, 2, T], F32R), st.sb("act_low", [P, 2, T], F32R)
        u_loaded, v_loaded = st.sems("u_loaded0", "u_loaded1"), st.sems("v_loaded0", "v_loaded1")
        (w_loaded, turned, uT_high, uT_low, hidden_done, gelu_ready, weighted, act_high, act_ready, v_high, v_low, out_done,
         added) = st.sems(
            "weights_loaded", "turned", "uT_high", "uT_low", "hidden_done", "gelu_ready", "weighted", "act_high", "act_ready",
            "v_high", "v_low", "out_done", "added")
        u_in, v_in = (A[n][0].rearrange("(s c p) d -> s c p d", c=2, p=P) for n in ("peer_u", "peer_v"))
        w_in = S["peer_weights"].rearrange("k p (s c) t -> s p k c t", c=2)
        with nc.Block() as block:
            @block.sync
            def _(sp):
                for c in range(2):
                    sp.dma_start(U[:, c, :], u_in[0, c]).then_inc(u_loaded[c], 16)
                sp.dma_start(W[:], w_in[0]).then_inc(w_loaded, 16)
                for c in range(2):
                    sp.dma_start(V[:, c, :], v_in[0, c]).then_inc(v_loaded[c], 16)
                sp.wait_ge(turned, 4)
                sp.dma_start(U[:, 0, :], u_in[1, 0]).then_inc(u_loaded[0], 16)
                sp.wait_ge(turned, 8)
                sp.dma_start(U[:, 1, :], u_in[1, 1]).then_inc(u_loaded[1], 16)

                def step(s, more):
                    if more:
                        sp.wait_ge(turned, s * 8 + 4)
                        sp.dma_start(U[:, 0, :], u_in[s + 1, 0]).then_inc(u_loaded[0], 16)
                    sp.wait_ge(weighted, s * 2)
                    sp.dma_start(W[:], w_in[s]).then_inc(w_loaded, 16)
                    sp.wait_ge(v_low, s * 2 - 1)
                    sp.dma_start(V[:, 0, :], v_in[s, 0]).then_inc(v_loaded[0], 16)
                    if more:
                        sp.wait_ge(turned, s * 8 + 8)
                        sp.dma_start(U[:, 1, :], u_in[s + 1, 1]).then_inc(u_loaded[1], 16)
                    sp.wait_ge(v_low, s * 2)
                    sp.dma_start(V[:, 1, :], v_in[s, 1]).then_inc(v_loaded[1], 16)

                with sp.Fori(1, STEPS - 1) as s:
                    step(s, True)
                step(STEPS - 1, False)

            @block.gpsimd
            def _(pool):
                with pool.Fori(0, STEPS) as s:
                    for c in range(2):
                        pool.wait_ge(v_high, s * 2 + c + 1)
                        pool.tensor_tensor(VL[:, c, :], V[:, c, :], VH[:, c, :], ALU.subtract).then_inc(v_low, 1)

            @block.scalar
            def _(act):
                def first_split():
                    for b in range(4):
                        act.wait_ge(turned, b + 1)
                        act.activation(UH[:, 0, 4 * b:4 * b + 4, :], PS[:, b, :].rearrange("p (j e) -> p j e", j=4), ACT.Copy).then_inc(uT_high, 1)

                def split_second(s):
                    for b in range(4):
                        act.wait_ge(turned, s * 8 + 4 + b + 1)
                        if b == 0:
                            act.wait_ge(hidden_done, s * 2)
                        act.activation(UH[:, 1, 4 * b:4 * b + 4, :], PS[:, b, :].rearrange("p (j e) -> p j e", j=4), ACT.Copy).then_inc(uT_high, 1)

                def split_next(s):
                    for b in range(4):
                        act.wait_ge(turned, s * 8 + 8 + b + 1)
                        if b == 0:
                            act.wait_ge(hidden_done, s * 2 + 1)
                        act.activation(UH[:, 0, 4 * b:4 * b + 4, :], PS[:, b, :].rearrange("p (j e) -> p j e", j=4), ACT.Copy).then_inc(uT_high, 1)

                def gelu(s, c):
                    act.wait_ge(hidden_done, s * 2 + c + 1)
                    act.wait_ge(weighted, s * 2)
                    act.activation(GE[:, c, :], PS[:, 4 + c, 0:T], ACT.Gelu).then_inc(gelu_ready, 1)

                def split_v(s):
                    act.wait_ge(out_done, s * KT)
                    for c in range(2):
                        act.wait_ge(v_loaded[c], s * 16 + 16)
                        act.activation(VH[:, c, :], V[:, c, :], ACT.Copy).then_inc(v_high, 1)

                first_split()
                with act.Fori(0, STEPS - 1) as s:
                    split_second(s)
                    split_next(s)
                    gelu(s, 0)
                    gelu(s, 1)
                    split_v(s)
                split_second(STEPS - 1)
                gelu(STEPS - 1, 0)
                gelu(STEPS - 1, 1)
                split_v(STEPS - 1)

            @block.vector
            def _(dve):
                def low_u(c, n):
                    for b in range(4):
                        dve.wait_ge(uT_high, n + b + 1)
                        dve.tensor_tensor(UL[:, c, 4 * b:4 * b + 4, :], PS[:, b, :].rearrange("p (j e) -> p j e", j=4),
                                          UH[:, c, 4 * b:4 * b + 4, :], ALU.subtract).then_inc(uT_low, 1)

                def add_outputs(s):
                    for d in range(KT):
                        dve.wait_ge(out_done, s * KT + d + 1)
                        dve.tensor_tensor(hT[:, d, :], PS[:, 6 + d % 2, 0:T], hT[:, d, :], ALU.add).then_inc(added, 1)

                def weigh(s):
                    dve.wait_ge(w_loaded, s * 16 + 16)
                    for c in range(2):
                        dve.wait_ge(gelu_ready, s * 2 + c + 1)
                        dve.wait_ge(act_ready, s * 2)
                        dve.tensor_tensor(GA[:, c, :].rearrange("p (k t) -> p k t", k=TOKEN_BLOCKS),
                                          GE[:, c, :].rearrange("p (k t) -> p k t", k=TOKEN_BLOCKS), W[:, :, c, :], ALU.mult).then_inc(weighted, 1)
                    for c in range(2):
                        dve.wait_ge(weighted, s * 2 + c + 1)
                        dve.tensor_copy(GH[:, c, :], GA[:, c, :]).then_inc(act_high, 1)
                    for c in range(2):
                        dve.wait_ge(act_high, s * 2 + c + 1)
                        dve.tensor_tensor(GL[:, c, :], GA[:, c, :], GH[:, c, :], ALU.subtract).then_inc(act_ready, 1)

                low_u(0, 0)
                low_u(1, 4)
                low_u(0, 8)
                weigh(0)
                with dve.Fori(1, STEPS - 1) as s:
                    low_u(1, s * 8 + 4)
                    low_u(0, s * 8 + 8)
                    add_outputs(s - 1)
                    weigh(s)
                low_u(1, STEPS * 8 - 4)
                add_outputs(STEPS - 2)
                weigh(STEPS - 1)
                add_outputs(STEPS - 1)

            @block.tensor
            def _(pe):
                def turn(s, c):
                    pe.wait_ge(u_loaded[c], s * 16 + 16)
                    for b in range(4):
                        pe.wait_ge(uT_low, s * 8 + 4 * c - 4 + b + 1)
                        for j in range(4):
                            k = 4 * b + j
                            last = pe.transpose(PS[:, b, j * P:(j + 1) * P], U[:, c, k * P:(k + 1) * P], ident[:])
                        last.then_inc(turned, 1)

                def turn_first():
                    pe.wait_ge(u_loaded[0], 16)
                    for b in range(4):
                        for j in range(4):
                            k = 4 * b + j
                            last = pe.transpose(PS[:, b, j * P:(j + 1) * P], U[:, 0, k * P:(k + 1) * P], ident[:])
                        last.then_inc(turned, 1)

                def hidden(s, c):
                    out = PS[:, 4 + c, 0:T]
                    pe.wait_ge(gelu_ready, s * 2)
                    pe.wait_ge(uT_low, s * 8 + 4 * c + 4)
                    for k in range(KT):
                        pe.matmul(out, UH[:, c, k, :], XH[:, k, :], start=(k == 0), stop=False)
                        pe.matmul(out, UH[:, c, k, :], XL[:, k, :], start=False, stop=False)
                        last = pe.matmul(out, UL[:, c, k, :], XH[:, k, :], start=False, stop=(k == KT - 1))
                    last.then_inc(hidden_done, 1)

                def output(s):
                    pe.wait_ge(act_ready, s * 2 + 2)
                    pe.wait_ge(v_low, s * 2 + 2)
                    for d in range(KT):
                        if d >= 2:
                            pe.wait_ge(added, s * KT + d - 1)
                        else:
                            pe.wait_ge(added, s * KT)
                        out = PS[:, 6 + d % 2, 0:T]
                        cols = slice(d * P, (d + 1) * P)
                        for c in range(2):
                            pe.matmul(out, VH[:, c, cols], GH[:, c, :], start=(c == 0), stop=False)
                            pe.matmul(out, VH[:, c, cols], GL[:, c, :], start=False, stop=False)
                            last = pe.matmul(out, VL[:, c, cols], GH[:, c, :], start=False, stop=(c == 1))
                        last.then_inc(out_done, 1)

                turn_first()
                turn(0, 1)
                hidden(0, 0)
                turn(1, 0)
                hidden(0, 1)
                with pe.Fori(1, STEPS - 1) as s:
                    turn(s, 1)
                    hidden(s, 0)
                    turn(s + 1, 0)
                    hidden(s, 1)
                    output(s - 1)
                turn(STEPS - 1, 1)
                hidden(STEPS - 1, 0)
                hidden(STEPS - 1, 1)
                output(STEPS - 2)
                output(STEPS - 1)


def store_outputs(nc, G, yT):
    PS, ident, O = G["PS"], G["ident"], G["O"]
    with ExitStack() as ctx:
        st = Stage(nc, ctx, "y")
        Y = st.sb("rows", [P, 3, D_MODEL])
        turned, ready, stored = st.sems("turned", "ready", "stored")
        outs = [O["y_prompt"][0, 0:P], O["y_prompt"][0, P:SEQ], O["y_sample"].rearrange("b s d -> (b s) d")]
        with nc.Block() as block:
            @block.tensor
            def _(pe):
                for n in range(12):
                    (t0, r), g = TOKEN_TILES[n // 4], n % 4
                    if n >= 8:
                        pe.wait_ge(ready, n - 7)
                    for j in range(4):
                        last = pe.transpose(PS[0:r, n % 8, j * P:(j + 1) * P], yT[:, 4 * g + j, t0:t0 + r], ident[:])
                    last.then_inc(turned, 1)

            @block.vector
            def _(dve):
                for n in range(12):
                    (t0, r), g = TOKEN_TILES[n // 4], n % 4
                    dve.wait_ge(turned, n + 1)
                    dve.tensor_copy(Y[0:r, n // 4, g * 512:(g + 1) * 512], PS[0:r, n % 8, :]).then_inc(ready, 1)

            @block.sync
            def _(sp):
                for i, (_, r) in enumerate(TOKEN_TILES):
                    sp.wait_ge(ready, 4 * i + 4)
                    sp.dma_start(outs[i], Y[0:r, i, :]).then_inc(stored, 16)
                sp.wait_ge(stored, 48)


_OUTS = [
    ("y_prompt", (1, SEQ, D_MODEL)),
    ("y_sample", (DEC_BATCH, DEC_SEQ, D_MODEL)),
    ("ret_state_prompt", (1, 1, RET_HEADS, RET_DK, RET_DV)),
    ("diff_k_prompt", (1, 1, SEQ, 2 * DIFF_HEADS, DIFF_HD)),
    ("diff_v_prompt", (1, 1, SEQ, DIFF_HEADS, 2 * DIFF_HD)),
    ("mem_k_prompt", (1, 1, MEM_TOKENS, MEM_HEADS, MEM_HD)),
    ("mem_v_prompt", (1, 1, MEM_TOKENS, MEM_HEADS, MEM_HD)),
    ("ret_state_sample", (1, DEC_BATCH, RET_HEADS, RET_DK, RET_DV)),
    ("diff_k_sample", (1, DEC_BATCH, DEC_SEQ, 2 * DIFF_HEADS, DIFF_HD)),
    ("diff_v_sample", (1, DEC_BATCH, DEC_SEQ, DIFF_HEADS, 2 * DIFF_HD)),
]


def kernel(**inputs):
    import numpy as _np
    import concourse.bacc as _bacc
    from concourse import mybir as _mybir
    from concourse.bass_utils import run_bass_kernel_spmd as _run

    nc = _bacc.Bacc("TRN2", target_bir_lowering=False, num_devices=1)
    arrays, A = {}, {}
    for name, value in inputs.items():
        a = _np.ascontiguousarray(value)
        arrays[f"in_{name}_dram"] = a
        A[name] = nc.dram_tensor(f"in_{name}_dram", a.shape, _mybir.dt.from_np(a.dtype), kind="ExternalInput").ap()
    O = {name: nc.dram_tensor(f"out_{name}_dram", shape, _mybir.dt.float32, kind="ExternalOutput").ap() for name, shape in _OUTS}
    decoder_step_kernel(nc, A, O)
    r = _run(nc, [arrays], core_ids=[0])
    return tuple(r.results[0][f"out_{name}_dram"] for name, _ in _OUTS)
```

```python
import math
from contextlib import ExitStack

import numpy as np

import concourse.bass as bass
from concourse import mybir

ALU = mybir.AluOpType
ACT = mybir.ActivationFunctionType
AX = mybir.AxisListType
F32 = mybir.dt.float32
F32R = mybir.dt.float32r
U32 = mybir.dt.uint32
I32 = mybir.dt.int32
ds = bass.ds

P = 128
D_MODEL = 2048
KT = D_MODEL // P
SEQ = 256
DEC_BATCH = 8
DEC_SEQ = 4
PAST = 256
PAGE = 128
N_PAGES = PAST // PAGE
NEW = DEC_BATCH * DEC_SEQ
T = SEQ + NEW
TOKEN_TILES = ((0, P), (P, P), (SEQ, NEW))
RET_HEADS = 8
RET_DK = D_MODEL // 16
RET_DV = 2 * RET_DK
DIFF_HEADS = 8
DIFF_HD = D_MODEL // 32
MEM_TOKENS = 256
MEM_HEADS = 4
MEM_HD = D_MODEL // 16
REL_BUCKETS = 32
REL_MAX_DIST = 128
PEER_HEADS = 8
NKEYS = 128
EXPERTS = NKEYS * NKEYS
TOPK = 16
EPS = 1e-6
LAMBDA_INIT = 0.8 - 0.6 * math.exp(-0.3 * 0)
MASKED = -1e30

RQ, RK, RV, RG, DQ, DK, DV, MQ = 0, 8, 16, 32, 48, 56, 64, 72
Z_TILES = 76
GATE_TILES = 3 * KT
O_RET, O_DIFF, O_MEM, O_TILES = 0, 16, 24, 28


START = 32


def after(count):
    return count + START


class Signals:

    def __init__(self, nc, ctx, first):
        self.nc = nc
        self.sems = [ctx.enter_context(nc.semaphore(f"signal_{n}")) for n in sorted(nc.free_semaphores)]
        self.taken = 0
        self.start(first)

    def take(self):
        self.taken += 1
        assert self.taken <= self.started
        return self.sems[self.taken - 1]

    def restart(self, count):
        with self.nc.Block() as block:
            @block.gpsimd
            def _(pool):
                numbers = [s.num for s in self.sems]
                for first in [n for n in numbers if n - 1 not in numbers]:
                    last = first
                    while last + 1 in numbers:
                        last += 1
                    pool.sem_clear(range(first, last + 1))
        self.taken = 0
        self.start(count)

    def start(self, count):
        self.started = count

        def share(engine, k):
            for sem in self.sems[k:count:4]:
                engine.sem_inc(sem, START)

        with self.nc.Block() as block:
            @block.scalar
            def _(act):
                share(act, 0)

            @block.vector
            def _(dve):
                share(dve, 1)

            @block.tensor
            def _(pe):
                share(pe, 2)

            @block.gpsimd
            def _(pool):
                share(pool, 3)


class WeightStream:

    UNITS = 4

    def __init__(self, nc, G, ctx, name, kt=KT, loads=(1, 1), buffers=None, side="left"):
        sem = G["signals"].take

        self.kt = kt
        self.loads = loads
        self.psum = G["PS"]
        if buffers is None:
            buffers = (ctx.enter_context(nc.sbuf_tensor(f"{name}_raw", [P, 2, kt, 2 * P], F32, side=side)),
                       ctx.enter_context(nc.sbuf_tensor(f"{name}_high", [P, 2, kt, P], F32R, side=side)),
                       ctx.enter_context(nc.sbuf_tensor(f"{name}_low", [P, 2, kt, P], F32R, side=side)))
        self.buffers = self.raw, self.high, self.low = buffers
        self.loaded = [sem(), sem()]
        self.high_ready = sem()
        self.low_ready = sem()
        self.product_done = sem()
        self.slot_free = sem()
        self.bank_free = sem()

    def half(self, u):
        return self.raw[:, u // 2, :, (u % 2) * P:(u % 2 + 1) * P]

    def load(self, sp, i, b, columns, first=False):
        if not first:
            sp.wait_ge(self.low_ready, after(self.UNITS * i - self.UNITS + 2 * b + 2))
        k = 0
        for part in columns:
            sp.dma_start(self.raw[:, b, k:k + part.shape[1], :], part).then_inc(self.loaded[b], 16)
            k += part.shape[1]

    def load_ahead(self, sp, columns, before=None, units=0):
        for b in range(2):
            if before is not None:
                sp.wait_ge(before.low_ready, after(units - 2 + 2 * b))
            self.load(sp, 0, b, columns(b), first=True)

    def open(self, pe):
        pe.sem_inc(self.slot_free, 2)
        pe.sem_inc(self.bank_free, 2)

    def wait_product(self, dve, i, u):
        dve.wait_ge(self.product_done, after(i * self.UNITS + u + 1))
        dve.sem_inc(self.slot_free, 1)

    def split_high(self, act, i, u, kt=None):
        kt = kt or self.kt
        act.wait_ge(self.loaded[u // 2], after(i * (16 * self.loads[u // 2]) + 16 * self.loads[u // 2]))
        act.wait_ge(self.slot_free, after(i * self.UNITS + u + 1))
        act.activation(self.high[:, u % 2, 0:kt, :], self.half(u)[:, 0:kt, :], ACT.Copy).then_inc(self.high_ready, 1)

    def split_low(self, dve, i, u, kt=None):
        kt = kt or self.kt
        dve.wait_ge(self.high_ready, after(i * self.UNITS + u + 1))
        dve.tensor_tensor(self.low[:, u % 2, 0:kt, :], self.half(u)[:, 0:kt, :], self.high[:, u % 2, 0:kt, :],
                          ALU.subtract).then_inc(self.low_ready, 1)

    def follow(self, dve, i, evacuate, last=False, kts=None):
        kts = kts or [self.kt] * self.UNITS
        for u in range(self.UNITS):
            if u < self.UNITS - 1:
                self.split_low(dve, i, u + 1, kts[u + 1])
            elif not last:
                self.split_low(dve, i + 1, 0, kts[0])
            self.wait_product(dve, i, u)
            evacuate(i, u)

    def product(self, pe, i, u, groups):
        n = i * self.UNITS + u + 1
        pe.wait_ge(self.high_ready, after(n))
        pe.wait_ge(self.bank_free, after(n))
        for out, k0, (xh, xl) in groups:
            kts = xh.shape[1]
            for k in range(kts):
                w = self.high[:, u % 2, k0 + k, :]
                pe.matmul(out, w, xh[:, k, :], start=(k == 0), stop=False)
                pe.matmul(out, w, xl[:, k, :], start=False, stop=False)
        pe.wait_ge(self.low_ready, after(n))
        for out, k0, (xh, xl) in groups:
            kts = xh.shape[1]
            for k in range(kts):
                last = pe.matmul(out, self.low[:, u % 2, k0 + k, :], xh[:, k, :], start=False, stop=(k == kts - 1))
        last.then_inc(self.product_done, 1)


def decoder_step_kernel(nc, A, O):
    top = ExitStack()
    with top:
        PS = top.enter_context(nc.psum_tensor("banks", [P, 8, 512], F32))

        def const(name, array):
            t = nc.inline_tensor(np.ascontiguousarray(array, np.float32), name)
            return t.ap() if hasattr(t, "ap") and callable(t.ap) else t

        def scratch(name, shape):
            return nc.dram_tensor(name, shape, F32, kind="Internal").ap()

        C = constants(const)
        S = {"x_T": scratch("x_T", (KT, P, T)), "gates_T": scratch("gates_T", (GATE_TILES, P, T)),
             "bias_rows": scratch("bias_rows", (DIFF_HEADS, P, 512)),
             "gelu": scratch("gelu", (2 * HEAD, P, T)),
             "peer_weights": scratch("peer_weights", (TOKEN_BLOCKS, P, NKEYS, TB)),
             "mem_T": scratch("mem_T", (2 * MEM_HEADS, P, MEM_TOKENS))}
        signals = Signals(nc, top, 45)
        ident = top.enter_context(nc.sbuf_tensor("ident", [P, P], F32))
        ones = top.enter_context(nc.sbuf_tensor("ones", [P, P], F32))
        load_constants(nc, signals, C, ident, ones)
        G = dict(signals=signals, PS=PS, ident=ident, ones=ones, A=A, O=O, C=C, S=S)
        memory_projection(nc, G)
        with ExitStack() as left, ExitStack() as right:
            def tensor(stack, side, name, shape, dt=F32):
                return stack.enter_context(nc.sbuf_tensor(name, shape, dt, side=side))

            Z = tensor(left, "left", "Z", [P, Z_TILES, T])
            input_projection(nc, G, Z)
            signals.restart(111)
            ODM = tensor(left, "left", "branch_outputs", [P, DIFF_HEADS + MEM_HEADS, T])
            attention(nc, G, Z, ODM)
            OTH = tensor(right, "right", "o_high", [P, O_TILES, T], F32R)
            OTL = tensor(right, "right", "o_low", [P, O_TILES, T], F32R)
            split_branch_outputs(nc, G, Z, ODM, OTH, OTL)
            signals.restart(62)
            left.close()
            w_up = WeightStream(nc, G, left, "w", loads=(1, 2))
            w_out, w_q = (WeightStream(nc, G, left, name, buffers=w_up.buffers) for name in ("wout", "wq"))
            with ExitStack() as inner:
                MH = tensor(inner, "left", "mixed_high", [P, KT, T], F32R)
                ML = tensor(inner, "left", "mixed_low", [P, KT, T], F32R)
                up_projections(nc, G, OTH, OTL, MH, ML, w_up, w_out)
                right.close()
                hT = tensor(right, "right", "h_T", [P, KT, T])
                output_projection(nc, G, MH, ML, hT, w_out, w_q)
            XH = tensor(right, "right", "x2_high", [P, KT, T], F32R)
            XL = tensor(right, "right", "x2_low", [P, KT, T], F32R)
            with nc.sbuf_tensor("selection_area", [P, 2 * NKEYS * TB], F32, side="right") as area:
                norm_split(nc, G, "ffn", hT, T, A["norm_ffn_w"][0], XH, XL)
                QT = area[:, 5 * 2 * PEER_HEADS * P:5 * 2 * PEER_HEADS * P + 2 * PEER_HEADS * TPAD].rearrange("p (g t) -> p g t", t=TPAD)
                peer_queries(nc, G, XH, XL, QT, w_q)
                left.close()
                peer_selection(nc, G, area, QT, XH, XL)
            signals.restart(66)
            U = tensor(right, "right", "u", [P, 2, D_MODEL])
            u_loaded = [signals.take(), signals.take()]
            peer_stashed(nc, G, hT, U, u_loaded)
            peer_experts(nc, G, XH, XL, hT, U, u_loaded)
            norm_split(nc, G, "final", hT, T, A["norm_final_w"], None, None, plain=hT)
            store_outputs(nc, G, hT)


def constants(const):
    f = np.float32
    C = {"ident": const("c_ident", np.eye(P))}
    half = RET_DK // 2
    inv = f(1.0) / (f(10000.0) ** np.linspace(0.0, 1.0, half, dtype=f))
    pos = np.concatenate([np.arange(SEQ), PAST + np.tile(np.arange(DEC_SEQ), DEC_BATCH)]).astype(f)
    angle = (pos[None, :] * inv[:, None]).astype(f).astype(np.float64)
    cos = np.tile(np.cos(angle), (2, 1))
    sin = np.tile(np.sin(angle), (2, 1))
    scale = RET_DK ** -0.5
    C["cos"] = const("c_cos", np.stack([cos, cos * scale], 1))
    C["sin"] = const("c_sin", np.stack([sin, sin * scale], 1))
    R = np.zeros((P, P))
    for m in range(half):
        R[m + half, m] = -1.0
        R[m, m + half] = 1.0
    C["rotate"] = const("c_rotate", R)
    lg = np.log1p(-np.exp2(-5.0 - np.arange(RET_HEADS)))
    j, i = np.arange(P)[:, None], np.arange(SEQ)[None, :]
    D = np.where(i >= j, np.exp(lg[:, None, None] * np.maximum(i - j, 0)), 0.0)
    C["decay"] = const("c_decay", np.concatenate([D, D[:, :, :P]], 2).transpose(1, 0, 2))
    b, s = np.divmod(np.arange(NEW), DEC_SEQ)
    same = (b[:, None] == b[None, :]) & (s[None, :] >= s[:, None])
    Dn = np.where(same, np.exp(lg[:, None, None] * np.maximum(s[None, :] - s[:, None], 0)), 0.0)
    C["decay_new"] = const("c_decay_new", Dn.transpose(1, 0, 2))
    tok = np.arange(SEQ).reshape(2, P).T
    C["decay_to_end"] = const("c_decay_to_end", np.exp(lg[None, :, None] * (SEQ - 1 - tok[:, None, :])))
    own = (b[:, None] == np.arange(DEC_BATCH)[None, :])
    C["decay_to_end_new"] = const("c_decay_to_end_new", np.exp(lg[None, :, None] * (DEC_SEQ - 1 - s[:, None, None])) * own[:, None, :])
    C["decay_from_state"] = const("c_decay_from_state", np.broadcast_to(np.exp(lg[:, None] * (s[None, :] + 1)), (P, RET_HEADS, NEW)))
    C["decay_state"] = const("c_decay_state", np.broadcast_to(np.exp(lg * DEC_SEQ), (P, RET_HEADS)))
    def bucket(rel):
        n = np.maximum(rel, 0)
        exact = REL_BUCKETS // 2
        nf = np.maximum(n, 1).astype(f)
        large = exact + (np.log(nf / exact) / math.log(REL_MAX_DIST / exact) * (REL_BUCKETS - exact)).astype(np.int32)
        return np.where(n < exact, n, np.minimum(large, REL_BUCKETS - 1))
    rel = 255 - np.arange(512)
    hot = np.zeros((REL_BUCKETS + 1, 512))
    hot[bucket(rel), np.arange(512)] = rel >= 0
    hot[REL_BUCKETS] = np.where(rel < 0, MASKED, 0.0)
    C["buckets"] = const("c_buckets", hot)
    kpos = np.concatenate([np.arange(PAST), PAST + s])
    hot = np.zeros((DEC_SEQ, REL_BUCKETS, PAST + NEW))
    for q in range(DEC_SEQ):
        hot[q, bucket(PAST + q - kpos), np.arange(PAST + NEW)] = 1.0
    C["buckets_new"] = const("c_buckets_new", hot.reshape(P, -1))
    C["own_position"] = const("c_own_position", (np.repeat(np.arange(DEC_SEQ), REL_BUCKETS)[:, None] == np.tile(np.arange(DEC_SEQ), 2)[None, :]))
    rb, rh, rm, rs = np.unravel_index(np.arange(P), (2, DIFF_HEADS, 2, DEC_SEQ))
    mask = np.zeros((P, DEC_BATCH // 2, NEW))
    for pair in range(DEC_BATCH // 2):
        seen = (b[None, :] == 2 * pair + rb[:, None]) & (s[None, :] <= rs[:, None])
        mask[:, pair] = np.where(seen, 0.0, MASKED)
    C["mask_new"] = const("c_mask_new", mask)
    C["map_is_0_1"] = const("c_map_is_0_1", np.stack([rm == 0, rm == 1], 1))
    C["iota"] = const("c_iota", np.broadcast_to(np.arange(P), (P, P)))
    return C


class Stage:

    def __init__(self, nc, G, ctx, name):
        self.nc, self.signals, self.ctx, self.name = nc, G["signals"], ctx, name

    def sb(self, what, shape, dt=F32):
        return self.ctx.enter_context(self.nc.sbuf_tensor(f"{self.name}_{what}", shape, dt))

    def sems(self, *names):
        return [self.signals.take() for _ in names]


def load_tables(nc, st, tables):
    (loaded,) = st.sems("tables_loaded")
    with nc.Block() as block:
        @block.sync
        def _(sp):
            for dst, src in tables:
                sp.dma_start(dst, src).then_inc(loaded, 16)
            sp.wait_ge(loaded, after(16 * len(tables)))


def retention(nc, G, Z):
    PS, ident, ones, A, O, C = (G[k] for k in ("PS", "ident", "ones", "A", "O", "C"))
    with ExitStack() as ctx:
        st = Stage(nc, G, ctx, "ret")
        cos, sin = st.sb("cos", [P, 2, T]), st.sb("sin", [P, 2, T])
        rotate = st.sb("rotate", [P, P])
        decay = st.sb("decay", [P, RET_HEADS, SEQ + P])
        decay_new = st.sb("decay_new", [NEW, RET_HEADS, NEW])
        to_end = st.sb("to_end", [P, RET_HEADS, 2])
        to_end_new = st.sb("to_end_new", [NEW, RET_HEADS, DEC_BATCH])
        from_state = st.sb("from_state", [P, RET_HEADS, NEW])
        state_decay = st.sb("state_decay", [P, RET_HEADS])
        load_tables(nc, st, [(cos[:], C["cos"]), (sin[:], C["sin"]), (rotate[:], C["rotate"]), (decay[:], C["decay"]),
                             (decay_new[:], C["decay_new"]), (to_end[:], C["decay_to_end"]),
                             (to_end_new[:], C["decay_to_end_new"]), (from_state[:], C["decay_from_state"]),
                             (state_decay[:], C["decay_state"])])
        QK = st.sb("qk", [P, 2, T])
        rsin, rcos = st.sb("rsin", [P, 2, T]), st.sb("rcos", [P, 2, T])
        VT = st.sb("vT", [P, 2, T])
        V = st.sb("v", [P, 3, RET_DV])
        KD = st.sb("k_decayed", [P, 2, P])
        KDN = st.sb("k_decayed_new", [NEW, DEC_BATCH, P])
        PT, PTN = st.sb("scores", [P, SEQ + P]), st.sb("scores_new", [NEW, NEW])
        QG = st.sb("q_for_state", [P, NEW])
        ST = st.sb("state", [P, 2, DEC_BATCH, RET_DV])
        NS = st.sb("new_state", [P, DEC_BATCH, RET_DV])
        PST = st.sb("prompt_state", [P, RET_DV])
        SQ = st.sb("squares", [P, 2, T])
        MS, LN, R0, T1 = (st.sb(w, [P, RET_HEADS, T]) for w in ("mean_squares", "logs", "first_rstd", "t1"))
        T2 = ST[:].rearrange("p s b e -> p (s b e)")[:, 0:RET_HEADS * T].rearrange("p (h t) -> p h t", t=T)
        R1 = LN
        (silu_done, vT_ready, rotated, v_turned, v_ready, rope_parts, qk_ready, k_turned, kd_ready, scores_done, pt_ready,
         qg_ready, o_done, states_done, states_added, pstate_done, pstate_ready, squared, summed, ms_ready, logs, rstd_steps, gated,
         new_stored, pstate_stored) = st.sems(
            "silu_done", "vT_ready", "rotated", "v_turned", "v_ready", "rope_parts", "qk_ready", "k_turned", "kd_ready",
            "scores_done", "pt_ready", "qg_ready", "o_done", "states_done", "states_added", "pstate_done", "pstate_ready",
            "squared", "summed", "ms_ready", "logs", "rstd_steps", "gated", "new_stored", "pstate_stored")
        state_loaded = st.sems("state_loaded0", "state_loaded1")
        qk_z = Z[:, RQ:RQ + 16, :].rearrange("p (c h) t -> p h c t", c=2)
        v_z = Z[:, RV:RV + 16, :].rearrange("p (h e) t -> p h e t", e=2)
        g_z = Z[:, RG:RG + 16, :].rearrange("p (h e) t -> p h e t", e=2)
        state_in = A["state_ret"][0].rearrange("b h d e -> h d b e")
        state_out = O["ret_state_sample"][0].rearrange("b h d e -> h d b e")
        with nc.Block() as block:
            @block.sync
            def _(sp):
                for s in range(2):
                    sp.dma_start(ST[:, s, :, :], state_in[s]).then_inc(state_loaded[s], 16)

                def store(h):
                    sp.wait_ge(pstate_ready, after(h + 1))
                    sp.dma_start(O["ret_state_prompt"][0, 0, h], PST[:]).then_inc(pstate_stored, 16)
                    sp.wait_ge(states_added, after(h * 4 + 4))
                    sp.dma_start(state_out[h], NS[:]).then_inc(new_stored, 16)

                with sp.Fori(0, RET_HEADS // 2 - 1) as i:
                    for s in range(2):
                        store(i * 2 + s)
                        sp.dma_start(ST[:, s, :, :], state_in[i * 2 + s + 2]).then_inc(state_loaded[s], 16)
                for h in (RET_HEADS - 2, RET_HEADS - 1):
                    store(h)
                sp.wait_ge(pstate_stored, after(16 * RET_HEADS))
                sp.wait_ge(new_stored, after(16 * RET_HEADS))

            @block.scalar
            def _(act):
                def squares(h):
                    act.wait_ge(o_done, after(h + 1))
                    act.wait_ge(summed, after(h))
                    act.activation(SQ[:], PS[:, 6:8, 0:T], ACT.Square).then_inc(squared, 1)

                def head(h, first=False):
                    act.wait_ge(v_turned, after(h))
                    act.activation(VT[:], v_z[:, h], ACT.Copy).then_inc(vT_ready, 1)
                    if not first:
                        squares(h - 1)
                    act.wait_ge(v_turned, after(h + 1))
                    act.wait_ge(states_done, after(h * 4))
                    act.activation(V[:, 0:2, :], PS[:, 2, :].rearrange("p (t e) -> p t e", t=2), ACT.Copy)
                    act.activation(V[0:NEW, 2, :], PS[0:NEW, 3, 0:RET_DV], ACT.Copy).then_inc(v_ready, 1)
                    act.wait_ge(pstate_done, after(h + 1))
                    act.wait_ge(pstate_stored, after(h * 16))
                    act.activation(PST[:], PS[:, 5, 0:RET_DV], ACT.Copy).then_inc(pstate_ready, 1)

                for q in range(4):
                    g = Z[:, RG + 4 * q:RG + 4 * q + 4, :]
                    act.activation(g, g, ACT.Silu).then_inc(silu_done, 1)
                head(0, True)
                with act.Fori(1, RET_HEADS) as h:
                    head(h)
                squares(RET_HEADS - 1)
                act.wait_ge(ms_ready, after(RET_HEADS))
                act.activation(LN[:], MS[:], ACT.Ln).then_inc(logs, 1)
                act.wait_ge(logs, after(1))
                act.activation(R0[:], LN[:], ACT.Exp, scale=-0.5).then_inc(rstd_steps, 1)

            @block.vector
            def _(dve):
                def gate(h):
                    dve.wait_ge(squared, after(h + 1))
                    dve.tensor_tensor(g_z[:, h], PS[:, 6:8, 0:T], g_z[:, h], ALU.mult).then_inc(gated, 1)

                def add_states(h, s, loads):
                    dve.wait_ge(new_stored, after(h * 16))
                    dve.wait_ge(state_loaded[s], after(loads))
                    for r in range(4):
                        dve.wait_ge(states_done, after(h * 4 + r + 1))
                        dve.scalar_tensor_tensor(out=NS[:, 2 * r:2 * r + 2, :], in0=ST[:, s, 2 * r:2 * r + 2, :],
                                                 scalar=state_decay[:, ds(h, 1)],
                                                 in1=PS[:, 2 + r % 2, :].rearrange("p (b e) -> p b e", b=2),
                                                 op0=ALU.mult, op1=ALU.add).then_inc(states_added, 1)

                def mean_square(h):
                    dve.wait_ge(summed, after(h + 1))
                    dve.tensor_scalar(MS[:, h, :], PS[:, 0, 0:T], float(P) / RET_DV, EPS, ALU.mult, ALU.add).then_inc(ms_ready, 1)

                def head(h, s, loads):
                    dve.wait_ge(qk_ready, after(h))
                    dve.tensor_tensor(rcos[:], qk_z[:, h], cos[:], ALU.mult).then_inc(rope_parts, 1)
                    if loads is not None:
                        gate(h - 1)
                    dve.wait_ge(rotated, after(h + 1))
                    dve.tensor_tensor(rsin[:], PS[:, 0:2, 0:T], sin[:], ALU.mult).then_inc(rope_parts, 1)
                    dve.wait_ge(rope_parts, after(h * 2 + 2))
                    dve.wait_ge(scores_done, after(h))
                    dve.wait_ge(qg_ready, after(h))
                    dve.tensor_tensor(QK[:], rsin[:], rcos[:], ALU.add).then_inc(qk_ready, 1)
                    dve.wait_ge(qk_ready, after(h + 1))
                    dve.wait_ge(o_done, after(h))
                    dve.tensor_tensor(QG[:], QK[:, 0, SEQ:T], from_state[:, h, :], ALU.mult).then_inc(qg_ready, 1)
                    if loads is not None:
                        add_states(h - 1, 1 - s, loads)
                    dve.wait_ge(k_turned, after(h + 1))
                    dve.tensor_tensor(KD[:], PS[:, 1, 0:2 * P].rearrange("p (t d) -> p t d", t=2),
                                      to_end[:, h, :].unsqueeze(2).to_broadcast([P, 2, P]), ALU.mult).then_inc(kd_ready, 1)
                    dve.wait_ge(states_done, after(h * 4))
                    dve.tensor_tensor(KDN[:], PS[0:NEW, 1, 2 * P:3 * P].unsqueeze(1).to_broadcast([NEW, DEC_BATCH, P]),
                                      to_end_new[:, h, :].unsqueeze(2).to_broadcast([NEW, DEC_BATCH, P]), ALU.mult).then_inc(kd_ready, 1)
                    dve.wait_ge(scores_done, after(h + 1))
                    dve.tensor_tensor(PT[:], PS[:, 4, 0:SEQ + P], decay[:, h, :], ALU.mult).then_inc(pt_ready, 1)
                    dve.tensor_tensor(PTN[:], PS[0:NEW, 4, 3 * P:3 * P + NEW], decay_new[:, h, :], ALU.mult).then_inc(pt_ready, 1)
                    if loads is not None:
                        mean_square(h - 1)

                head(0, 0, None)
                dve.wait_ge(silu_done, after(4))
                with dve.Fori(0, RET_HEADS // 2 - 1) as i:
                    head(i * 2 + 1, 1, i * 16 + 16)
                    head(i * 2 + 2, 0, i * 16 + 16)
                last = RET_HEADS - 1
                head(last, 1, 16 * RET_HEADS // 2)
                gate(last)
                add_states(last, 1, 16 * RET_HEADS // 2)
                mean_square(last)
                dve.wait_ge(states_added, after(4 * RET_HEADS))
                dve.wait_ge(ms_ready, after(RET_HEADS))
                refine_rstd(dve, MS, R0, T1, T2, R1, rstd_steps, 1)
                dve.wait_ge(rstd_steps, after(4))
                dve.wait_ge(gated, after(RET_HEADS))
                dve.tensor_tensor(g_z[:, :], g_z[:, :], R1[:].unsqueeze(2).to_broadcast([P, RET_HEADS, 2, T]), ALU.mult)

            @block.tensor
            def _(pe):
                def states(h):
                    for r in range(4):
                        if r >= 2:
                            pe.wait_ge(states_added, after(h * 4 + r - 1))
                        for b in (2 * r, 2 * r + 1):
                            last = pe.matmul(PS[:, 2 + r % 2, (b % 2) * RET_DV:(b % 2 + 1) * RET_DV], KDN[:, b, :],
                                             V[0:NEW, 2, :], start=True, stop=True)
                        last.then_inc(states_done, 1)

                def sum_squares(h):
                    pe.wait_ge(squared, after(h + 1))
                    for e in range(2):
                        last = pe.matmul(PS[:, 0, 0:T], ones[:], SQ[:, e, :], start=(e == 0), stop=(e == 1))
                    last.then_inc(summed, 1)

                def head(h, s, loads, first=False):
                    pe.wait_ge(ms_ready, after(h - 1))
                    pe.matmul(PS[:, 0, 0:T], rotate[:], qk_z[:, h, 0, :], start=True, stop=True)
                    pe.matmul(PS[:, 1, 0:T], rotate[:], qk_z[:, h, 1, :], start=True, stop=True).then_inc(rotated, 1)
                    if not first:
                        states(h - 1)
                    pe.wait_ge(qk_ready, after(h + 1))
                    for t in range(2):
                        pe.transpose(PS[:, 1, t * P:(t + 1) * P], QK[:, 1, t * P:(t + 1) * P], ident[:])
                    pe.transpose(PS[0:NEW, 1, 2 * P:3 * P], QK[:, 1, SEQ:T], ident[:]).then_inc(k_turned, 1)
                    pe.wait_ge(pt_ready, after(h * 2))
                    pe.matmul(PS[:, 4, 0:SEQ], QK[:, 1, 0:P], QK[:, 0, 0:SEQ], start=True, stop=True)
                    pe.matmul(PS[:, 4, SEQ:SEQ + P], QK[:, 1, P:SEQ], QK[:, 0, P:SEQ], start=True, stop=True)
                    pe.matmul(PS[0:NEW, 4, 3 * P:3 * P + NEW], QK[:, 1, SEQ:T], QK[:, 0, SEQ:T], start=True, stop=True).then_inc(scores_done, 1)
                    pe.wait_ge(vT_ready, after(h + 1))
                    pe.wait_ge(states_added, after(h * 4))
                    for e in range(2):
                        for t in range(2):
                            pe.transpose(PS[:, 2, t * RET_DV + e * P:t * RET_DV + (e + 1) * P], VT[:, e, t * P:(t + 1) * P], ident[:])
                        last = pe.transpose(PS[0:NEW, 3, e * P:(e + 1) * P], VT[:, e, SEQ:T], ident[:])
                    last.then_inc(v_turned, 1)
                    if not first:
                        sum_squares(h - 1)
                    pe.wait_ge(v_ready, after(h + 1))
                    pe.wait_ge(kd_ready, after(h * 2 + 2))
                    pe.wait_ge(pt_ready, after(h * 2 + 2))
                    pe.wait_ge(pstate_ready, after(h))
                    for t in range(2):
                        last = pe.matmul(PS[:, 5, 0:RET_DV], KD[:, t, :], V[:, t, :], start=(t == 0), stop=(t == 1))
                    last.then_inc(pstate_done, 1)
                    pe.wait_ge(qg_ready, after(h + 1))
                    pe.wait_ge(gated, after(h))
                    pe.wait_ge(squared, after(h))
                    pe.wait_ge(state_loaded[s], after(loads))
                    for e in range(2):
                        es = slice(e * P, (e + 1) * P)
                        pe.matmul(PS[:, 6 + e, 0:SEQ], V[:, 0, es], PT[:, 0:SEQ], start=True, stop=False, skip_group_check=True)
                        pe.matmul(PS[:, 6 + e, P:SEQ], V[:, 1, es], PT[:, SEQ:SEQ + P], start=False, stop=False, skip_group_check=True)
                        pe.matmul(PS[:, 6 + e, SEQ:T], V[0:NEW, 2, es], PTN[:], start=False, stop=False, skip_group_check=True)
                        for b in range(DEC_BATCH):
                            c = slice(b * DEC_SEQ, (b + 1) * DEC_SEQ)
                            last = pe.matmul(PS[:, 6 + e, SEQ + b * DEC_SEQ:SEQ + (b + 1) * DEC_SEQ], ST[:, s, b, es], QG[:, c],
                                             start=False, stop=(b == DEC_BATCH - 1), skip_group_check=True)
                    last.then_inc(o_done, 1)

                head(0, 0, 16, True)
                with pe.Fori(0, RET_HEADS // 2 - 1) as i:
                    head(i * 2 + 1, 1, i * 16 + 16)
                    head(i * 2 + 2, 0, i * 16 + 32)
                last = RET_HEADS - 1
                head(last, 1, 16 * RET_HEADS // 2)
                states(last)
                sum_squares(last)


def refine_rstd(dve, ms, rstd, t1, t2, out, steps, n):
    dve.wait_ge(steps, after(n))
    dve.tensor_tensor(t1[:], ms[:], rstd[:], ALU.mult).then_inc(steps, 1)
    dve.wait_ge(steps, after(n + 1))
    dve.scalar_tensor_tensor(out=t2[:], in0=t1[:], scalar=-0.5, in1=rstd[:], op0=ALU.mult, op1=ALU.mult).then_inc(steps, 1)
    dve.wait_ge(steps, after(n + 2))
    dve.scalar_tensor_tensor(out=out[:], in0=t2[:], scalar=1.5, in1=rstd[:], op0=ALU.add, op1=ALU.mult).then_inc(steps, 1)


def load_constants(nc, signals, C, ident, ones):
    ident_loaded, ones_set = signals.take(), signals.take()
    with nc.Block() as block:
        @block.sync
        def _(sp):
            sp.dma_start(ident[:], C["ident"]).then_inc(ident_loaded, 16)
            sp.wait_ge(ident_loaded, after(16))

        @block.vector
        def _(dve):
            dve.memset(ones[:], 1.0 / P).then_inc(ones_set, 1)
            dve.wait_ge(ones_set, after(1))


def transposed_norm(nc, G, name, rows, gain, x, xT, XH, XL, spill=None, ahead=None):
    PS, ident = G["PS"], G["ident"]
    n = sum(r for _, r, _ in rows)
    with ExitStack() as ctx:
        sem = lambda what: G["signals"].take()
        x_loaded = [sem(f"x_loaded{i}") for i in range(len(rows))]
        transposed, xT_ready, spilled = (sem(w) for w in ("transposed", "xT_ready", "spilled"))
        with nc.Block() as block:
            @block.sync
            def _(sp):
                for i, (_, r, src) in enumerate(rows):
                    sp.dma_start(x[0:r, i, :], src).then_inc(x_loaded[i], 16)
                if ahead is not None:
                    ahead(sp)
                if spill is not None:
                    sp.wait_ge(xT_ready, after(4 * len(rows)))
                    sp.dma_start(spill.rearrange("k p t -> p k t"), xT[:]).then_inc(spilled, 16)
                    sp.wait_ge(spilled, after(16))

            @block.tensor
            def _(pe):
                for i, (_, r, _src) in enumerate(rows):
                    pe.wait_ge(x_loaded[i], after(16))
                    for g in range(4):
                        q = 4 * i + g
                        if q >= 4:
                            pe.wait_ge(xT_ready, after(q - 3))
                        for j in range(4):
                            k = 4 * g + j
                            last = pe.transpose(PS[:, q % 4, j * P:j * P + r], x[0:r, i, k * P:(k + 1) * P], ident[0:r, 0:r])
                        last.then_inc(transposed, 1)

            @block.vector
            def _(dve):
                for i, (t0, r, _src) in enumerate(rows):
                    for g in range(4):
                        q = 4 * i + g
                        dve.wait_ge(transposed, after(q + 1))
                        dve.tensor_copy(xT[:, 4 * g:4 * g + 4, t0:t0 + r],
                                        PS[:, q % 4, :].rearrange("p (j t) -> p j t", j=4)[:, :, 0:r]).then_inc(xT_ready, 1)
        norm_split(nc, G, name, xT, n, gain, XH, XL)


def norm_split(nc, G, name, xT, n, gain, XH, XL, plain=None, ahead=None):
    PS, ones = G["PS"], G["ones"]
    with ExitStack() as ctx:
        sem = lambda what: G["signals"].take()
        sq = ctx.enter_context(nc.sbuf_tensor(f"{name}_sq", [P, 4, n], F32))
        xn = ctx.enter_context(nc.sbuf_tensor(f"{name}_xn", [P, 4, n], F32))
        ms, root, raw_rstd, t1, t2, rstd = (ctx.enter_context(nc.sbuf_tensor(f"{name}_{w}", [P, n], F32))
                                            for w in ("ms", "root", "raw_rstd", "t1", "t2", "rstd"))
        g = ctx.enter_context(nc.sbuf_tensor(f"{name}_gain", [P, KT], F32))
        gain_loaded, squared, summed, rstd_steps, normed, high, low = (
            sem(w) for w in ("gain_loaded", "squared", "summed", "rstd_steps", "normed", "high", "low"))
        with nc.Block() as block:
            @block.sync
            def _(sp):
                with nc.allow_non_contiguous_dma(reason="one gain per partition"):
                    sp.dma_start(g[:], gain.rearrange("(k p) -> p k", p=P)).then_inc(gain_loaded, 16)
                if ahead is not None:
                    ahead(sp)

            @block.scalar
            def _(act):
                for k in range(KT):
                    if k >= 4:
                        act.wait_ge(summed, after(k - 3))
                    act.activation(sq[:, k % 4, :], xT[:, k, :], ACT.Square).then_inc(squared, 1)
                act.wait_ge(rstd_steps, after(1))
                act.activation(root[:], ms[:], ACT.Sqrt).then_inc(rstd_steps, 1)
                for k in range(KT) if plain is None else ():
                    act.wait_ge(normed, after(k + 1))
                    act.activation(XH[:, k, 0:n], xn[:, k % 4, :], ACT.Copy).then_inc(high, 1)

            @block.tensor
            def _(pe):
                for k in range(KT):
                    pe.wait_ge(squared, after(k + 1))
                    pe.matmul(PS[:, 0, 0:n], ones[:], sq[:, k % 4, :], start=(k == 0), stop=(k == KT - 1)).then_inc(summed, 1)

            @block.vector
            def _(dve):
                dve.wait_ge(summed, after(KT))
                dve.tensor_scalar(ms[:], PS[:, 0, 0:n], 1.0 / KT, EPS, ALU.mult, ALU.add).then_inc(rstd_steps, 1)
                dve.wait_ge(rstd_steps, after(2))
                dve.reciprocal(raw_rstd[:], root[:]).then_inc(rstd_steps, 1)
                refine_rstd(dve, ms, raw_rstd, t1, t2, rstd, rstd_steps, 3)
                dve.wait_ge(rstd_steps, after(6))
                dve.wait_ge(gain_loaded, after(16))
                for k in range(KT) if plain is not None else ():
                    dve.scalar_tensor_tensor(out=plain[:, k, :], in0=xT[:, k, :], scalar=g[:, k:k + 1], in1=rstd[:],
                                             op0=ALU.mult, op1=ALU.mult).then_inc(normed, 1)
                for k in range(KT) if plain is None else ():
                    if k >= 4:
                        dve.wait_ge(low, after(k - 3))
                    dve.scalar_tensor_tensor(out=xn[:, k % 4, :], in0=xT[:, k, :], scalar=g[:, k:k + 1], in1=rstd[:],
                                             op0=ALU.mult, op1=ALU.mult).then_inc(normed, 1)

            @block.gpsimd
            def _(pool):
                for k in range(KT) if plain is None else ():
                    pool.wait_ge(high, after(k + 1))
                    pool.tensor_tensor(XL[:, k, 0:n], xn[:, k % 4, :], XH[:, k, 0:n], ALU.subtract).then_inc(low, 1)


def memory_projection(nc, G):
    A = G["A"]
    with ExitStack() as ctx:
        MH = ctx.enter_context(nc.sbuf_tensor("mem_high", [P, KT, MEM_TOKENS], F32R))
        ML = ctx.enter_context(nc.sbuf_tensor("mem_low", [P, KT, MEM_TOKENS], F32R))
        mem = A["mem_prompt"][0]
        w = WeightStream(nc, G, ctx, "wmem")
        ws = [A[n][0].rearrange("(k p) n -> p k n", p=P) for n in ("w_mem_k", "w_mem_v")]
        x = ctx.enter_context(nc.sbuf_tensor("mem_rows", [P, 2, D_MODEL], F32))
        xT = ctx.enter_context(nc.sbuf_tensor("mem_rows_T", [P, KT, MEM_TOKENS], F32))
        transposed_norm(nc, G, "mem", [(0, P, mem[0:P]), (P, P, mem[P:2 * P])], A["norm_mem_w"][0], x[:], xT[:], MH, ML,
                        ahead=lambda sp: w.load_ahead(sp, lambda b: [ws[0][:, :, b * 2 * P:(b + 1) * 2 * P]]))
        out = ctx.enter_context(nc.sbuf_tensor("mem_kv_T", [P, 4, MEM_TOKENS], F32))
        projected = G["signals"].take()
        stored = G["signals"].take()
        with nc.Block() as block:
            @block.sync
            def _(sp):
                for b in range(2):
                    w.load(sp, 1, b, [ws[1][:, :, b * 2 * P:(b + 1) * 2 * P]])
                for i in range(2):
                    sp.wait_ge(projected, after(i + 1))
                    sp.dma_start(G["S"]["mem_T"][4 * i:4 * i + 4].rearrange("k p t -> p k t"), out[:]).then_inc(stored, 16)
                sp.wait_ge(stored, after(32))

            @block.scalar
            def _(act):
                for i in range(2):
                    for u in range(4):
                        w.split_high(act, i, u)

            @block.tensor
            def _(pe):
                w.open(pe)
                for i in range(2):
                    for u in range(4):
                        w.product(pe, i, u, [(w.psum[:, u % 2, 0:MEM_TOKENS], 0, (MH, ML))])

            @block.vector
            def _(dve):
                def keep(i, u):
                    if i:
                        dve.wait_ge(stored, after(16 * i))
                    dve.tensor_copy(out[:, u, :], w.psum[:, u % 2, 0:MEM_TOKENS]).then_inc(w.bank_free, 1)
                    if u == 3:
                        dve.wait_ge(w.bank_free, after(2 + 4 * i + u + 1))
                        dve.sem_inc(projected, 1)

                w.split_low(dve, 0, 0)
                w.follow(dve, 0, keep)
                w.follow(dve, 1, keep, last=True)


def input_projection(nc, G, Z):
    A, S = G["A"], G["S"]
    with ExitStack() as ctx:
        XH = ctx.enter_context(nc.sbuf_tensor("x_high", [P, KT, T], F32R))
        XL = ctx.enter_context(nc.sbuf_tensor("x_low", [P, KT, T], F32R))
        xp = A["x_prompt"][0]
        xs = A["x_sample"].rearrange("b s d -> (b s) d")
        w = WeightStream(nc, G, ctx, "win")
        win = A["w_in"][0].rearrange("(k p) n -> p k n", p=P)
        flat = Z[:].rearrange("p f t -> p (f t)")
        transposed_norm(nc, G, "x", [(0, P, xp[0:P]), (P, P, xp[P:2 * P]), (SEQ, NEW, xs)], A["norm_mix_w"][0],
                        flat[:, KT * T:KT * T + 3 * D_MODEL].rearrange("p (i d) -> p i d", i=3), Z[:, 0:KT, :], XH, XL, spill=S["x_T"],
                        ahead=lambda sp: w.load_ahead(sp, lambda b: [win[:, :, b * 2 * P:(b + 1) * 2 * P]]))
        gates = ctx.enter_context(nc.sbuf_tensor("gates", [P, 4, T], F32))
        gates_ready = G["signals"].take()
        gates_stored = G["signals"].take()
        ZI = Z_TILES // 4
        GI = GATE_TILES // 4
        gates_dram = S["gates_T"].rearrange("(i u) p t -> i p u t", u=4)
        with nc.Block() as block:
            @block.sync
            def _(sp):
                with sp.Fori(1, ZI + 1) as i:
                    for b in range(2):
                        w.load(sp, i, b, [win[:, :, ds(i * 512 + b * 2 * P, 2 * P)]])
                with sp.Fori(0, GI - 1) as g:
                    for b in range(2):
                        w.load(sp, g + ZI + 1, b, [win[:, :, ds(g * 512 + (ZI + 1) * 512 + b * 2 * P, 2 * P)]])
                    sp.wait_ge(gates_ready, after(g + 1))
                    sp.dma_start(gates_dram[g], gates[:]).then_inc(gates_stored, 16)
                sp.wait_ge(gates_ready, after(GI))
                sp.dma_start(gates_dram[GI - 1], gates[:]).then_inc(gates_stored, 16)
                sp.wait_ge(gates_stored, after(16 * GI))

            @block.scalar
            def _(act):
                with act.Fori(0, ZI + GI) as i:
                    for u in range(4):
                        w.split_high(act, i, u)

            @block.tensor
            def _(pe):
                w.open(pe)
                with pe.Fori(0, ZI + GI) as i:
                    for u in range(4):
                        w.product(pe, i, u, [(w.psum[:, u % 2, 0:T], 0, (XH, XL))])

            @block.vector
            def _(dve):
                def keep(i, u):
                    dve.tensor_copy(Z[:, i * 4 + u, :], w.psum[:, u % 2, 0:T]).then_inc(w.bank_free, 1)

                def keep_gate(i, u):
                    if u == 0:
                        dve.wait_ge(gates_stored, after((i - ZI) * 16))
                    dve.tensor_copy(gates[:, u, :], w.psum[:, u % 2, 0:T]).then_inc(w.bank_free, 1)
                    if u == 3:
                        dve.wait_ge(w.bank_free, after(i * 4 + 2 + 4))
                        dve.sem_inc(gates_ready, 1)

                w.split_low(dve, 0, 0)
                with dve.Fori(0, ZI) as i:
                    w.follow(dve, i, keep)
                with dve.Fori(ZI, ZI + GI - 1) as i:
                    w.follow(dve, i, keep_gate)
                w.follow(dve, ZI + GI - 1, keep_gate, last=True)


def diff_tables(nc, G, st):
    PS, A, C, S = (G[k] for k in ("PS", "A", "C", "S"))
    bias = st.sb("bias", [P, DIFF_HEADS, SEQ + P])
    bias_new = st.sb("bias_new", [P, PAST])
    bias_own = st.sb("bias_own", [P, DEC_BATCH // 2, NEW])
    neg_lam = st.sb("neg_lam", [P, 1])
    map_weights = st.sb("map_weights", [P, 4])
    row_weights = st.sb("row_weights", [P, 1])
    with ExitStack() as ctx:
        t = Stage(nc, G, ctx, "tab")
        rb = t.sb("rel_bias", [REL_BUCKETS + 1, DIFF_HEADS])
        rb_wide = t.sb("rel_bias_wide", [REL_BUCKETS + 1, DIFF_HEADS, P])
        buckets = t.sb("buckets", [REL_BUCKETS + 1, 512])
        rows = t.sb("bias_rows", [P, 2, 512])
        rb4 = t.sb("rel_bias_by_position", [P, DIFF_HEADS])
        own_pos = t.sb("own_position", [P, 8])
        picks = t.sb("picks", [P, 2, DIFF_HEADS, 8])
        buckets_new = t.sb("buckets_new", [P, PAST + NEW])
        mask_new = t.sb("mask_new", [P, DEC_BATCH // 2, NEW])
        lq = t.sb("lambda_parts", [P, 4, DIFF_HD])
        lp, le = t.sb("lambda_products", [P, 2, DIFF_HD]), t.sb("lambda_sums", [P, 2])
        lexp, ld = t.sb("lambda_exps", [P, 2]), t.sb("lambda_difference", [P, 1])
        maps = t.sb("maps", [P, 2])
        stored = t.sems("stored0", "stored1")
        ones_row, loaded, wide, biased, rows_ready, picked, new_done, lam_steps, read = t.sems(
            "ones_row", "loaded", "wide", "biased", "rows_ready", "picked", "new_done", "lam_steps", "read")
        with nc.Block() as block:
            @block.sync
            def _(sp):
                n = 0
                for dst, src in [(rb[0:REL_BUCKETS, :], A["rel_bias"]), (buckets[:], C["buckets"]),
                                 (own_pos[:], C["own_position"]), (buckets_new[:], C["buckets_new"]),
                                 (mask_new[:], C["mask_new"]), (maps[:], C["map_is_0_1"])] + [
                                     (rb4[q * REL_BUCKETS:(q + 1) * REL_BUCKETS, :], A["rel_bias"]) for q in range(DEC_SEQ)] + [
                                     (lq[:, j, :], A[k][0].partition_broadcast(P)) for j, k in enumerate(
                                         ("diff_lambda_q1", "diff_lambda_k1", "diff_lambda_q2", "diff_lambda_k2"))]:
                    sp.dma_start(dst, src).then_inc(loaded, 16)
                    n += 16
                G["table_loads"] = n
                for h in range(DIFF_HEADS):
                    sp.wait_ge(rows_ready, after(h + 1))
                    sp.dma_start(S["bias_rows"][h], rows[:, h % 2, :]).then_inc(stored[h % 2], 16)
                for b in range(2):
                    sp.wait_ge(stored[b], after(16 * DIFF_HEADS // 2))
                whole = S["bias_rows"]
                skewed = bass.AP(whole.tensor, P - 1, [[511, P], [P * 512, DIFF_HEADS], [1, SEQ + P]])
                sp.dma_start(bias[:], skewed).then_inc(read, 16)
                sp.wait_ge(read, after(16))
            n_loads = G["table_loads"]

            @block.vector
            def _(dve):
                dve.memset(rb[REL_BUCKETS:REL_BUCKETS + 1, :], 1.0).then_inc(ones_row, 1)
                dve.wait_ge(ones_row, after(1))
                dve.wait_ge(loaded, after(n_loads))
                dve.tensor_copy(rb_wide[:], rb[:].unsqueeze(2).to_broadcast([REL_BUCKETS + 1, DIFF_HEADS, P])).then_inc(wide, 1)
                for b in range(2):
                    dve.tensor_tensor(picks[:, b], rb4[:].unsqueeze(2).to_broadcast([P, DIFF_HEADS, 8]),
                                      own_pos[:].unsqueeze(1).to_broadcast([P, DIFF_HEADS, 8]), ALU.mult).then_inc(picked, 1)
                for h in range(DIFF_HEADS):
                    dve.wait_ge(biased, after(h + 1))
                    if h >= 2:
                        dve.wait_ge(stored[h % 2], after(16 * (h // 2)))
                    dve.tensor_copy(rows[:, h % 2, :], PS[:, h % 4, :]).then_inc(rows_ready, 1)
                dve.wait_ge(new_done, after(1))
                dve.tensor_copy(bias_new[:], PS[:, 4, 0:PAST])
                dve.tensor_tensor(bias_own[:], PS[:, 4, PAST:PAST + NEW].unsqueeze(1).to_broadcast([P, DEC_BATCH // 2, NEW]),
                                  mask_new[:], ALU.add)
                for j in range(2):
                    dve.tensor_tensor_reduce(lp[:, j, :], lq[:, 2 * j, :], lq[:, 2 * j + 1, :], 1.0, 0.0, ALU.mult, ALU.add,
                                             le[:, j:j + 1]).then_inc(lam_steps, 1)
                dve.wait_ge(lam_steps, after(3))
                dve.tensor_tensor(ld[:], lexp[:, 1:2], lexp[:, 0:1], ALU.subtract).then_inc(lam_steps, 1)
                dve.wait_ge(lam_steps, after(4))
                dve.tensor_scalar(neg_lam[:], ld[:], -LAMBDA_INIT, None, ALU.add).then_inc(lam_steps, 1)
                dve.wait_ge(lam_steps, after(5))
                dve.memset(map_weights[:], 1.0).then_inc(lam_steps, 1)
                dve.wait_ge(lam_steps, after(6))
                dve.tensor_scalar(map_weights[:, 2:4], map_weights[:, 2:4], neg_lam[:], None, ALU.mult)
                dve.scalar_tensor_tensor(out=row_weights[:], in0=maps[:, 1:2], scalar=neg_lam[:], in1=maps[:, 0:1],
                                         op0=ALU.mult, op1=ALU.add)

            @block.scalar
            def _(act):
                act.wait_ge(lam_steps, after(2))
                act.activation(lexp[:], le[:], ACT.Exp).then_inc(lam_steps, 1)

            @block.tensor
            def _(pe):
                pe.wait_ge(wide, after(1))
                for h in range(DIFF_HEADS):
                    if h >= 4:
                        pe.wait_ge(rows_ready, after(h - 3))
                    pe.matmul(PS[:, h % 4, :], rb_wide[:, h, :], buckets[:], start=True, stop=True).then_inc(biased, 1)
                pe.wait_ge(picked, after(2))
                pe.matmul(PS[:, 4, 0:PAST + NEW], picks[:].rearrange("p b h m -> p (b h m)"), buckets_new[:], start=True, stop=True).then_inc(new_done, 1)
    return bias, bias_new, bias_own, map_weights, row_weights


def diff_prompt(nc, G, Z, OD, v_new, bias, map_weights):
    PS, ident, O = (G[k] for k in ("PS", "ident", "O"))
    with ExitStack() as ctx:
        st = Stage(nc, G, ctx, "dp")
        QKV = st.sb("qkv_T", [P, 3, T])
        KV = st.sb("kv", [P, 2, 2, 3, P])
        S, E = st.sb("scores", [P, 2, 2, SEQ]), st.sb("exps", [P, 2, 2, SEQ])
        A1, A_ = st.sb("second_map", [P, 2, SEQ]), st.sb("a", [P, 2, SEQ])
        AT = st.sb("a_T", [P, SEQ + P])
        mx, nmx, sums, rec, coef = (st.sb(w, [P, 4]) for w in ("max", "neg_max", "sums", "reciprocals", "coefficients"))
        (staged, turned, kv_ready, scores_done, biased, soft, exps, parts, a_ready, a_turned, aT_ready, o_done,
         o_ready) = st.sems("staged", "turned", "kv_ready", "scores_done", "biased", "soft", "exps", "parts", "a_ready",
                              "a_turned", "aT_ready", "o_done", "o_ready")
        kv_stored = st.sems("kv_stored0", "kv_stored1")
        qkv_z = Z[:, DQ:DQ + 24, :].rearrange("p (c h) t -> p h c t", c=3)
        outs = []
        for c, (prompt, new) in enumerate((("diff_k_prompt", "diff_k_sample"), ("diff_v_prompt", "diff_v_sample"))):
            outs.append((O[prompt][0, 0].rearrange("(t p) m d -> p t (m d)", p=P), O[new][0].rearrange("b s m d -> (b s) (m d)")))
        last = DIFF_HEADS - 1
        with nc.Block() as block:
            @block.sync
            def _(sp):
                with sp.Fori(0, DIFF_HEADS // 2) as i:
                    for b in range(2):
                        sp.wait_ge(kv_ready, after(i * 2 + b + 1))
                        for c in range(2):
                            sp.dma_start(outs[c][0][:, :, ds(i * (2 * P) + b * P, P)], KV[:, b, c, 0:2, :]).then_inc(kv_stored[b], 16)
                            sp.dma_start(outs[c][1][:, ds(i * (2 * P) + b * P, P)], KV[0:NEW, b, c, 2, :]).then_inc(kv_stored[b], 16)
                for b in range(2):
                    sp.wait_ge(kv_stored[b], after(64 * DIFF_HEADS // 2))

            @block.scalar
            def _(act):
                def stage(h):
                    act.wait_ge(scores_done, after(h))
                    act.activation(QKV[:], qkv_z[:, h], ACT.Copy).then_inc(staged, 1)

                def keep(h, b, stores):
                    act.wait_ge(turned, after(h + 1))
                    act.wait_ge(kv_stored[b], after(stores))
                    act.wait_ge(o_done, after(h - 1))
                    act.activation(KV[:, b, :, 0:2, :], PS[:, 0:2, 0:2 * P].rearrange("p c (t d) -> p c t d", t=2), ACT.Copy)
                    act.activation(v_new[:, ds(h * P, P)], PS[0:NEW, 1, 2 * P:3 * P], ACT.Copy)
                    act.activation(KV[0:NEW, b, :, 2, :], PS[0:NEW, 0:2, 2 * P:3 * P], ACT.Copy).then_inc(kv_ready, 1)

                def exponentials(h):
                    act.wait_ge(soft, after(h * 4 + 2))
                    act.wait_ge(a_ready, after(h * 2))
                    for j in range(4):
                        act.activation(E[:, j // 2, j % 2, :], S[:, j // 2, j % 2, :], ACT.Exp, bias=nmx[:, j:j + 1],
                                       accum_out=sums[:, j:j + 1]).then_inc(exps, 1)

                def outputs(h):
                    act.wait_ge(a_turned, after(h + 1))
                    act.wait_ge(o_done, after(h))
                    act.activation(AT[:], PS[:, 4, 0:SEQ + P], ACT.Copy).then_inc(aT_ready, 1)
                    act.wait_ge(o_done, after(h + 1))
                    act.activation(OD[:, h, 0:SEQ], PS[:, 5, 0:SEQ], ACT.Copy).then_inc(o_ready, 1)

                def head(h, b, stores):
                    stage(h + 1)
                    exponentials(h)
                    keep(h + 1, b, stores)
                    outputs(h)

                stage(0)
                keep(0, 0, 0)
                with act.Fori(0, DIFF_HEADS // 2 - 1) as i:
                    head(i * 2, 1, i * 64)
                    head(i * 2 + 1, 0, i * 64 + 64)
                head(last - 1, 1, 64 * (DIFF_HEADS // 2 - 1))
                exponentials(last)
                outputs(last)

            @block.vector
            def _(dve):
                with dve.Fori(0, DIFF_HEADS) as h:
                    dve.wait_ge(scores_done, after(h + 1))
                    dve.wait_ge(exps, after(h * 4))
                    dve.wait_ge(soft, after(h * 4))
                    for q in range(2):
                        tile = bias[:, h, P - q * P:P - q * P + SEQ]
                        dve.scalar_tensor_tensor(out=S[:, :, q, :], in0=PS[:, 2:4, q * SEQ:(q + 1) * SEQ], scalar=DIFF_HD ** -0.5,
                                                 in1=tile.unsqueeze(1).to_broadcast([P, 2, SEQ]), op0=ALU.mult, op1=ALU.add).then_inc(biased, 1)
                    dve.wait_ge(biased, after(h * 2 + 2))
                    dve.tensor_reduce(mx[:], S[:].rearrange("p m q k -> p (m q) k"), AX.X, ALU.max).then_inc(soft, 1)
                    dve.wait_ge(soft, after(h * 4 + 1))
                    dve.tensor_scalar(nmx[:], mx[:], -1.0, None, ALU.mult).then_inc(soft, 1)
                    dve.wait_ge(exps, after(h * 4 + 4))
                    dve.reciprocal(rec[:], sums[:]).then_inc(soft, 1)
                    dve.wait_ge(soft, after(h * 4 + 3))
                    dve.wait_ge(a_ready, after(h * 2))
                    dve.tensor_tensor(coef[:], rec[:], map_weights[:], ALU.mult).then_inc(soft, 1)
                    dve.wait_ge(soft, after(h * 4 + 4))
                    for q in range(2):
                        dve.tensor_scalar(A1[:, q, :], E[:, 1, q, :], coef[:, 2 + q:3 + q], None, ALU.mult).then_inc(parts, 1)
                    dve.wait_ge(a_turned, after(h))
                    for q in range(2):
                        dve.wait_ge(parts, after(h * 2 + 1 + q))
                        dve.scalar_tensor_tensor(out=A_[:, q, :], in0=E[:, 0, q, :], scalar=coef[:, q:q + 1], in1=A1[:, q, :],
                                                 op0=ALU.mult, op1=ALU.add).then_inc(a_ready, 1)

            @block.tensor
            def _(pe):
                def scores(h):
                    pe.wait_ge(staged, after(h + 1))
                    pe.wait_ge(kv_ready, after(h))
                    for c in range(2):
                        for t, (t0, r) in enumerate(TOKEN_TILES):
                            final = pe.transpose(PS[0:r, c, t * P:(t + 1) * P], QKV[:, 1 + c, t0:t0 + r], ident[:])
                    final.then_inc(turned, 1)
                    pe.wait_ge(biased, after(h * 2))
                    for m in range(2):
                        rows = slice(m * DIFF_HD, (m + 1) * DIFF_HD)
                        for q in range(2):
                            final = pe.matmul(PS[:, 2 + m, q * SEQ:(q + 1) * SEQ], QKV[rows, 0, q * P:(q + 1) * P], QKV[rows, 1, 0:SEQ],
                                              start=True, stop=True)
                    final.then_inc(scores_done, 1)

                def attend(h, b):
                    pe.wait_ge(a_ready, after(h * 2 + 2))
                    pe.wait_ge(aT_ready, after(h))
                    pe.transpose(PS[:, 4, 0:P], A_[:, 0, 0:P], ident[:])
                    pe.transpose(PS[:, 4, P:SEQ], A_[:, 1, 0:P], ident[:])
                    pe.transpose(PS[:, 4, SEQ:SEQ + P], A_[:, 1, P:SEQ], ident[:]).then_inc(a_turned, 1)
                    pe.wait_ge(aT_ready, after(h + 1))
                    pe.wait_ge(kv_ready, after(h + 1))
                    pe.wait_ge(o_ready, after(h))
                    pe.matmul(PS[:, 5, 0:SEQ], KV[:, b, 1, 0, :], AT[:, 0:SEQ], start=True, stop=False)
                    pe.matmul(PS[:, 5, P:SEQ], KV[:, b, 1, 1, :], AT[:, SEQ:SEQ + P], start=False, stop=True).then_inc(o_done, 1)

                scores(0)
                with pe.Fori(0, DIFF_HEADS // 2 - 1) as i:
                    for b in range(2):
                        scores(i * 2 + b + 1)
                        attend(i * 2 + b, b)
                scores(last)
                attend(last - 1, 0)
                attend(last, 1)


def diff_sample(nc, G, Z, OD, v_new, bias_new, bias_own, row_weights):
    PS, ident, A = (G[k] for k in ("PS", "ident", "A"))
    ROWS = DIFF_HEADS * 2 * DEC_SEQ
    FT = DIFF_HEADS
    with ExitStack() as ctx:
        st = Stage(nc, G, ctx, "ds")
        pages = st.sb("pages", [1, DEC_BATCH * N_PAGES], I32)
        KP, VP = st.sb("k_pages", [P, 2, N_PAGES, FT * P]), st.sb("v_pages", [P, 2, N_PAGES, FT * P])
        KTT = st.sb("k_T", [P, 2, FT, PAST])
        QB = st.sb("q_blocks", [P, 2, FT * (ROWS + 8)])
        S, E, PN = (st.sb(w, [P, PAST + NEW]) for w in ("scores", "exps", "probs"))
        AT, ATN = st.sb("a_T", [P, 2, ROWS]), st.sb("a_T_new", [NEW, ROWS])
        mx, nmx, sums, rec, coef = (st.sb(w, [P, 1]) for w in ("max", "neg_max", "sums", "reciprocal", "coefficient"))
        (pages_loaded, zeroed, k_turned, kT_act, kT_dve, q_ready, scores_done, biased, soft, exps, probs, p_turned,
         aT_ready, o_done, o_ready) = st.sems(
            "pages_loaded", "zeroed", "k_turned", "kT_act", "kT_dve", "q_ready", "scores_done", "biased", "soft", "exps",
            "probs", "p_turned", "aT_ready", "o_done", "o_ready")
        k_loaded, v_loaded = (st.sems(f"{w}0", f"{w}1") for w in ("k_loaded", "v_loaded"))
        cache_k = A["cache_diff_k"][0].rearrange("n t m d -> n t (m d)")
        cache_v = A["cache_diff_v"][0].rearrange("n t m d -> n t (m d)")
        n_phys = cache_k.shape[0]
        q_blocks = QB[:].rearrange("p b (f c) -> p b f c", f=FT)

        def load(sp, i, s, pool_, buffer, loaded):
            for g in range(N_PAGES):
                page = sp.value_load(pages[0:1, ds(i * 4 + s * 2 + g, 1)], min_val=0, max_val=n_phys - 1)
                sp.dma_start(buffer[:, s, g, :], pool_[page]).then_inc(loaded[s], 16)

        with nc.Block() as block:
            @block.sync
            def _(sp):
                sp.dma_start(pages[:], A["page_table"].rearrange("(o b) g -> o (b g)", o=1)).then_inc(pages_loaded, 16)
                sp.wait_ge(pages_loaded, after(16))

                def load_keys(i, first=False):
                    for s in range(2):
                        if not first:
                            sp.wait_ge(k_turned, after(i * 8 + s * 4 - 4))
                        load(sp, i, s, cache_k, KP, k_loaded)

                def load_values(i):
                    sp.wait_ge(o_done, after(i))
                    for s in range(2):
                        load(sp, i, s, cache_v, VP, v_loaded)

                load_keys(0, True)
                load_values(0)
                load_keys(1)
                with sp.Fori(1, DEC_BATCH // 2 - 1) as i:
                    load_keys(i + 1)
                    load_values(i)
                load_values(DEC_BATCH // 2 - 1)

            @block.scalar
            def _(act):
                def turn_keys(i):
                    for s in range(2):
                        act.wait_ge(scores_done, after(i * 2 + s))
                        for j in (0, 2):
                            act.wait_ge(k_turned, after(i * 8 + s * 4 + j + 1))
                            act.activation(KTT[:, s, 2 * j:2 * j + 2, :], PS[:, j, :].rearrange("p (f t) -> p f t", f=2), ACT.Copy).then_inc(kT_act, 1)

                def attend(i, more=True):
                    act.wait_ge(soft, after(i * 4 + 2))
                    act.wait_ge(probs, after(i))
                    act.activation(E[:], S[:], ACT.Exp, bias=nmx[:], accum_out=sums[:]).then_inc(exps, 1)
                    if more:
                        turn_keys(i + 1)
                    act.wait_ge(o_done, after(i + 1))
                    act.activation(OD[:, 0:FT, ds(i * 8 + SEQ, 8)].rearrange("p h (b s) -> p h b s", b=2),
                                   PS[:, 6, 0:ROWS].rearrange("p (b h s) -> p h b s", b=2, s=DEC_SEQ), ACT.Copy).then_inc(o_ready, 1)

                turn_keys(0)
                with act.Fori(0, DEC_BATCH // 2 - 1) as i:
                    attend(i)
                attend(DEC_BATCH // 2 - 1, False)

            @block.vector
            def _(dve):
                def queries_and_keys(i):
                    for s in range(2):
                        dve.wait_ge(scores_done, after(i * 2 + s))
                        for m in range(2):
                            rows = slice(m * DIFF_HD, (m + 1) * DIFF_HD)
                            dve.tensor_scalar(q_blocks[rows, s, :, m * DEC_SEQ:(m + 1) * DEC_SEQ],
                                              Z[rows, DQ:DQ + FT, ds(i * 8 + SEQ + s * DEC_SEQ, DEC_SEQ)],
                                              DIFF_HD ** -0.5, None, ALU.mult).then_inc(q_ready, 1)
                        for j in (1, 3):
                            dve.wait_ge(k_turned, after(i * 8 + s * 4 + j + 1))
                            dve.tensor_copy(KTT[:, s, 2 * j:2 * j + 2, :], PS[:, j, :].rearrange("p (f t) -> p f t", f=2)).then_inc(kT_dve, 1)

                def attend(i, more=True):
                    dve.wait_ge(scores_done, after(i * 2 + 2))
                    dve.wait_ge(exps, after(i))
                    dve.tensor_tensor(S[:, 0:PAST], PS[:, 4, 0:PAST], bias_new[:], ALU.add).then_inc(biased, 1)
                    dve.tensor_tensor(S[:, PAST:PAST + NEW], PS[:, 4, PAST:PAST + NEW], bias_own[:, i, :], ALU.add).then_inc(biased, 1)
                    dve.wait_ge(biased, after(i * 2 + 2))
                    dve.tensor_reduce(mx[:], S[:], AX.X, ALU.max).then_inc(soft, 1)
                    dve.wait_ge(soft, after(i * 4 + 1))
                    dve.tensor_scalar(nmx[:], mx[:], -1.0, None, ALU.mult).then_inc(soft, 1)
                    dve.wait_ge(exps, after(i + 1))
                    dve.reciprocal(rec[:], sums[:]).then_inc(soft, 1)
                    dve.wait_ge(soft, after(i * 4 + 3))
                    dve.wait_ge(probs, after(i))
                    dve.tensor_tensor(coef[:], rec[:], row_weights[:], ALU.mult).then_inc(soft, 1)
                    dve.wait_ge(soft, after(i * 4 + 4))
                    dve.wait_ge(p_turned, after(i))
                    dve.tensor_scalar(PN[:], E[:], coef[:], None, ALU.mult).then_inc(probs, 1)
                    if more:
                        queries_and_keys(i + 1)
                    dve.wait_ge(p_turned, after(i + 1))
                    dve.wait_ge(o_done, after(i))
                    turned = PS[:, 5, 0:2 * P].rearrange("p (g x m s) -> p g x m s", g=2, m=2, s=DEC_SEQ)
                    at = AT[:].rearrange("p g (x s) -> p g x s", s=DEC_SEQ)
                    dve.tensor_copy(at, turned[:, :, :, 0, :]).then_inc(aT_ready, 1)
                    dve.wait_ge(aT_ready, after(i * 4 + 1))
                    dve.tensor_tensor(at, at, turned[:, :, :, 1, :], ALU.add).then_inc(aT_ready, 1)
                    turned = PS[0:NEW, 5, 2 * P:3 * P].rearrange("p (x m s) -> p x m s", m=2, s=DEC_SEQ)
                    at = ATN[:].rearrange("p (x s) -> p x s", s=DEC_SEQ)
                    dve.tensor_copy(at, turned[:, :, 0, :]).then_inc(aT_ready, 1)
                    dve.wait_ge(aT_ready, after(i * 4 + 3))
                    dve.tensor_tensor(at, at, turned[:, :, 1, :], ALU.add).then_inc(aT_ready, 1)

                dve.memset(QB[:], 0.0).then_inc(zeroed, 1)
                dve.wait_ge(zeroed, after(1))
                queries_and_keys(0)
                with dve.Fori(0, DEC_BATCH // 2 - 1) as i:
                    attend(i)
                attend(DEC_BATCH // 2 - 1, False)

            @block.tensor
            def _(pe):
                def scores(i):
                    for s in range(2):
                        pe.wait_ge(k_loaded[s], after(i * 32 + 32))
                        for j in range(4):
                            if j % 2 == 0:
                                pe.wait_ge(kT_act, after(i * 4 + 2 * s + j // 2 - 1))
                            else:
                                pe.wait_ge(kT_dve, after(i * 4 + 2 * s + j // 2 - 1))
                            for f in range(2):
                                for g in range(N_PAGES):
                                    ft = 2 * j + f
                                    last = pe.transpose(PS[:, j, f * PAST + g * P:f * PAST + (g + 1) * P],
                                                        KP[:, s, g, ft * P:(ft + 1) * P], ident[:])
                            last.then_inc(k_turned, 1)
                        pe.wait_ge(q_ready, after(i * 4 + 2 * s + 2))
                        pe.wait_ge(kT_act, after(i * 4 + 2 * s + 2))
                        pe.wait_ge(kT_dve, after(i * 4 + 2 * s + 2))
                        pe.wait_ge(biased, after(i * 2))
                        rows = slice(s * ROWS, (s + 1) * ROWS)
                        for f in range(FT):
                            q = QB[:, s, f * ROWS:(f + 1) * ROWS]
                            pe.matmul(PS[rows, 4, 0:PAST], q, KTT[:, s, f, :], start=(f == 0), stop=(f == FT - 1), skip_group_check=True)
                            last = pe.matmul(PS[rows, 4, PAST:PAST + NEW], q, Z[:, DK + f, SEQ:T], start=False, stop=(f == FT - 1),
                                             skip_group_check=True)
                        last.then_inc(scores_done, 1)

                def attend(i):
                    pe.wait_ge(probs, after(i + 1))
                    pe.wait_ge(aT_ready, after(i * 4))
                    for g in range(2):
                        pe.transpose(PS[:, 5, g * P:(g + 1) * P], PN[:, g * P:(g + 1) * P], ident[:])
                    pe.transpose(PS[0:NEW, 5, 2 * P:3 * P], PN[:, PAST:PAST + NEW], ident[:]).then_inc(p_turned, 1)
                    pe.wait_ge(aT_ready, after(i * 4 + 4))
                    pe.wait_ge(o_ready, after(i))
                    for s in range(2):
                        pe.wait_ge(v_loaded[s], after(i * 32 + 32))
                        for h in range(FT):
                            c = slice(s * ROWS // 2 + h * DEC_SEQ, s * ROWS // 2 + (h + 1) * DEC_SEQ)
                            out = PS[:, 6, c]
                            for g in range(N_PAGES):
                                pe.matmul(out, VP[:, s, g, h * P:(h + 1) * P], AT[:, g, c], start=(s == 0 and h == 0 and g == 0),
                                          stop=False, skip_group_check=True)
                    for h in range(FT):
                        out = PS[:, 6, 0:ROWS].rearrange("p (b c) -> p b c", b=2)[:, :, h * DEC_SEQ:(h + 1) * DEC_SEQ]
                        new = ATN[:].rearrange("p (b c) -> p b c", b=2)[:, :, h * DEC_SEQ:(h + 1) * DEC_SEQ]
                        last = pe.matmul(out, v_new[:, h * P:(h + 1) * P], new, start=False, stop=True, skip_group_check=True)
                    last.then_inc(o_done, 1)

                scores(0)
                with pe.Fori(0, DEC_BATCH // 2 - 1) as i:
                    scores(i + 1)
                    attend(i)
                attend(DEC_BATCH // 2 - 1)


GROUP = 4
GROUPS = DEC_BATCH // GROUP


def mem_prompt(nc, G, Z, OM, K, V, sample_loaded):
    PS, ident, O, S_ = (G[k] for k in ("PS", "ident", "O", "S"))
    SCALE = MEM_HD ** -0.5
    with ExitStack() as ctx:
        st = Stage(nc, G, ctx, "mp")
        Q, KVT = st.sb("q_T", [P, SEQ]), st.sb("kv_T", [P, 2, 2, MEM_TOKENS])
        KV = st.sb("kv", [P, 2, 2, 2, P])
        E, PN, PT = st.sb("exps", [P, 2, MEM_TOKENS]), st.sb("probs", [P, 2, MEM_TOKENS]), st.sb("probs_T", [P, 2, SEQ])
        mx, nmx, sums, rec = (st.sb(w, [P, 2]) for w in ("max", "neg_max", "sums", "reciprocals"))
        (staged, turned, kv_ready, scores_done, soft, exps, probs, p_turned, pT_ready, o_done, o_ready) = st.sems(
            "staged", "turned", "kv_ready", "scores_done", "soft", "exps", "probs", "p_turned", "pT_ready", "o_done",
            "o_ready")
        kv_stored = st.sems("kv_stored0", "kv_stored1")
        loaded = st.sems("loaded0", "loaded1")
        k_in, v_in = (G["A"][n][0].rearrange("(i b) (t p) h d -> i b p t (h d)", b=GROUP, p=P) for n in ("cache_mem_k", "cache_mem_v"))
        kv_dram = S_["mem_T"].rearrange("(c h) p t -> h p c t", c=2)
        outs = [O[n][0, 0].rearrange("(t p) h d -> h p t d", p=P) for n in ("mem_k_prompt", "mem_v_prompt")]
        with nc.Block() as block:
            @block.sync
            def _(sp):
                for b in range(2):
                    sp.dma_start(KVT[:, b, :, :], kv_dram[b]).then_inc(loaded[b], 16)

                def store(h, b):
                    sp.wait_ge(kv_ready, after(h + 1))
                    for c in range(2):
                        sp.dma_start(outs[c][h], KV[:, b, c, :, :]).then_inc(kv_stored[b], 16)

                with sp.Fori(0, MEM_HEADS // 2 - 1) as i:
                    for b in range(2):
                        sp.wait_ge(scores_done, after(i * 2 + b + 1))
                        sp.wait_ge(turned, after(i * 2 + b + 1))
                        sp.dma_start(KVT[:, b, :, :], kv_dram[i * 2 + b + 2]).then_inc(loaded[b], 16)
                        store(i * 2 + b, b)
                for b in range(2):
                    store(MEM_HEADS - 2 + b, b)
                for b in range(2):
                    sp.wait_ge(kv_stored[b], after(32 * MEM_HEADS // 2))

            @block.scalar
            def _(act):
                for b in range(2):
                    act.wait_ge(loaded[b], after(16))
                for i in range(GROUPS):
                    for w, (buffer, source) in enumerate(((K, k_in), (V, v_in))):
                        for b in range(GROUP):
                            act.dma_start(buffer[:, i, b, :, :], source[i, b]).then_inc(sample_loaded[2 * i + w], 16)
                with act.Fori(0, MEM_HEADS // 2) as i:
                    for b in range(2):
                        h = i * 2 + b
                        act.wait_ge(scores_done, after(h))
                        act.activation(Q[:], Z[:, h + MQ, 0:SEQ], ACT.Copy).then_inc(staged, 1)
                        act.wait_ge(turned, after(h + 1))
                        act.wait_ge(kv_stored[b], after(i * 32))
                        act.wait_ge(o_done, after(h - 1))
                        act.activation(KV[:, b, :, :, :], PS[:, 0, :].rearrange("p (c t d) -> p c t d", c=2, t=2), ACT.Copy).then_inc(kv_ready, 1)
                        act.wait_ge(soft, after(h * 3 + 2))
                        act.wait_ge(probs, after(h))
                        for q in range(2):
                            act.activation(E[:, q, :], PS[:, 1, q * MEM_TOKENS:(q + 1) * MEM_TOKENS], ACT.Exp, bias=nmx[:, q:q + 1],
                                           scale=SCALE, accum_out=sums[:, q:q + 1]).then_inc(exps, 1)
                        act.wait_ge(p_turned, after(h + 1))
                        act.activation(PT[:], PS[:, 2, :].rearrange("p (k q) -> p k q", k=2), ACT.Copy).then_inc(pT_ready, 1)
                        act.wait_ge(o_done, after(h + 1))
                        act.activation(OM[:, h, 0:SEQ], PS[:, 3, 0:SEQ], ACT.Copy).then_inc(o_ready, 1)

            @block.vector
            def _(dve):
                with dve.Fori(0, MEM_HEADS) as h:
                    dve.wait_ge(scores_done, after(h + 1))
                    dve.wait_ge(soft, after(h * 3))
                    dve.tensor_reduce(mx[:], PS[:, 1, :].rearrange("p (q k) -> p q k", q=2), AX.X, ALU.max).then_inc(soft, 1)
                    dve.wait_ge(soft, after(h * 3 + 1))
                    dve.wait_ge(exps, after(h * 2))
                    dve.tensor_scalar(nmx[:], mx[:], -SCALE, None, ALU.mult).then_inc(soft, 1)
                    dve.wait_ge(exps, after(h * 2 + 2))
                    dve.wait_ge(probs, after(h))
                    dve.reciprocal(rec[:], sums[:]).then_inc(soft, 1)
                    dve.wait_ge(soft, after(h * 3 + 3))
                    dve.wait_ge(p_turned, after(h))
                    dve.tensor_tensor(PN[:], E[:], rec[:].unsqueeze(2).to_broadcast([P, 2, MEM_TOKENS]), ALU.mult).then_inc(probs, 1)

            @block.tensor
            def _(pe):
                with pe.Fori(0, MEM_HEADS // 2) as i:
                    for b in range(2):
                        h = i * 2 + b
                        pe.wait_ge(loaded[b], after(i * 16 + 16))
                        pe.wait_ge(kv_ready, after(h))
                        for c in range(2):
                            for t in range(2):
                                last = pe.transpose(PS[:, 0, (2 * c + t) * P:(2 * c + t + 1) * P], KVT[:, b, c, t * P:(t + 1) * P], ident[:])
                        last.then_inc(turned, 1)
                        pe.wait_ge(staged, after(h + 1))
                        pe.wait_ge(exps, after(h * 2))
                        for q in range(2):
                            last = pe.matmul(PS[:, 1, q * MEM_TOKENS:(q + 1) * MEM_TOKENS], Q[:, q * P:(q + 1) * P], KVT[:, b, 0, :], start=True, stop=True)
                        last.then_inc(scores_done, 1)
                        pe.wait_ge(probs, after(h + 1))
                        pe.wait_ge(pT_ready, after(h))
                        for k in range(2):
                            for q in range(2):
                                last = pe.transpose(PS[:, 2, k * SEQ + q * P:k * SEQ + (q + 1) * P], PN[:, q, k * P:(k + 1) * P], ident[:])
                        last.then_inc(p_turned, 1)
                        pe.wait_ge(pT_ready, after(h + 1))
                        pe.wait_ge(kv_ready, after(h + 1))
                        pe.wait_ge(o_ready, after(h))
                        for k in range(2):
                            last = pe.matmul(PS[:, 3, 0:SEQ], KV[:, b, 1, k, :], PT[:, k, :], start=(k == 0), stop=(k == 1))
                        last.then_inc(o_done, 1)


def mem_sample(nc, G, Z, OM, K, V, loaded):
    PS, ident, A = (G[k] for k in ("PS", "ident", "A"))
    SCALE = MEM_HD ** -0.5
    ROWS, FT = 32, MEM_HEADS
    with ExitStack() as ctx:
        st = Stage(nc, G, ctx, "msm")
        KTT = st.sb("k_T", [P, 2, FT, MEM_TOKENS])
        QB = st.sb("q_blocks", [P, 2, FT * (ROWS + DEC_SEQ)])
        E, PN, PT = st.sb("exps", [P, MEM_TOKENS]), st.sb("probs", [P, MEM_TOKENS]), st.sb("probs_T", [P, 2, P])
        mx, nmx, sums, rec = (st.sb(w, [P, 1]) for w in ("max", "neg_max", "sums", "reciprocal"))
        (zeroed, k_turned, kT_ready, q_ready, scores_done, soft, exps, probs, p_turned, pT_ready, o_done, o_ready) = st.sems(
            "zeroed", "k_turned", "kT_ready", "q_ready", "scores_done", "soft", "exps", "probs", "p_turned", "pT_ready",
            "o_done", "o_ready")
        q_blocks = QB[:].rearrange("p b (f c) -> p b f c", f=FT)
        with nc.Block() as block:
            @block.scalar
            def _(act):
                def turn_keys(i):
                    for b in range(GROUP):
                        act.wait_ge(k_turned, after(i * 4 + b + 1))
                        act.activation(KTT[:, b % 2, :, :].rearrange("p (j f) t -> p j f t", j=2),
                                       PS[:, 2 * (b % 2):2 * (b % 2) + 2, :].rearrange("p j (f t) -> p j f t", f=2), ACT.Copy).then_inc(kT_ready, 1)

                def attend(i):
                    act.wait_ge(soft, after(i * 3 + 2))
                    act.wait_ge(probs, after(i))
                    act.activation(E[:], PS[:, 4, 0:MEM_TOKENS], ACT.Exp, bias=nmx[:], scale=SCALE, accum_out=sums[:]).then_inc(exps, 1)
                    if i + 1 < GROUPS:
                        turn_keys(i + 1)
                    act.wait_ge(p_turned, after(i + 1))
                    act.activation(PT[:], PS[:, 5, 0:2 * P].rearrange("p (k r) -> p k r", k=2), ACT.Copy).then_inc(pT_ready, 1)
                    act.wait_ge(o_done, after(i + 1))
                    act.activation(OM[:, 0:FT, ds(i * 16 + SEQ, 16)].rearrange("p h (b s) -> p h b s", b=GROUP),
                                   PS[:, 6, 0:64].rearrange("p (b h s) -> p h b s", b=GROUP, s=DEC_SEQ), ACT.Copy).then_inc(o_ready, 1)

                turn_keys(0)
                for i in range(GROUPS):
                    attend(i)

            @block.vector
            def _(dve):
                dve.memset(QB[:], 0.0).then_inc(zeroed, 1)
                dve.wait_ge(zeroed, after(1))

                def queries(i):
                    for b in range(GROUP):
                        n = i * 4 + b
                        if b >= 2:
                            dve.wait_ge(scores_done, after(n - 1))
                        else:
                            dve.wait_ge(scores_done, after(i * 4))
                        dve.tensor_copy(q_blocks[:, b % 2, :, 0:DEC_SEQ],
                                        Z[:, MQ:MQ + FT, ds(i * 16 + SEQ + b * DEC_SEQ, DEC_SEQ)]).then_inc(q_ready, 1)

                queries(0)
                for i in range(GROUPS):
                    dve.wait_ge(scores_done, after(i * 4 + 4))
                    dve.wait_ge(soft, after(i * 3))
                    dve.tensor_reduce(mx[:], PS[:, 4, 0:MEM_TOKENS], AX.X, ALU.max).then_inc(soft, 1)
                    dve.wait_ge(soft, after(i * 3 + 1))
                    dve.wait_ge(exps, after(i))
                    dve.tensor_scalar(nmx[:], mx[:], -SCALE, None, ALU.mult).then_inc(soft, 1)
                    if i + 1 < GROUPS:
                        queries(i + 1)
                    dve.wait_ge(exps, after(i + 1))
                    dve.wait_ge(probs, after(i))
                    dve.reciprocal(rec[:], sums[:]).then_inc(soft, 1)
                    dve.wait_ge(soft, after(i * 3 + 3))
                    dve.wait_ge(p_turned, after(i))
                    dve.tensor_scalar(PN[:], E[:], rec[:], None, ALU.mult).then_inc(probs, 1)

            @block.tensor
            def _(pe):
                def scores(i):
                    pe.wait_ge(loaded[2 * i], after(16 * GROUP))
                    for b in range(GROUP):
                        if b >= 2:
                            pe.wait_ge(kT_ready, after(i * 4 + b - 1))
                        for f in range(FT):
                            for k in range(2):
                                last = pe.transpose(PS[:, 2 * (b % 2) + f // 2, (f % 2) * MEM_TOKENS + k * P:(f % 2) * MEM_TOKENS + (k + 1) * P],
                                                    K[:, i, b, k, f * P:(f + 1) * P], ident[:])
                        last.then_inc(k_turned, 1)
                        pe.wait_ge(kT_ready, after(i * 4 + b + 1))
                        pe.wait_ge(q_ready, after(i * 4 + b + 1))
                        if b == 0:
                            pe.wait_ge(exps, after(i))
                        for f in range(FT):
                            last = pe.matmul(PS[b * ROWS:(b + 1) * ROWS, 4, 0:MEM_TOKENS], QB[:, b % 2, f * ROWS:(f + 1) * ROWS],
                                             KTT[:, b % 2, f, :], start=(f == 0), stop=(f == FT - 1))
                        last.then_inc(scores_done, 1)

                def attend(i):
                    pe.wait_ge(probs, after(i + 1))
                    pe.wait_ge(pT_ready, after(i))
                    for k in range(2):
                        last = pe.transpose(PS[:, 5, k * P:(k + 1) * P], PN[:, k * P:(k + 1) * P], ident[:])
                    last.then_inc(p_turned, 1)
                    pe.wait_ge(pT_ready, after(i + 1))
                    pe.wait_ge(o_ready, after(i))
                    pe.wait_ge(loaded[2 * i + 1], after(16 * GROUP))
                    for b in range(GROUP):
                        for h in range(FT):
                            for k in range(2):
                                last = pe.matmul(PS[:, 6, (b * FT + h) * DEC_SEQ:(b * FT + h + 1) * DEC_SEQ], V[:, i, b, k, h * P:(h + 1) * P],
                                                 PT[:, k, b * ROWS + h * DEC_SEQ:b * ROWS + (h + 1) * DEC_SEQ],
                                                 start=(b == 0 and h == 0 and k == 0), stop=True, skip_group_check=True)
                    last.then_inc(o_done, 1)

                scores(0)
                for i in range(GROUPS):
                    if i + 1 < GROUPS:
                        scores(i + 1)
                    attend(i)


def diff_norm(nc, G, OD):
    PS, ones, A = (G[k] for k in ("PS", "ones", "A"))
    with ExitStack() as ctx:
        st = Stage(nc, G, ctx, "dn")
        w, ws = st.sb("subln", [P, 1]), st.sb("subln_scaled", [P, 1])
        sq, ms, logs, rstd, t1, t2, rstd2 = (st.sb(x, [P, 2, 4, T]) for x in ("squares", "ms", "logs", "rstd", "t1", "t2", "rstd2"))
        loaded, scaled, squared, summed = st.sems("loaded", "scaled", "squared", "summed")
        steps = st.sems("rstd_steps0", "rstd_steps1")
        heads = [OD[:, 4 * g:4 * g + 4, :] for g in range(2)]
        with nc.Block() as block:
            @block.sync
            def _(sp):
                with nc.allow_non_contiguous_dma(reason="one weight per partition"):
                    sp.dma_start(w[:], A["diff_subln_w"][0].rearrange("(p o) -> p o", o=1)).then_inc(loaded, 16)

            @block.scalar
            def _(act):
                for g in range(2):
                    act.activation(sq[:, g], heads[g], ACT.Square).then_inc(squared, 1)
                for g in range(2):
                    act.wait_ge(steps[g], after(1))
                    act.activation(logs[:, g], ms[:, g], ACT.Ln).then_inc(steps[g], 1)
                for g in range(2):
                    act.wait_ge(steps[g], after(2))
                    act.activation(rstd[:, g], logs[:, g], ACT.Exp, scale=-0.5).then_inc(steps[g], 1)

            @block.tensor
            def _(pe):
                for g in range(2):
                    pe.wait_ge(squared, after(g + 1))
                    for j in range(4):
                        last = pe.matmul(PS[:, 4 * g + j, 0:T], ones[:], sq[:, g, j, :], start=True, stop=True)
                    last.then_inc(summed, 1)

            @block.vector
            def _(dve):
                dve.wait_ge(loaded, after(16))
                dve.tensor_scalar(ws[:], w[:], 1.0 - LAMBDA_INIT, None, ALU.mult).then_inc(scaled, 1)
                dve.wait_ge(scaled, after(1))
                for g in range(2):
                    dve.wait_ge(summed, after(g + 1))
                    dve.tensor_scalar(ms[:, g], PS[:, 4 * g:4 * g + 4, 0:T], EPS, None, ALU.add).then_inc(steps[g], 1)
                for g in range(2):
                    refine_rstd(dve, ms[:, g], rstd[:, g], t1[:, g], t2[:, g], rstd2[:, g], steps[g], 3)
                    dve.wait_ge(steps[g], after(6))
                    dve.scalar_tensor_tensor(out=heads[g], in0=heads[g], scalar=ws[:], in1=rstd2[:, g], op0=ALU.mult, op1=ALU.mult)


def attention(nc, G, Z, ODM):
    OD, OM = ODM[:, 0:DIFF_HEADS, :], ODM[:, DIFF_HEADS:, :]
    retention(nc, G, Z)
    with ExitStack() as ctx:
        st = Stage(nc, G, ctx, "diff")
        v_new = st.sb("v_new", [NEW, DIFF_HEADS * P])
        bias, bias_new, bias_own, map_weights, row_weights = diff_tables(nc, G, st)
        diff_prompt(nc, G, Z, OD, v_new, bias, map_weights)
        diff_sample(nc, G, Z, OD, v_new, bias_new, bias_own, row_weights)
    with ExitStack() as ctx:
        st = Stage(nc, G, ctx, "memory_cache")
        K, V = (st.sb(w, [P, GROUPS, GROUP, 2, MEM_HEADS * P]) for w in ("k", "v"))
        loaded = st.sems(*(f"{w}_loaded{i}" for i in range(GROUPS) for w in "kv"))
        mem_prompt(nc, G, Z, OM, K, V, loaded)
        mem_sample(nc, G, Z, OM, K, V, loaded)
    diff_norm(nc, G, OD)


def split_branch_outputs(nc, G, Z, ODM, OTH, OTL):
    with ExitStack() as ctx:
        (high,) = Stage(nc, G, ctx, "so").sems("high")
        parts = [(4 * q, Z[:, RG + 4 * q:RG + 4 * q + 4, :]) for q in range(4)] + [
            (O_DIFF + 4 * q, ODM[:, 4 * q:4 * q + 4, :]) for q in range(3)]
        with nc.Block() as block:
            @block.scalar
            def _(act):
                for o, src in parts:
                    act.activation(OTH[:, o:o + 4, :], src, ACT.Copy).then_inc(high, 1)

            def low(engine, mine):
                for n, (o, src) in enumerate(parts):
                    if n in mine:
                        engine.wait_ge(high, after(n + 1))
                        engine.tensor_tensor(OTL[:, o:o + 4, :], src, OTH[:, o:o + 4, :], ALU.subtract)

            @block.vector
            def _(dve):
                low(dve, (1, 3, 4, 5, 6))

            @block.gpsimd
            def _(pool):
                low(pool, (0, 2))


def up_projections(nc, G, OTH, OTL, MH, ML, w, following):
    A, S, PS = G["A"], G["S"], G["PS"]
    with ExitStack() as ctx:
        st = Stage(nc, G, ctx, "up")
        gates = st.sb("gates", [P, 3, 2, T])
        mix = st.sb("mix", [P, 2, T])
        t1, t2, t3, t4 = (st.sb(x, [P, T]) for x in ("diff_part", "mem_part", "sum", "total"))
        gates_loaded, sigmoids, mixed = st.sems("gates_loaded", "sigmoids", "mixed")
        ret, diff, mem = (A[n][0].rearrange("(k p) n -> p k n", p=P) for n in ("w_up_ret", "w_up_diff", "w_up_mem"))
        gates_dram = S["gates_T"].rearrange("(g i f) p t -> g i p f t", g=3, f=2)
        STEPS = KT // 2
        o = (OTH, OTL)

        def branch(a, n):
            return tuple(x[:, a:a + n, :] for x in o)

        with nc.Block() as block:
            @block.sync
            def _(sp):
                def step(i, first):
                    cols = ds(i * 2 * P, 2 * P)
                    w.load(sp, i, 0, [ret[:, :, cols]], first)
                    w.load(sp, i, 1, [diff[:, :, cols], mem[:, :, cols]], first)
                    sp.wait_ge(mixed, after(i * 14))
                    for g in range(3):
                        sp.dma_start(gates[:, g, :, :], gates_dram[g, i]).then_inc(gates_loaded, 16)
                step(0, True)
                with sp.Fori(1, STEPS) as i:
                    step(i, False)
                wout = A["w_out"][0].rearrange("(k p) n -> p k n", p=P)
                following.load_ahead(sp, lambda b: [wout[:, :, b * 2 * P:(b + 1) * 2 * P]], w, 4 * STEPS)

            @block.scalar
            def _(act):
                with act.Fori(0, STEPS) as i:
                    for u in range(4):
                        w.split_high(act, i, u, KT if u < 2 else 12)
                        if u == 1:
                            act.wait_ge(gates_loaded, after(i * 48 + 48))
                            act.activation(gates[:], gates[:], ACT.Sigmoid).then_inc(sigmoids, 1)

            @block.vector
            def _(dve):
                def mix_in(i, u):
                    f = u % 2
                    n = i * 14 + (u if u < 2 else 2 + 6 * (u - 2))
                    if u < 2:
                        if u == 0:
                            dve.wait_ge(sigmoids, after(i + 1))
                        dve.wait_ge(mixed, after(n))
                        dve.tensor_tensor(mix[:, f, :], PS[:, f, 0:T], gates[:, 0, f, :], ALU.mult).then_inc(mixed, 1)
                        dve.wait_ge(mixed, after(n + 1))
                        dve.sem_inc(w.bank_free, 1)
                    else:
                        dve.wait_ge(mixed, after(n))
                        dve.tensor_tensor(t1[:], PS[:, 2 + f, 0:T], gates[:, 1, f, :], ALU.mult).then_inc(mixed, 1)
                        dve.tensor_tensor(t2[:], PS[:, 4 + f, 0:T], gates[:, 2, f, :], ALU.mult).then_inc(mixed, 1)
                        dve.wait_ge(mixed, after(n + 2))
                        dve.sem_inc(w.bank_free, 1)
                        dve.tensor_tensor(t3[:], mix[:, f, :], t1[:], ALU.add).then_inc(mixed, 1)
                        dve.wait_ge(mixed, after(n + 3))
                        dve.tensor_tensor(t4[:], t3[:], t2[:], ALU.add).then_inc(mixed, 1)
                        dve.wait_ge(mixed, after(n + 4))
                        dve.tensor_copy(MH[:, i * 2 + f, :], t4[:]).then_inc(mixed, 1)
                        dve.wait_ge(mixed, after(n + 5))
                        dve.tensor_tensor(ML[:, i * 2 + f, :], t4[:], MH[:, i * 2 + f, :], ALU.subtract).then_inc(mixed, 1)

                kts = [KT, KT, 12, 12]
                w.split_low(dve, 0, 0, KT)
                with dve.Fori(0, STEPS - 1) as i:
                    w.follow(dve, i, mix_in, kts=kts)
                w.follow(dve, STEPS - 1, mix_in, last=True, kts=kts)

            @block.tensor
            def _(pe):
                w.open(pe)
                with pe.Fori(0, STEPS) as i:
                    for u in range(2):
                        w.product(pe, i, u, [(PS[:, u, 0:T], 0, branch(O_RET, KT))])
                    for u in (2, 3):
                        w.product(pe, i, u, [(PS[:, u, 0:T], 0, branch(O_DIFF, DIFF_HEADS)),
                                             (PS[:, 2 + u, 0:T], DIFF_HEADS, branch(O_MEM, MEM_HEADS))])


def output_projection(nc, G, MH, ML, hT, w, following):
    A, S, PS = G["A"], G["S"], G["PS"]
    with ExitStack() as ctx:
        (x_loaded,) = Stage(nc, G, ctx, "out").sems("x_loaded")
        wout = A["w_out"][0].rearrange("(k p) n -> p k n", p=P)
        with nc.Block() as block:
            @block.sync
            def _(sp):
                sp.dma_start(hT[:], S["x_T"].rearrange("k p t -> p k t")).then_inc(x_loaded, 16)
                with sp.Fori(1, KT // 4) as i:
                    for b in range(2):
                        w.load(sp, i, b, [wout[:, :, ds(i * 512 + b * 2 * P, 2 * P)]])
                wq = A["peer_w_q"][0].rearrange("(k p) n -> p k n", p=P)
                following.load_ahead(sp, lambda b: [wq[:, :, b * 2 * P:(b + 1) * 2 * P]], w, KT)

            @block.scalar
            def _(act):
                with act.Fori(0, KT // 4) as i:
                    for u in range(4):
                        w.split_high(act, i, u)

            @block.vector
            def _(dve):
                def add(i, u):
                    dve.tensor_tensor(hT[:, i * 4 + u, :], PS[:, u % 2, 0:T], hT[:, i * 4 + u, :], ALU.add).then_inc(w.bank_free, 1)

                w.split_low(dve, 0, 0)
                dve.wait_ge(x_loaded, after(16))
                with dve.Fori(0, KT // 4 - 1) as i:
                    w.follow(dve, i, add)
                w.follow(dve, KT // 4 - 1, add, last=True)

            @block.tensor
            def _(pe):
                w.open(pe)
                with pe.Fori(0, KT // 4) as i:
                    for u in range(4):
                        w.product(pe, i, u, [(PS[:, u % 2, 0:T], 0, (MH, ML))])


TPAD = 3 * P


def peer_queries(nc, G, XH, XL, QT, w):
    A, PS = G["A"], G["PS"]
    with ExitStack() as ctx:
        wq = A["peer_w_q"][0].rearrange("(k p) n -> p k n", p=P)
        with nc.Block() as block:
            @block.sync
            def _(sp):
                with sp.Fori(1, KT // 4) as i:
                    for b in range(2):
                        w.load(sp, i, b, [wq[:, :, ds(i * 512 + b * 2 * P, 2 * P)]])

            @block.gpsimd
            def _(pool):
                pool.memset(QT[:, :, T:TPAD], 0.0)

            @block.scalar
            def _(act):
                with act.Fori(0, KT // 4) as i:
                    for u in range(4):
                        w.split_high(act, i, u)

            @block.vector
            def _(dve):
                def keep(i, u):
                    dve.tensor_copy(QT[:, i * 4 + u, 0:T], PS[:, u % 2, 0:T]).then_inc(w.bank_free, 1)

                w.split_low(dve, 0, 0)
                with dve.Fori(0, KT // 4 - 1) as i:
                    w.follow(dve, i, keep)
                w.follow(dve, KT // 4 - 1, keep, last=True)

            @block.tensor
            def _(pe):
                w.open(pe)
                with pe.Fori(0, KT // 4) as i:
                    for u in range(4):
                        w.product(pe, i, u, [(PS[:, u % 2, 0:T], 0, (XH, XL))])


LOWEST = -3.0e38
TOKEN_BLOCKS = 4
TB = T // TOKEN_BLOCKS

TILE_STEPS = (4, 4, 4)
SELECTION_STEPS = sum(TILE_STEPS)
HEAD = SELECTION_STEPS + 3 * TOKEN_BLOCKS
GROUPS_A_STEP = TB // 3 // 4


def top16(dve, values, best, index, found, n, base):
    for g in range(n):
        dve.max(best[:, g, 0:8], values[:, g, :]).then_inc(found, 1)
    for g in range(n):
        dve.wait_ge(found, after(base + g + 1))
        dve.max_index(index[:, g, 0:8], best[:, g, 0:8], values[:, g, :]).then_inc(found, 1)
    for g in range(n):
        dve.wait_ge(found, after(base + n + g + 1))
        dve.match_replace(values[:, g, :], best[:, g, 0:8], values[:, g, :], LOWEST).then_inc(found, 1)
    for g in range(n):
        dve.wait_ge(found, after(base + 2 * n + g + 1))
        dve.max(best[:, g, 8:16], values[:, g, :]).then_inc(found, 1)
    for g in range(n):
        dve.wait_ge(found, after(base + 3 * n + g + 1))
        dve.max_index(index[:, g, 8:16], best[:, g, 8:16], values[:, g, :]).then_inc(found, 1)


def peer_selection(nc, G, area, QT, XH, XL):
    A, PS, ident, C, S = (G[k] for k in ("A", "PS", "ident", "C", "S"))
    GR = 2 * PEER_HEADS
    PICKS = PEER_HEADS * TOPK
    with ExitStack() as ctx:
        st = Stage(nc, G, ctx, "sel")

        def view(first, shape, pattern, **sizes):
            return area[:, first:first + shape[0] * shape[1]].rearrange(pattern, **sizes)

        tile = GR * P
        SC = view(0, (GR, NKEYS), "p (g n) -> p g n", g=GR)
        CA = view(tile, (PEER_HEADS, TOPK * TOPK), "p (h n) -> p h n", h=PEER_HEADS)
        EQ = view(2 * tile, (PICKS, TOPK), "p (k a) -> p k a", a=TOPK)
        MU = view(3 * tile, (PICKS, TOPK), "p (k a) -> p k a", a=TOPK)
        keys = view(4 * tile, (GR, P), "p (g n) -> p g n", g=GR)
        Q = view(5 * tile + GR * TPAD, (GR, P), "p (g n) -> p g n", g=GR)
        shared = st.sb("keys_T_and_hot_rows", [P, GR * P])
        KYT = shared[:].rearrange("p (g n) -> p g n", g=GR)
        SECOND, FIRST = (shared[:, k * 8 * P:(k + 1) * 8 * P].rearrange("p (b j n) -> p b j n", b=2, j=4) for k in range(2))
        W = area[:, 0:2 * NKEYS * TB].rearrange("p (b i t) -> p b i t", b=2, t=TB)
        V, IX, IXF = st.sb("best", [P, GR, TOPK]), st.sb("best_index", [P, GR, TOPK], U32), st.sb("best_index_f", [P, GR, TOPK])
        TS, J = st.sb("top", [P, PEER_HEADS, TOPK]), st.sb("top_index", [P, PEER_HEADS, TOPK], U32)
        JJ = st.sb("top_parts", [P, 2, PICKS], U32)
        JF = st.sb("top_parts_f", [P, 2, PICKS])
        D, E = st.sb("below_top", [P, PEER_HEADS, TOPK]), st.sb("exps", [P, PEER_HEADS, TOPK])
        sums, rec = st.sb("sums", [P, PEER_HEADS]), st.sb("reciprocals", [P, PEER_HEADS])
        PK = st.sb("picks", [P, 3, PICKS])
        SEL = st.sb("picks_T", [P, 3, TPAD])
        iota = st.sb("iota", [P, P])
        U = st.sb("u", [P, 2, D_MODEL])
        UT = st.sb("uT", [P, KT, P])
        UH, UL = st.sb("uT_high", [P, 2, KT, P], F32R), st.sb("uT_low", [P, 2, KT, P], F32R)
        GE = st.sb("gelu", [P, 2, T])
        (loaded, key_turned, keys_ready, staged, scored, scores_ready, found1, paired, found2, steps, exped, picks_ready,
         picks_turned, sel_ready, second_ready, first_ready, placed, w_ready) = st.sems(
            "loaded", "key_turned", "keys_ready", "staged", "scored", "scores_ready", "found1", "paired", "found2", "steps",
            "exped", "picks_ready", "picks_turned", "sel_ready", "second_ready", "first_ready", "placed", "weights_ready")
        turned, uT_ready, uT_high, uT_low, hidden_done, gelu_ready = st.sems(
            "turned", "uT_ready", "uT_high", "uT_low", "hidden_done", "gelu_ready")
        w_stored, u_loaded, ge_stored = (st.sems(f"{w}0", f"{w}1") for w in ("w_stored", "u_loaded", "gelu_stored"))
        N1, N2, NS_ = 5 * GR, 5 * PEER_HEADS, 14
        u_in = A["peer_u"][0].rearrange("(s c p) d -> s c p d", c=2, p=P)

        def run(engine, first, count, step):
            n = count - (first + count == HEAD)
            if n:
                with engine.Fori(first, first + n) as s_:
                    step(s_, True)
            if n < count:
                step(HEAD - 1, False)

        with nc.Block() as block:
            @block.sync
            def _(sp):
                sp.dma_start(keys[:], A["peer_keys"][0].rearrange("h c n d -> n (h c) d")).then_inc(loaded, 16)
                sp.dma_start(iota[:], C["iota"]).then_inc(loaded, 16)
                for c in range(2):
                    sp.dma_start(U[:, c, :], u_in[0, c]).then_inc(u_loaded[c], 16)
                sp.wait_ge(turned, after(4))
                sp.dma_start(U[:, 0, :], u_in[1, 0]).then_inc(u_loaded[0], 16)

                def step(s_, more):
                    for c in range(2):
                        if more:
                            sp.wait_ge(turned, after(s_ * 8 + 4 * c + 8))
                            sp.dma_start(U[:, 1 - c, :], u_in[s_ + 1 + c, 1 - c]).then_inc(u_loaded[1 - c], 16)
                        sp.wait_ge(gelu_ready, after(s_ * 2 + c + 1))
                        sp.dma_start(S["gelu"][s_ * 2 + c], GE[:, c, :]).then_inc(ge_stored[c], 16)

                run(sp, 0, SELECTION_STEPS, step)
                for k in range(TOKEN_BLOCKS):
                    run(sp, SELECTION_STEPS + 3 * k, 3, step)
                    sp.wait_ge(w_ready, after(TB // 4 * (k + 1)))
                    sp.dma_start(S["peer_weights"][k], W[:, k % 2, :, :]).then_inc(w_stored[k % 2], 16)
                for b in range(2):
                    sp.wait_ge(w_stored[b], after(16 * TOKEN_BLOCKS // 2))
                    sp.wait_ge(ge_stored[b], after(16 * HEAD))
                    sp.wait_ge(u_loaded[b], after(16 * HEAD + 16 * (b == 0)))

            @block.tensor
            def _(pe):
                def turn(s_, c):
                    pe.wait_ge(u_loaded[c], after(s_ * 16 + 16))
                    for b in range(4):
                        pe.wait_ge(uT_ready, after(s_ * 8 + 4 * c - 4 + b + 1))
                        pe.wait_ge(uT_high, after(s_ * 8 + 4 * c - 4 + b + 1))
                        for j in range(4):
                            k = 4 * b + j
                            last = pe.transpose(PS[:, b, j * P:(j + 1) * P], U[:, c, k * P:(k + 1) * P], ident[:])
                        last.then_inc(turned, 1)

                def hidden(s_, c):
                    out = PS[:, 4 + c, 0:T]
                    pe.wait_ge(gelu_ready, after(s_ * 2 + c - 1))
                    for k in range(KT):
                        if k % 4 == 0:
                            pe.wait_ge(uT_high, after(s_ * 8 + 4 * c + k // 4 + 1))
                        pe.matmul(out, UH[:, c, k, :], XH[:, k, :], start=(k == 0), stop=False)
                        pe.matmul(out, UH[:, c, k, :], XL[:, k, :], start=False, stop=False)
                    for k in range(KT):
                        if k % 4 == 0:
                            pe.wait_ge(uT_low, after(s_ * 8 + 4 * c + k // 4 + 1))
                        last = pe.matmul(out, UL[:, c, k, :], XH[:, k, :], start=False, stop=(k == KT - 1))
                    last.then_inc(hidden_done, 1)

                def turn_next(s_, c, more):
                    if c == 0:
                        turn(s_, 1)
                    elif more:
                        turn(s_ + 1, 0)

                def step(s_, more):
                    for c in range(2):
                        turn_next(s_, c, more)
                        hidden(s_, c)

                def scores(t, half):
                    pe.wait_ge(staged, after(t + 1))
                    pe.wait_ge(scores_ready, after(2 * t + half))
                    for g in range(GR // 2):
                        last = pe.matmul(PS[:, 6 + g // 4, (g % 4) * P:(g % 4 + 1) * P], Q[:, half * GR // 2 + g, :],
                                         KYT[:, half * GR // 2 + g, :], start=True, stop=True)
                    last.then_inc(scored, 1)

                def picks(t):
                    pe.wait_ge(picks_ready, after(t + 1))
                    pe.wait_ge(scores_ready, after(min(2 * t + 4, 6)))
                    for j in range(3):
                        last = pe.transpose(PS[:, 6, j * P:(j + 1) * P], PK[:, j, :], ident[:])
                    last.then_inc(picks_turned, 1)
                    pe.wait_ge(sel_ready, after(t + 1))

                pe.wait_ge(loaded, after(32))
                for b in range(4):
                    if b >= 2:
                        pe.wait_ge(keys_ready, after(b - 1))
                    for j in range(4):
                        last = pe.transpose(PS[:, 6 + b % 2, j * P:(j + 1) * P], keys[:, 4 * b + j, :], ident[:])
                    last.then_inc(key_turned, 1)
                pe.wait_ge(keys_ready, after(4))
                scores(0, 0)
                scores(0, 1)
                turn(0, 0)
                first = 0
                for t in range(3):
                    if t < 2:
                        run(pe, first, 2, step)
                        scores(t + 1, 0)
                        run(pe, first + 2, 1, step)
                        scores(t + 1, 1)
                        run(pe, first + 3, TILE_STEPS[t] - 3, step)
                    else:
                        run(pe, first, TILE_STEPS[t], step)
                    picks(t)
                    first += TILE_STEPS[t]

                def spread(s_, q):
                    n, b = (s_ - SELECTION_STEPS) * GROUPS_A_STEP + q, q % 2
                    pe.wait_ge(first_ready, after(n + 1))
                    pe.wait_ge(second_ready, after(n + 1))
                    pe.wait_ge(w_ready, after(n - 1))
                    for j in range(4):
                        last = pe.matmul(PS[:, 6 + b, j * P:(j + 1) * P], SECOND[:, b, j, :], FIRST[:, b, j, :], start=True, stop=True)
                    last.then_inc(placed, 1)

                def spread_step(s_, more):
                    for c in range(2):
                        spread(s_, 3 * c)
                        turn_next(s_, c, more)
                        spread(s_, 3 * c + 1)
                        hidden(s_, c)
                        spread(s_, 3 * c + 2)

                run(pe, SELECTION_STEPS, 3 * TOKEN_BLOCKS, spread_step)

            @block.gpsimd
            def _(pool):
                def low(s_, c):
                    for b in range(4):
                        pool.wait_ge(uT_ready, after(s_ * 8 + 4 * c + b + 1))
                        pool.wait_ge(uT_high, after(s_ * 8 + 4 * c + b + 1))
                        if b == 0:
                            pool.wait_ge(hidden_done, after(s_ * 2 + c - 1))
                        pool.tensor_tensor(UL[:, c, 4 * b:4 * b + 4, :], UT[:, 4 * b:4 * b + 4, :],
                                           UH[:, c, 4 * b:4 * b + 4, :], ALU.subtract).then_inc(uT_low, 1)

                with pool.Fori(0, HEAD) as s_:
                    for c in range(2):
                        low(s_, c)

            @block.scalar
            def _(act):
                def high(s_, c):
                    for b in range(4):
                        tiles = PS[:, b, :].rearrange("p (j e) -> p j e", j=4)
                        act.wait_ge(turned, after(s_ * 8 + 4 * c + b + 1))
                        act.wait_ge(uT_low, after(s_ * 8 + 4 * c - 4 + b + 1))
                        act.activation(UT[:, 4 * b:4 * b + 4, :], tiles, ACT.Copy).then_inc(uT_ready, 1)
                        if b == 0:
                            act.wait_ge(hidden_done, after(s_ * 2 + c - 1))
                        act.activation(UH[:, c, 4 * b:4 * b + 4, :], tiles, ACT.Copy).then_inc(uT_high, 1)

                def high_next(s_, c, more):
                    if c == 0:
                        high(s_, 1)
                    elif more:
                        high(s_ + 1, 0)

                def gelu(s_, c):
                    act.wait_ge(hidden_done, after(s_ * 2 + c + 1))
                    act.wait_ge(ge_stored[c], after(s_ * 16))
                    act.activation(GE[:, c, :], PS[:, 4 + c, 0:T], ACT.Gelu).then_inc(gelu_ready, 1)

                def step(s_, more):
                    for c in range(2):
                        high_next(s_, c, more)
                        gelu(s_, c)

                def stage(t):
                    act.wait_ge(scored, after(2 * t))
                    act.activation(Q[:], QT[:, :, t * P:(t + 1) * P], ACT.Copy).then_inc(staged, 1)

                def scores(t, half):
                    act.wait_ge(scored, after(2 * t + half + 1))
                    act.wait_ge(found1, after(t * N1))
                    act.activation(SC[:, half * GR // 2:(half + 1) * GR // 2, :].rearrange("p (b j) n -> p b (j n)", b=2),
                                   PS[:, 6:8, :], ACT.Copy).then_inc(scores_ready, 1)

                def exps(t):
                    act.wait_ge(steps, after(t * NS_ + 1))
                    act.activation(E[:], D[:], ACT.Exp).then_inc(exped, 1)

                def picks(t):
                    act.wait_ge(picks_turned, after(t + 1))
                    act.activation(SEL[:, :, t * P:(t + 1) * P], PS[:, 6, 0:3 * P].rearrange("p (j t) -> p j t", j=3), ACT.Copy).then_inc(sel_ready, 1)

                for b in range(4):
                    act.wait_ge(key_turned, after(b + 1))
                    act.activation(KYT[:, 4 * b:4 * b + 4, :], PS[:, 6 + b % 2, :].rearrange("p (j n) -> p j n", j=4), ACT.Copy).then_inc(keys_ready, 1)
                stage(0)
                scores(0, 0)
                scores(0, 1)
                stage(1)
                high(0, 0)
                first = 0
                for t in range(3):
                    if t < 2:
                        run(act, first, 2, step)
                        scores(t + 1, 0)
                        run(act, first + 2, 1, step)
                        scores(t + 1, 1)
                        if t < 1:
                            stage(t + 2)
                        exps(t)
                        run(act, first + 3, TILE_STEPS[t] - 3, step)
                    else:
                        run(act, first, 3, step)
                        exps(t)
                        run(act, first + 3, TILE_STEPS[t] - 3, step)
                    picks(t)
                    first += TILE_STEPS[t]

                for k in range(TOKEN_BLOCKS):
                    if k >= 2:
                        act.wait_ge(w_stored[k % 2], after(16))

                    def keep(s_, q):
                        act.wait_ge(placed, after((s_ - SELECTION_STEPS) * GROUPS_A_STEP + q + 1))
                        t = (s_ - SELECTION_STEPS - 3 * k) * (4 * GROUPS_A_STEP) + 4 * q
                        act.activation(W[:, k % 2, :, ds(t, 4)].rearrange("p i t -> p t i"),
                                       PS[:, 6 + q % 2, :].rearrange("p (t i) -> p t i", t=4), ACT.Copy).then_inc(w_ready, 1)

                    def spread_step(s_, more):
                        for c in range(2):
                            keep(s_, 3 * c)
                            high_next(s_, c, more)
                            keep(s_, 3 * c + 1)
                            gelu(s_, c)
                            keep(s_, 3 * c + 2)

                    run(act, SELECTION_STEPS + 3 * k, 3, spread_step)

            @block.vector
            def _(dve):
                for t in range(3):
                    dve.wait_ge(scores_ready, after(2 * t + 2))
                    dve.wait_ge(steps, after(t * NS_))
                    top16(dve, SC, V, IX, found1, GR, t * N1)
                    dve.wait_ge(found1, after(t * N1 + N1))
                    dve.wait_ge(found2, after(t * N2))
                    best = V[:].rearrange("p (h c) k -> p c h k", c=2)
                    dve.tensor_tensor(CA[:].rearrange("p h (a b) -> p h a b", a=TOPK),
                                      best[:, 0].unsqueeze(3).to_broadcast([P, PEER_HEADS, TOPK, TOPK]),
                                      best[:, 1].unsqueeze(2).to_broadcast([P, PEER_HEADS, TOPK, TOPK]), ALU.add).then_inc(paired, 1)
                    dve.wait_ge(paired, after(t + 1))
                    top16(dve, CA, TS, J, found2, PEER_HEADS, t * N2)
                    dve.wait_ge(found2, after(t * N2 + N2))
                    dve.wait_ge(picks_turned, after(t))
                    n = t * NS_
                    dve.tensor_tensor(D[:], TS[:], TS[:, :, 0:1].to_broadcast([P, PEER_HEADS, TOPK]), ALU.subtract).then_inc(steps, 1)
                    j = J[:].rearrange("p h k -> p (h k)")
                    dve.tensor_scalar(JJ[:, 0, :], j, 4, None, ALU.logical_shift_right).then_inc(steps, 1)
                    dve.tensor_scalar(JJ[:, 1, :], j, 15, None, ALU.bitwise_and).then_inc(steps, 1)
                    dve.tensor_copy(IXF[:], IX[:]).then_inc(steps, 1)
                    dve.wait_ge(steps, after(n + 4))
                    dve.tensor_copy(JF[:], JJ[:]).then_inc(steps, 1)
                    dve.wait_ge(steps, after(n + 5))
                    index = IXF[:].rearrange("p (h c) k -> p c h k", c=2)
                    for c in range(2):
                        dve.tensor_tensor(EQ[:], JF[:, c, :].unsqueeze(2).to_broadcast([P, PICKS, TOPK]),
                                          iota[:, 0:TOPK].unsqueeze(1).to_broadcast([P, PICKS, TOPK]), ALU.is_equal).then_inc(steps, 1)
                        dve.wait_ge(steps, after(n + 6 + 3 * c))
                        dve.tensor_tensor(MU[:].rearrange("p (h k) a -> p h k a", h=PEER_HEADS),
                                          EQ[:].rearrange("p (h k) a -> p h k a", h=PEER_HEADS),
                                          index[:, c].unsqueeze(2).to_broadcast([P, PEER_HEADS, TOPK, TOPK]), ALU.mult).then_inc(steps, 1)
                        dve.wait_ge(steps, after(n + 7 + 3 * c))
                        dve.tensor_reduce(PK[:, c, :], MU[:], AX.X, ALU.add).then_inc(steps, 1)
                        dve.wait_ge(steps, after(n + 8 + 3 * c))
                    dve.wait_ge(exped, after(t + 1))
                    dve.tensor_reduce(sums[:], E[:], AX.X, ALU.add).then_inc(steps, 1)
                    dve.wait_ge(steps, after(n + 12))
                    dve.reciprocal(rec[:], sums[:]).then_inc(steps, 1)
                    dve.wait_ge(steps, after(n + 13))
                    dve.tensor_tensor(PK[:, 2, :].rearrange("p (h k) -> p h k", h=PEER_HEADS), E[:],
                                      rec[:].unsqueeze(2).to_broadcast([P, PEER_HEADS, TOPK]), ALU.mult).then_inc(steps, 1)
                    dve.wait_ge(steps, after(n + 14))
                    dve.sem_inc(picks_ready, 1)
                dve.wait_ge(sel_ready, after(3))
                with dve.Fori(0, T // 8) as i:
                    for b in range(2):
                        dve.wait_ge(placed, after(i * 2 + b - 1))
                        dve.tensor_tensor(SECOND[:, b, :, :], iota[:].unsqueeze(1).to_broadcast([P, 4, P]),
                                          SEL[:, 1, ds(i * 8 + b * 4, 4)].unsqueeze(2).to_broadcast([P, 4, P]),
                                          ALU.is_equal).then_inc(second_ready, 1)
                        for j in range(4):
                            t = i * 8 + b * 4 + j
                            ins = dve.tensor_scalar(FIRST[:, b, j, :], iota[:], SEL[:, 0, ds(t, 1)], SEL[:, 2, ds(t, 1)],
                                                    ALU.is_equal, ALU.mult)
                        ins.then_inc(first_ready, 1)


def peer_stashed(nc, G, hT, U, u_loaded):
    A, PS, S = G["A"], G["PS"], G["S"]
    REST = D_MODEL // 2
    with ExitStack() as ctx:
        st = Stage(nc, G, ctx, "stash")
        V = st.sb("v", [P, 2, 2, D_MODEL])
        VH, VL = st.sb("v_high", [P, 2, 2, D_MODEL], F32R), st.sb("v_low", [P, 2, 2, D_MODEL], F32R)
        W = st.sb("weights", [P, 2, TOKEN_BLOCKS, 2, TB])
        GE, GA = st.sb("gelu", [P, 2, 2, T]), st.sb("act", [P, 2, 2, T])
        GH, GL = st.sb("act_high", [P, 2, 2, T], F32R), st.sb("act_low", [P, 2, 2, T], F32R)
        v_loaded, w_loaded = (st.sems(f"{w}0", f"{w}1") for w in ("v_loaded", "gelu_and_weights_loaded"))
        weighted, act_high, act_low, v_high, v_low, v_low_rest, out_done, added = st.sems(
            "weighted", "act_high", "act_low", "v_high", "v_low", "v_low_rest", "out_done", "added")
        v_in = A["peer_v"][0].rearrange("(i s c p) d -> i s p c d", s=2, c=2, p=P)
        u_in = A["peer_u"][0].rearrange("(n p) d -> n p d", p=P)[2 * HEAD:]
        ge_in = S["gelu"].rearrange("(i s c) p t -> i s p c t", s=2, c=2)
        w_in = S["peer_weights"].rearrange("k p (i s c) t -> i s p k c t", s=2, c=2)
        with nc.Block() as block:
            @block.sync
            def _(sp):
                for b in range(2):
                    sp.dma_start(V[:, b, :, :], v_in[0, b]).then_inc(v_loaded[b], 16)

                def load(i, first=False):
                    for b in range(2):
                        if not first:
                            sp.wait_ge(weighted, after(i * 2 + b - 1))
                        sp.dma_start(GE[:, b, :, :], ge_in[i, b]).then_inc(w_loaded[b], 16)
                        for c in range(2):
                            sp.dma_start(W[:, b, :, c, :], w_in[i, b, :, :, c, :]).then_inc(w_loaded[b], 16)
                        if not first:
                            sp.wait_ge(v_low, after(i * 4 + 2 * b - 2))
                            sp.wait_ge(v_low_rest, after(i * 2 + b - 1))
                            sp.dma_start(V[:, b, :, :], v_in[i, b]).then_inc(v_loaded[b], 16)

                load(0, True)
                with sp.Fori(1, HEAD // 2) as i:
                    load(i)
                for c in range(2):
                    sp.dma_start(U[:, c, :], u_in[c]).then_inc(u_loaded[c], 16)

            @block.scalar
            def _(act):
                with act.Fori(0, HEAD // 2) as i:
                    for b in range(2):
                        act.wait_ge(v_loaded[b], after(i * 16 + 16))
                        act.wait_ge(out_done, after(i * (2 * KT) + b * KT - KT))
                        for c in range(2):
                            act.activation(VH[:, b, c, :], V[:, b, c, :], ACT.Copy).then_inc(v_high, 1)

            @block.gpsimd
            def _(pool):
                with pool.Fori(0, HEAD // 2) as i:
                    for b in range(2):
                        for c in range(2):
                            pool.wait_ge(v_high, after(i * 4 + 2 * b + c + 1))
                            n = D_MODEL if c == 0 else D_MODEL - REST
                            pool.tensor_tensor(VL[:, b, c, 0:n], V[:, b, c, 0:n], VH[:, b, c, 0:n], ALU.subtract).then_inc(v_low, 1)

            @block.vector
            def _(dve):
                def weigh(i, b):
                    n = i * 2 + b
                    dve.wait_ge(w_loaded[b], after(i * 48 + 48))
                    dve.wait_ge(act_low, after(n))
                    for c in range(2):
                        ins = dve.tensor_tensor(GA[:, b, c, :].rearrange("p (k t) -> p k t", k=TOKEN_BLOCKS),
                                                GE[:, b, c, :].rearrange("p (k t) -> p k t", k=TOKEN_BLOCKS), W[:, b, :, c, :], ALU.mult)
                    ins.then_inc(weighted, 1)
                    dve.wait_ge(weighted, after(n + 1))
                    dve.wait_ge(out_done, after(i * (2 * KT) + b * KT - KT))
                    dve.tensor_copy(GH[:, b, :, :], GA[:, b, :, :]).then_inc(act_high, 1)
                    dve.wait_ge(act_high, after(n + 1))
                    dve.tensor_tensor(GL[:, b, :, :], GA[:, b, :, :], GH[:, b, :, :], ALU.subtract).then_inc(act_low, 1)

                def low_rest(i, b):
                    dve.wait_ge(v_high, after(i * 4 + 2 * b + 2))
                    rest = slice(D_MODEL - REST, D_MODEL)
                    dve.tensor_tensor(VL[:, b, 1, rest], V[:, b, 1, rest], VH[:, b, 1, rest], ALU.subtract).then_inc(v_low_rest, 1)

                def add(i, b, last=False):
                    for d in range(KT):
                        if d == KT // 2 and not last:
                            low_rest(*((i, 1) if b == 0 else (i + 1, 0)))
                        dve.wait_ge(out_done, after(i * (2 * KT) + b * KT + d + 1))
                        dve.tensor_tensor(hT[:, d, :], PS[:, d % 8, 0:T], hT[:, d, :], ALU.add).then_inc(added, 1)

                low_rest(0, 0)
                weigh(0, 0)
                with dve.Fori(0, HEAD // 2 - 1) as i:
                    weigh(i, 1)
                    add(i, 0)
                    weigh(i + 1, 0)
                    add(i, 1)
                weigh(HEAD // 2 - 1, 1)
                add(HEAD // 2 - 1, 0)
                add(HEAD // 2 - 1, 1, last=True)

            @block.tensor
            def _(pe):
                with pe.Fori(0, HEAD // 2) as i:
                    for b in range(2):
                        pe.wait_ge(act_low, after(i * 2 + b + 1))
                        pe.wait_ge(v_low, after(i * 4 + 2 * b + 2))
                        pe.wait_ge(v_low_rest, after(i * 2 + b + 1))
                        for d in range(KT):
                            m = i * (2 * KT) + b * KT + d
                            pe.wait_ge(added, after(m - 7))
                            cols = slice(d * P, (d + 1) * P)
                            for c in range(2):
                                pe.matmul(PS[:, d % 8, 0:T], VH[:, b, c, cols], GH[:, b, c, :], start=(c == 0), stop=False)
                                pe.matmul(PS[:, d % 8, 0:T], VH[:, b, c, cols], GL[:, b, c, :], start=False, stop=False)
                                last = pe.matmul(PS[:, d % 8, 0:T], VL[:, b, c, cols], GH[:, b, c, :], start=False, stop=(c == 1))
                            last.then_inc(out_done, 1)


def peer_experts(nc, G, XH, XL, hT, U, u_loaded):
    A, PS, ident, S = (G[k] for k in ("A", "PS", "ident", "S"))
    STEPS = EXPERTS // (2 * P) - HEAD
    OUT_BANKS = (0, 1, 6, 7)
    with ExitStack() as ctx:
        st = Stage(nc, G, ctx, "ex")
        V = st.sb("v", [P, 2, D_MODEL])
        UH, UL = st.sb("uT_high", [P, 2, KT, P], F32R), st.sb("uT_low", [P, 2, KT, P], F32R)
        VH, VL = st.sb("v_high", [P, 2, D_MODEL], F32R), st.sb("v_low", [P, 2, D_MODEL], F32R)
        W = st.sb("weights", [P, TOKEN_BLOCKS, 2, TB])
        GE, GA = st.sb("gelu", [P, 2, T]), st.sb("act", [P, 2, T])
        GH, GL = st.sb("act_high", [P, 2, T], F32R), st.sb("act_low", [P, 2, T], F32R)
        v_loaded = st.sems("v_loaded0", "v_loaded1")
        (w_loaded, turned, uT_high, uT_low, hidden_done, gelu_ready, weighted, act_high, act_ready, v_high, v_low, out_done,
         added) = st.sems(
            "weights_loaded", "turned", "uT_high", "uT_low", "hidden_done", "gelu_ready", "weighted", "act_high", "act_ready",
            "v_high", "v_low", "out_done", "added")
        u_in, v_in = (A[n][0].rearrange("(s c p) d -> s c p d", c=2, p=P)[HEAD:] for n in ("peer_u", "peer_v"))
        w_in = S["peer_weights"].rearrange("k p (s c) t -> s p k c t", c=2)[HEAD:]
        with nc.Block() as block:
            @block.sync
            def _(sp):
                sp.dma_start(W[:], w_in[0]).then_inc(w_loaded, 16)
                for c in range(2):
                    sp.dma_start(V[:, c, :], v_in[0, c]).then_inc(v_loaded[c], 16)
                sp.wait_ge(turned, after(4))
                sp.dma_start(U[:, 0, :], u_in[1, 0]).then_inc(u_loaded[0], 16)
                sp.wait_ge(turned, after(8))
                sp.dma_start(U[:, 1, :], u_in[1, 1]).then_inc(u_loaded[1], 16)

                def step(s, more):
                    if more:
                        sp.wait_ge(turned, after(s * 8 + 4))
                        sp.dma_start(U[:, 0, :], u_in[s + 1, 0]).then_inc(u_loaded[0], 16)
                    sp.wait_ge(weighted, after(s * 2))
                    sp.dma_start(W[:], w_in[s]).then_inc(w_loaded, 16)
                    sp.wait_ge(v_low, after(s * 2 - 1))
                    sp.dma_start(V[:, 0, :], v_in[s, 0]).then_inc(v_loaded[0], 16)
                    if more:
                        sp.wait_ge(turned, after(s * 8 + 8))
                        sp.dma_start(U[:, 1, :], u_in[s + 1, 1]).then_inc(u_loaded[1], 16)
                    sp.wait_ge(v_low, after(s * 2))
                    sp.dma_start(V[:, 1, :], v_in[s, 1]).then_inc(v_loaded[1], 16)

                with sp.Fori(1, STEPS - 1) as s:
                    step(s, True)
                step(STEPS - 1, False)

            @block.gpsimd
            def _(pool):
                with pool.Fori(0, STEPS) as s:
                    for c in range(2):
                        pool.wait_ge(v_high, after(s * 2 + c + 1))
                        pool.tensor_tensor(VL[:, c, :], V[:, c, :], VH[:, c, :], ALU.subtract).then_inc(v_low, 1)

            @block.scalar
            def _(act):
                def first_split():
                    for b in range(4):
                        act.wait_ge(turned, after(b + 1))
                        act.activation(UH[:, 0, 4 * b:4 * b + 4, :], PS[:, b, :].rearrange("p (j e) -> p j e", j=4), ACT.Copy).then_inc(uT_high, 1)

                def split_second(s):
                    for b in range(4):
                        act.wait_ge(turned, after(s * 8 + 4 + b + 1))
                        if b == 0:
                            act.wait_ge(hidden_done, after(s * 2))
                        act.activation(UH[:, 1, 4 * b:4 * b + 4, :], PS[:, b, :].rearrange("p (j e) -> p j e", j=4), ACT.Copy).then_inc(uT_high, 1)

                def split_next(s):
                    for b in range(4):
                        act.wait_ge(turned, after(s * 8 + 8 + b + 1))
                        if b == 0:
                            act.wait_ge(hidden_done, after(s * 2 + 1))
                        act.activation(UH[:, 0, 4 * b:4 * b + 4, :], PS[:, b, :].rearrange("p (j e) -> p j e", j=4), ACT.Copy).then_inc(uT_high, 1)

                def gelu(s, c):
                    act.wait_ge(hidden_done, after(s * 2 + c + 1))
                    act.wait_ge(weighted, after(s * 2))
                    act.activation(GE[:, c, :], PS[:, 4 + c, 0:T], ACT.Gelu).then_inc(gelu_ready, 1)

                def split_v(s):
                    act.wait_ge(out_done, after(s * KT))
                    for c in range(2):
                        act.wait_ge(v_loaded[c], after(s * 16 + 16))
                        act.activation(VH[:, c, :], V[:, c, :], ACT.Copy).then_inc(v_high, 1)

                first_split()
                with act.Fori(0, STEPS - 1) as s:
                    split_second(s)
                    split_next(s)
                    gelu(s, 0)
                    gelu(s, 1)
                    split_v(s)
                split_second(STEPS - 1)
                gelu(STEPS - 1, 0)
                gelu(STEPS - 1, 1)
                split_v(STEPS - 1)

            @block.vector
            def _(dve):
                def low_u(c, n):
                    for b in range(4):
                        dve.wait_ge(uT_high, after(n + b + 1))
                        dve.tensor_tensor(UL[:, c, 4 * b:4 * b + 4, :], PS[:, b, :].rearrange("p (j e) -> p j e", j=4),
                                          UH[:, c, 4 * b:4 * b + 4, :], ALU.subtract).then_inc(uT_low, 1)

                def add_outputs(s):
                    for d in range(KT):
                        dve.wait_ge(out_done, after(s * KT + d + 1))
                        dve.tensor_tensor(hT[:, d, :], PS[:, OUT_BANKS[d % 4], 0:T], hT[:, d, :], ALU.add).then_inc(added, 1)

                def weigh(s):
                    dve.wait_ge(w_loaded, after(s * 16 + 16))
                    for c in range(2):
                        dve.wait_ge(gelu_ready, after(s * 2 + c + 1))
                        dve.wait_ge(act_ready, after(s * 2))
                        dve.tensor_tensor(GA[:, c, :].rearrange("p (k t) -> p k t", k=TOKEN_BLOCKS),
                                          GE[:, c, :].rearrange("p (k t) -> p k t", k=TOKEN_BLOCKS), W[:, :, c, :], ALU.mult).then_inc(weighted, 1)
                    for c in range(2):
                        dve.wait_ge(weighted, after(s * 2 + c + 1))
                        dve.tensor_copy(GH[:, c, :], GA[:, c, :]).then_inc(act_high, 1)
                    for c in range(2):
                        dve.wait_ge(act_high, after(s * 2 + c + 1))
                        dve.tensor_tensor(GL[:, c, :], GA[:, c, :], GH[:, c, :], ALU.subtract).then_inc(act_ready, 1)

                low_u(0, 0)
                low_u(1, 4)
                low_u(0, 8)
                weigh(0)
                with dve.Fori(1, STEPS - 1) as s:
                    low_u(1, s * 8 + 4)
                    low_u(0, s * 8 + 8)
                    add_outputs(s - 1)
                    weigh(s)
                low_u(1, STEPS * 8 - 4)
                add_outputs(STEPS - 2)
                weigh(STEPS - 1)
                add_outputs(STEPS - 1)

            @block.tensor
            def _(pe):
                def turn(s, c):
                    pe.wait_ge(u_loaded[c], after(s * 16 + 16))
                    for b in range(4):
                        pe.wait_ge(uT_low, after(s * 8 + 4 * c - 4 + b + 1))
                        if c == 1 and b < 2:
                            pe.wait_ge(added, after(s * KT - 2 * KT + 13 + b))
                        for j in range(4):
                            k = 4 * b + j
                            last = pe.transpose(PS[:, b, j * P:(j + 1) * P], U[:, c, k * P:(k + 1) * P], ident[:])
                        last.then_inc(turned, 1)

                def turn_first():
                    pe.wait_ge(u_loaded[0], after(16))
                    for b in range(4):
                        for j in range(4):
                            k = 4 * b + j
                            last = pe.transpose(PS[:, b, j * P:(j + 1) * P], U[:, 0, k * P:(k + 1) * P], ident[:])
                        last.then_inc(turned, 1)

                def hidden(s, c):
                    out = PS[:, 4 + c, 0:T]
                    pe.wait_ge(gelu_ready, after(s * 2))
                    pe.wait_ge(uT_low, after(s * 8 + 4 * c + 4))
                    for k in range(KT):
                        pe.matmul(out, UH[:, c, k, :], XH[:, k, :], start=(k == 0), stop=False)
                        pe.matmul(out, UH[:, c, k, :], XL[:, k, :], start=False, stop=False)
                        last = pe.matmul(out, UL[:, c, k, :], XH[:, k, :], start=False, stop=(k == KT - 1))
                    last.then_inc(hidden_done, 1)

                def output(s, more=True):
                    pe.wait_ge(act_ready, after(s * 2 + 2))
                    pe.wait_ge(v_low, after(s * 2 + 2))
                    pe.wait_ge(uT_low, after(s * 8 + 20) if more else after(STEPS * 8))
                    for d in range(KT):
                        pe.wait_ge(added, after(s * KT + d - 3))
                        out = PS[:, OUT_BANKS[d % 4], 0:T]
                        cols = slice(d * P, (d + 1) * P)
                        for c in range(2):
                            pe.matmul(out, VH[:, c, cols], GH[:, c, :], start=(c == 0), stop=False)
                            pe.matmul(out, VH[:, c, cols], GL[:, c, :], start=False, stop=False)
                            last = pe.matmul(out, VL[:, c, cols], GH[:, c, :], start=False, stop=(c == 1))
                        last.then_inc(out_done, 1)

                turn_first()
                turn(0, 1)
                hidden(0, 0)
                turn(1, 0)
                hidden(0, 1)
                with pe.Fori(1, STEPS - 1) as s:
                    turn(s, 1)
                    hidden(s, 0)
                    turn(s + 1, 0)
                    hidden(s, 1)
                    output(s - 1)
                turn(STEPS - 1, 1)
                hidden(STEPS - 1, 0)
                hidden(STEPS - 1, 1)
                output(STEPS - 2, False)
                output(STEPS - 1, False)


def store_outputs(nc, G, yT):
    PS, ident, O = G["PS"], G["ident"], G["O"]
    with ExitStack() as ctx:
        st = Stage(nc, G, ctx, "y")
        Y = st.sb("rows", [P, 3, D_MODEL])
        turned, by_dve, by_act, stored = st.sems("turned", "ready_by_dve", "ready_by_act", "stored")
        outs = [O["y_prompt"][0, 0:P], O["y_prompt"][0, P:SEQ], O["y_sample"].rearrange("b s d -> (b s) d")]
        with nc.Block() as block:
            @block.tensor
            def _(pe):
                for n in range(12):
                    (t0, r), g = TOKEN_TILES[n // 4], n % 4
                    if n >= 8:
                        pe.wait_ge(by_act if n % 2 else by_dve, after((n - 8) // 2 + 1))
                    for j in range(4):
                        last = pe.transpose(PS[0:r, n % 8, j * P:(j + 1) * P], yT[:, 4 * g + j, t0:t0 + r], ident[:])
                    last.then_inc(turned, 1)

            @block.scalar
            def _(act):
                for n in range(1, 12, 2):
                    (t0, r), g = TOKEN_TILES[n // 4], n % 4
                    act.wait_ge(turned, after(n + 1))
                    act.activation(Y[0:r, n // 4, g * 512:(g + 1) * 512], PS[0:r, n % 8, :], ACT.Copy).then_inc(by_act, 1)

            @block.vector
            def _(dve):
                for n in range(0, 12, 2):
                    (t0, r), g = TOKEN_TILES[n // 4], n % 4
                    dve.wait_ge(turned, after(n + 1))
                    dve.tensor_copy(Y[0:r, n // 4, g * 512:(g + 1) * 512], PS[0:r, n % 8, :]).then_inc(by_dve, 1)

            @block.sync
            def _(sp):
                for i, (_, r) in enumerate(TOKEN_TILES):
                    sp.wait_ge(by_dve, after(2 * i + 2))
                    sp.wait_ge(by_act, after(2 * i + 2))
                    sp.dma_start(outs[i], Y[0:r, i, :]).then_inc(stored, 16)
                sp.wait_ge(stored, after(48))


_OUTS = [
    ("y_prompt", (1, SEQ, D_MODEL)),
    ("y_sample", (DEC_BATCH, DEC_SEQ, D_MODEL)),
    ("ret_state_prompt", (1, 1, RET_HEADS, RET_DK, RET_DV)),
    ("diff_k_prompt", (1, 1, SEQ, 2 * DIFF_HEADS, DIFF_HD)),
    ("diff_v_prompt", (1, 1, SEQ, DIFF_HEADS, 2 * DIFF_HD)),
    ("mem_k_prompt", (1, 1, MEM_TOKENS, MEM_HEADS, MEM_HD)),
    ("mem_v_prompt", (1, 1, MEM_TOKENS, MEM_HEADS, MEM_HD)),
    ("ret_state_sample", (1, DEC_BATCH, RET_HEADS, RET_DK, RET_DV)),
    ("diff_k_sample", (1, DEC_BATCH, DEC_SEQ, 2 * DIFF_HEADS, DIFF_HD)),
    ("diff_v_sample", (1, DEC_BATCH, DEC_SEQ, DIFF_HEADS, 2 * DIFF_HD)),
]


def kernel(**inputs):
    import numpy as _np
    import concourse.bacc as _bacc
    from concourse import mybir as _mybir
    from concourse.bass_utils import run_bass_kernel_spmd as _run

    nc = _bacc.Bacc("TRN2", target_bir_lowering=False, num_devices=1)
    arrays, A = {}, {}
    for name, value in inputs.items():
        a = _np.ascontiguousarray(value)
        arrays[f"in_{name}_dram"] = a
        A[name] = nc.dram_tensor(f"in_{name}_dram", a.shape, _mybir.dt.from_np(a.dtype), kind="ExternalInput").ap()
    O = {name: nc.dram_tensor(f"out_{name}_dram", shape, _mybir.dt.float32, kind="ExternalOutput").ap() for name, shape in _OUTS}
    decoder_step_kernel(nc, A, O)
    r = _run(nc, [arrays], core_ids=[0])
    return tuple(r.results[0][f"out_{name}_dram"] for name, _ in _OUTS)
```
